# Optimizing a Trainium2 kernel written in Bass

```python
import math
import jax, jax.numpy as jnp
from jax import lax
import numpy as np

D_MODEL = 1024
BATCH = 1
SEQ = 256
DEPTH = 2

MEM_LEN = 256
HG_HEADS = 8
HG_KDIM = 128
HG_VDIM = 128
HG_QK_W = HG_HEADS * HG_KDIM
HG_WIDTH = HG_HEADS * HG_VDIM
HG_CHUNK = 64
MLA_HEADS = 8
MLA_NOPE = 64
MLA_ROPE = 32
MLA_VDIM = 64
MLA_WIDTH = MLA_HEADS * MLA_VDIM
MLA_Q_RANK = 256
MLA_KV_RANK = 128
ROPE_THETA = 10000.0
Q_BLOCK = 128
MEM_HEADS = 4
MEM_HDIM = 128
MEM_WIDTH = MEM_HEADS * MEM_HDIM
MIX_WIDTH = HG_WIDTH + MLA_WIDTH + MEM_WIDTH
IN_SIZES = (HG_QK_W, HG_QK_W, HG_WIDTH, HG_WIDTH,
            MLA_Q_RANK, MLA_KV_RANK, MLA_ROPE, MLA_WIDTH,
            MEM_WIDTH, MEM_WIDTH)
IN_WIDTH = sum(IN_SIZES)
IN_OFFSETS = tuple(int(v) for v in np.cumsum(IN_SIZES)[:-1])
DEEPNORM_ALPHA = (2 * DEPTH) ** 0.25
DEEPNORM_BETA = (8 * DEPTH) ** -0.25
RMS_EPS = 1e-6
LN_EPS = 1e-5
NEG_BIG = -1e30


def _rmsnorm(t, g):
    t32 = t.astype(jnp.float32)
    t32 = t32 * lax.rsqrt(jnp.mean(t32 * t32, axis=-1, keepdims=True) + RMS_EPS)
    return t32.astype(t.dtype) * g

def _layernorm(t, g, b):
    t32 = t.astype(jnp.float32)
    mu = jnp.mean(t32, axis=-1, keepdims=True)
    var = jnp.mean(jnp.square(t32 - mu), axis=-1, keepdims=True)
    return ((t32 - mu) * lax.rsqrt(var + LN_EPS)).astype(t.dtype) * g + b

def _rope(t, cos, sin):
    half = t.shape[-1] // 2
    t1, t2 = t[..., :half], t[..., half:]
    return jnp.concatenate([t1 * cos - t2 * sin, t1 * sin + t2 * cos], axis=-1)

def _chunk_gated_recurrence(q, k, v, logf):
    B, S, H, dk = q.shape
    dv = v.shape[-1]
    C = HG_CHUNK
    n = S // C

    def to_chunks(t):
        return t.reshape(B, n, C, H, t.shape[-1]).transpose(1, 0, 3, 2, 4)

    tri = jnp.tril(jnp.ones((C, C), dtype=jnp.float32))

    def step(state, inp):
        qc, kc, vc, gc = inp
        b = jnp.cumsum(gc, axis=2)
        diff = b[:, :, :, None, :] - b[:, :, None, :, :]
        decay = jnp.exp(jnp.minimum(diff, 0.0)) * tri[:, :, None]
        A = jnp.einsum('bhtsd,bhsd->bhts', qc[:, :, :, None, :] * decay, kc)
        o = (jnp.einsum('bhts,bhsv->bhtv', A, vc)
             + jnp.einsum('bhtd,bhdv->bhtv', qc * jnp.exp(b), state))
        b_last = b[:, :, -1:, :]
        state = (jnp.exp(b_last[:, :, 0, :])[..., None] * state
                 + jnp.einsum('bhsd,bhsv->bhdv', kc * jnp.exp(b_last - b), vc))
        return state, o

    state0 = jnp.zeros((B, H, dk, dv), jnp.float32)
    _, o = lax.scan(step, state0, (to_chunks(q), to_chunks(k), to_chunks(v), to_chunks(logf)))
    return o.transpose(1, 0, 3, 2, 4).reshape(B, S, H, dv)

def _hgrn2_group(q, f_pre, i, lb, out_g):
    B, S, _ = q.shape
    q32 = q.reshape(B, S, HG_HEADS, HG_KDIM).astype(jnp.float32)
    z = f_pre.reshape(B, S, HG_HEADS, HG_KDIM).astype(jnp.float32)
    lb = lb.reshape(HG_HEADS, HG_KDIM)
    logf = jax.nn.log_sigmoid(z) + jnp.log1p(lb * jnp.exp(-z))
    k = (1.0 - lb) * jax.nn.sigmoid(-z)
    v = i.reshape(B, S, HG_HEADS, HG_VDIM).astype(jnp.float32)
    o = _chunk_gated_recurrence(q32, k, v, logf)
    o = o * lax.rsqrt(jnp.mean(o * o, axis=-1, keepdims=True) + RMS_EPS)
    return (o.astype(q.dtype) * out_g).reshape(B, S, HG_WIDTH)

def _mla_group(cq, ckv, kr, q_norm, kv_norm, w_uq, w_uk, w_uv, cos, sin):
    B, S, _ = cq.shape
    q = (_rmsnorm(cq, q_norm) @ w_uq).reshape(B, S, MLA_HEADS, MLA_NOPE + MLA_ROPE)
    q_nope = q[..., :MLA_NOPE]
    q_rope = _rope(q[..., MLA_NOPE:], cos[:, :, None, :], sin[:, :, None, :])
    c = _rmsnorm(ckv, kv_norm)
    k_nope = (c @ w_uk).reshape(B, S, MLA_HEADS, MLA_NOPE)
    v = (c @ w_uv).reshape(B, S, MLA_HEADS, MLA_VDIM)
    k_rope = _rope(kr, cos, sin)
    scale = 1.0 / math.sqrt(MLA_NOPE + MLA_ROPE)
    nb = S // Q_BLOCK
    qn_b = q_nope.reshape(B, nb, Q_BLOCK, MLA_HEADS, MLA_NOPE).transpose(1, 0, 2, 3, 4)
    qr_b = q_rope.reshape(B, nb, Q_BLOCK, MLA_HEADS, MLA_ROPE).transpose(1, 0, 2, 3, 4)
    key_idx = jnp.arange(S)

    def attend(args):
        qn, qr, blk = args
        s = (jnp.einsum('bqhd,bkhd->bhqk', qn, k_nope)
             + jnp.einsum('bqhr,bkr->bhqk', qr, k_rope)).astype(jnp.float32) * scale
        q_idx = blk * Q_BLOCK + jnp.arange(Q_BLOCK)
        mask = key_idx[None, :] <= q_idx[:, None]
        s = jnp.where(mask, s, NEG_BIG)
        p = jax.nn.softmax(s, axis=-1).astype(v.dtype)
        return jnp.einsum('bhqk,bkhd->bqhd', p, v)

    o = lax.map(attend, (qn_b, qr_b, jnp.arange(nb)))
    return o.transpose(1, 0, 2, 3, 4).reshape(B, S, MLA_WIDTH)

def _memory_group(qm, mem, w_k, w_v):
    B, S, _ = qm.shape
    M = mem.shape[1]
    q = qm.reshape(B, S, MEM_HEADS, MEM_HDIM)
    k = (mem @ w_k).reshape(B, M, MEM_HEADS, MEM_HDIM)
    v = (mem @ w_v).reshape(B, M, MEM_HEADS, MEM_HDIM)
    s = jnp.einsum('bshd,bmhd->bhsm', q, k).astype(jnp.float32) / math.sqrt(MEM_HDIM)
    p = jax.nn.softmax(s, axis=-1).astype(v.dtype)
    return jnp.einsum('bhsm,bmhd->bshd', p, v).reshape(B, S, MEM_WIDTH)

def first_inputs(seed: int = 0) -> dict:
    key = jax.random.key(seed)
    ks = jax.random.split(key, 16)
    nrm = jax.random.normal
    x = nrm(ks[0], (BATCH, SEQ, D_MODEL), jnp.float32)
    mem = nrm(ks[1], (BATCH, MEM_LEN, D_MODEL), jnp.float32)
    offsets = jax.random.randint(ks[2], (BATCH, 1), 0, 1024, dtype=jnp.int32)
    positions = (jnp.arange(SEQ, dtype=jnp.int32)[None, :] + offsets).astype(jnp.int32)
    w_in = nrm(ks[3], (DEPTH, D_MODEL, IN_WIDTH)) * D_MODEL ** -0.5
    hgrn_lb_logits = 0.1 * nrm(ks[4], (DEPTH, HG_QK_W))
    hgrn_out_norm = 1.0 + 0.02 * nrm(ks[5], (DEPTH, HG_VDIM))
    mla_q_norm = 1.0 + 0.02 * nrm(ks[6], (DEPTH, MLA_Q_RANK))
    mla_kv_norm = 1.0 + 0.02 * nrm(ks[7], (DEPTH, MLA_KV_RANK))
    w_mla_uq = nrm(ks[8], (DEPTH, MLA_Q_RANK, MLA_HEADS * (MLA_NOPE + MLA_ROPE))) * MLA_Q_RANK ** -0.5
    w_mla_uk = nrm(ks[9], (DEPTH, MLA_KV_RANK, MLA_HEADS * MLA_NOPE)) * MLA_KV_RANK ** -0.5
    w_mla_uv = nrm(ks[10], (DEPTH, MLA_KV_RANK, MLA_WIDTH)) * (MLA_KV_RANK ** -0.5 * DEEPNORM_BETA)
    w_mem_k = nrm(ks[11], (DEPTH, D_MODEL, MEM_WIDTH)) * D_MODEL ** -0.5
    w_mem_v = nrm(ks[12], (DEPTH, D_MODEL, MEM_WIDTH)) * (D_MODEL ** -0.5 * DEEPNORM_BETA)
    w_out = nrm(ks[13], (DEPTH, MIX_WIDTH, D_MODEL)) * (MIX_WIDTH ** -0.5 * DEEPNORM_BETA)
    ln_g = 1.0 + 0.02 * nrm(ks[14], (DEPTH, D_MODEL))
    ln_b = 0.02 * nrm(ks[15], (DEPTH, D_MODEL))
    return {'x': x, 'mem': mem, 'positions': positions, 'w_in': w_in,
            'hgrn_lb_logits': hgrn_lb_logits, 'hgrn_out_norm': hgrn_out_norm,
            'mla_q_norm': mla_q_norm, 'mla_kv_norm': mla_kv_norm,
            'w_mla_uq': w_mla_uq, 'w_mla_uk': w_mla_uk, 'w_mla_uv': w_mla_uv,
            'w_mem_k': w_mem_k, 'w_mem_v': w_mem_v, 'w_out': w_out,
            'ln_g': ln_g, 'ln_b': ln_b}

def first_block(x, mem, positions, w_in, hgrn_lb_logits, hgrn_out_norm, mla_q_norm,
              mla_kv_norm, w_mla_uq, w_mla_uk, w_mla_uv, w_mem_k, w_mem_v, w_out,
              ln_g, ln_b):
    inv_freq = 1.0 / (ROPE_THETA ** (jnp.arange(0, MLA_ROPE, 2, dtype=jnp.float32) / MLA_ROPE))
    ang = positions.astype(jnp.float32)[..., None] * inv_freq
    cos = jnp.cos(ang).astype(x.dtype)
    sin = jnp.sin(ang).astype(x.dtype)
    lb_soft = jax.nn.softmax(hgrn_lb_logits.astype(jnp.float32), axis=0)
    lower_bounds = jnp.cumsum(lb_soft, axis=0) - lb_soft[0]

    for l in range(DEPTH):
        h = x @ w_in[l]
        (hg_q, hg_f, hg_i, hg_gate, mla_cq, mla_ckv, mla_kr, mla_gate,
         mem_q, mem_gate) = jnp.split(h, IN_OFFSETS, axis=-1)
        y_hg = _hgrn2_group(hg_q, hg_f, hg_i, lower_bounds[l], hgrn_out_norm[l])
        y_mla = _mla_group(mla_cq, mla_ckv, mla_kr, mla_q_norm[l], mla_kv_norm[l],
                           w_mla_uq[l], w_mla_uk[l], w_mla_uv[l], cos, sin)
        y_mem = _memory_group(mem_q, mem, w_mem_k[l], w_mem_v[l])
        y = jnp.concatenate([y_hg * jax.nn.silu(hg_gate),
                             y_mla * jax.nn.silu(mla_gate),
                             y_mem * jax.nn.silu(mem_gate)], axis=-1)
        y = y @ w_out[l]
        x = _layernorm(DEEPNORM_ALPHA * x + y, ln_g[l], ln_b[l])
    return x


DEPTH_2 = 1

MIX_WIDTH_2 = D_MODEL
ATTN_WIDTH = MIX_WIDTH_2 // 2
POOL_WIDTH = MIX_WIDTH_2 - ATTN_WIDTH
N_HEADS = 8
HEAD_DIM = ATTN_WIDTH // N_HEADS
DILATED_BRANCHES = ((128, 1), (512, 4), (2048, 16))
MAX_SPAN = 2048
POOL_WINDOWS = (2, 4, 8, 16)
POOL_GROUP = POOL_WIDTH // len(POOL_WINDOWS)
PEER_HEADS = 8
PEER_NKEYS = 128
PEER_EXPERTS = PEER_NKEYS * PEER_NKEYS
PEER_QDIM = 256
PEER_TOPK = 16
TOKEN_CHUNK = 128
N_MOD = 6
EPS = 1e-6


def rmsnorm(x, g):
    xf = x.astype(jnp.float32)
    y = xf * lax.rsqrt(jnp.mean(xf * xf, axis=-1, keepdims=True) + EPS)
    return (y * g.astype(jnp.float32)).astype(x.dtype)

def alibi_slopes(n):
    return jnp.asarray([2.0 ** (-8.0 * (h + 1) / n) for h in range(n)], dtype=jnp.float32)

def dilated_attention(q, k, v):
    B, S, H, hd = q.shape
    nblk = S // Q_BLOCK
    pad = ((0, 0), (MAX_SPAN, 0), (0, 0), (0, 0))
    k_pad = jnp.pad(k, pad)
    v_pad = jnp.pad(v, pad)
    slopes = alibi_slopes(H)
    scale = HEAD_DIM ** -0.5
    qi = jnp.arange(Q_BLOCK)
    branches = []
    for w, d in DILATED_BRANCHES:
        j = jnp.arange(w // d + 1)
        gidx = qi[:, None] + MAX_SPAN - j[None, :] * d
        dist = j * d
        branches.append((gidx, dist))

    def block(idx):
        b = idx // nblk
        start = (idx % nblk) * Q_BLOCK
        qb = lax.dynamic_slice(q, (b, start, 0, 0), (1, Q_BLOCK, H, hd))[0].astype(jnp.float32) * scale
        ks = lax.dynamic_slice(k_pad, (b, start, 0, 0), (1, MAX_SPAN + Q_BLOCK, H, hd))[0]
        vs = lax.dynamic_slice(v_pad, (b, start, 0, 0), (1, MAX_SPAN + Q_BLOCK, H, hd))[0]
        pos = start + qi
        lses, outs = [], []
        for gidx, dist in branches:
            kg = jnp.take(ks, gidx, axis=0).astype(jnp.float32)
            vg = jnp.take(vs, gidx, axis=0).astype(jnp.float32)
            distf = dist.astype(jnp.float32)
            s = jnp.einsum('qhd,qjhd->hqj', qb, kg) - slopes[:, None, None] * distf[None, None, :]
            valid = (pos[:, None] - dist[None, :]) >= 0
            s = jnp.where(valid[None], s, -1e30)
            m = jnp.max(s, axis=-1, keepdims=True)
            p = jnp.exp(s - m)
            z = jnp.sum(p, axis=-1, keepdims=True)
            o = jnp.einsum('hqj,qjhd->qhd', p, vg) / jnp.transpose(z, (1, 0, 2))
            lses.append(jnp.transpose((m + jnp.log(z))[..., 0], (1, 0)))
            outs.append(o)
        wts = jax.nn.softmax(jnp.stack(lses, axis=0), axis=0)
        out = jnp.einsum('gqh,gqhd->qhd', wts, jnp.stack(outs, axis=0))
        return out.astype(q.dtype)

    out = lax.map(block, jnp.arange(B * nblk))
    return out.reshape(B, S, H, hd)

def multiscale_pool(u, w_pool, pool_scale):
    B, S, C = u.shape
    uf = u.astype(jnp.float32)
    cs = jnp.pad(jnp.cumsum(uf, axis=1), ((0, 0), (1, 0), (0, 0)))
    pos1 = jnp.arange(1, S + 1, dtype=jnp.float32)
    outs = []
    for g, w in enumerate(POOL_WINDOWS):
        sl = slice(g * POOL_GROUP, (g + 1) * POOL_GROUP)
        cg = cs[:, :, sl]
        upper = cg[:, 1:]
        lower = jnp.pad(cg, ((0, 0), (w - 1, 0), (0, 0)))[:, :S]
        cnt = jnp.minimum(pos1, float(w))[None, :, None]
        mixed = (upper - lower) / cnt - uf[:, :, sl]
        outs.append(jnp.einsum('bsc,ce->bse', mixed, w_pool[g].astype(jnp.float32)))
    y = jnp.concatenate(outs, axis=-1) * pool_scale.astype(jnp.float32)
    return y.astype(u.dtype)

def peer_ffn(h, w_q, sub_keys, expert_u, expert_v):
    B, S, D = h.shape
    T = B * S
    half = PEER_QDIM // 2
    K = PEER_TOPK
    hc = h.reshape(T // TOKEN_CHUNK, TOKEN_CHUNK, D)

    def chunk(xc):
        C = xc.shape[0]
        q = jnp.einsum('cd,de->ce', xc, w_q).astype(jnp.float32).reshape(C, PEER_HEADS, 2, half)
        s = jnp.einsum('chpk,pnk->chpn', q, sub_keys.astype(jnp.float32))
        sv, si = lax.top_k(s, K)
        cand = sv[:, :, 0, :, None] + sv[:, :, 1, None, :]
        cand_id = si[:, :, 0, :, None] * PEER_NKEYS + si[:, :, 1, None, :]
        cand = cand.reshape(C, PEER_HEADS, K * K)
        cand_id = cand_id.reshape(C, PEER_HEADS, K * K)
        top_v, top_pos = lax.top_k(cand, K)
        eid = jnp.take_along_axis(cand_id, top_pos, axis=-1)
        gate = jax.nn.softmax(top_v, axis=-1)
        u = expert_u[eid]
        act = jax.nn.gelu(jnp.einsum('cd,chkd->chk', xc, u).astype(jnp.float32), approximate=False)
        vv = expert_v[eid]
        y = jnp.einsum('chk,chkd->cd', (gate * act).astype(vv.dtype), vv)
        return y.astype(xc.dtype)

    return lax.map(chunk, hc).reshape(B, S, D)

def second_inputs(seed: int = 0) -> dict:
    key = jax.random.key(seed)
    ks = jax.random.split(key, 16)
    D = D_MODEL
    proj_out = 3 * ATTN_WIDTH + POOL_WIDTH
    f32 = jnp.float32
    x = jax.random.normal(ks[0], (BATCH, SEQ, D), f32)
    c = jax.random.normal(ks[1], (BATCH, D), f32)
    w_ada = jax.random.normal(ks[2], (DEPTH_2, D, N_MOD * D), f32) * (0.5 * D ** -0.5)
    b_ada = jax.random.normal(ks[3], (DEPTH_2, N_MOD * D), f32) * 0.01
    norm1_g = 1.0 + 0.05 * jax.random.normal(ks[4], (DEPTH_2, D), f32)
    w_in = jax.random.normal(ks[5], (DEPTH_2, D, proj_out), f32) * D ** -0.5
    pool_w = jax.random.normal(ks[6], (DEPTH_2, len(POOL_WINDOWS), POOL_GROUP, POOL_GROUP), f32) * POOL_GROUP ** -0.5
    pool_scale = 1.0 + 0.1 * jax.random.normal(ks[7], (DEPTH_2, POOL_WIDTH), f32)
    w_out = jax.random.normal(ks[8], (DEPTH_2, MIX_WIDTH_2, D), f32) * MIX_WIDTH_2 ** -0.5
    norm2_g = 1.0 + 0.05 * jax.random.normal(ks[9], (DEPTH_2, D), f32)
    peer_wq = jax.random.normal(ks[10], (DEPTH_2, D, PEER_HEADS * PEER_QDIM), f32) * D ** -0.5
    peer_subkeys = jax.random.normal(ks[11], (DEPTH_2, 2, PEER_NKEYS, PEER_QDIM // 2), f32) * (PEER_QDIM // 2) ** -0.5
    peer_u = jax.random.normal(ks[12], (DEPTH_2, PEER_EXPERTS, D), f32) * D ** -0.5
    peer_v = jax.random.normal(ks[13], (DEPTH_2, PEER_EXPERTS, D), f32) * 0.5
    final_g = 1.0 + 0.05 * jax.random.normal(ks[14], (D,), f32)
    return {"x": x, "c": c, "w_ada": w_ada, "b_ada": b_ada, "norm1_g": norm1_g,
            "w_in": w_in, "pool_w": pool_w, "pool_scale": pool_scale, "w_out": w_out,
            "norm2_g": norm2_g, "peer_wq": peer_wq, "peer_subkeys": peer_subkeys,
            "peer_u": peer_u, "peer_v": peer_v, "final_g": final_g}

def second_block(x, c, w_ada, b_ada, norm1_g, w_in, pool_w, pool_scale, w_out,
              norm2_g, peer_wq, peer_subkeys, peer_u, peer_v, final_g):
    B, S, D = x.shape
    A = ATTN_WIDTH
    for l in range(DEPTH_2):
        mod = jnp.einsum('bd,de->be', jax.nn.silu(c), w_ada[l]) + b_ada[l]
        sh1, sc1, g1, sh2, sc2, g2 = jnp.split(mod[:, None, :], N_MOD, axis=-1)
        h = rmsnorm(x, norm1_g[l]) * (1.0 + sc1) + sh1
        proj = jnp.einsum('bsd,de->bse', h, w_in[l])
        q, k, v, u = jnp.split(proj, [A, 2 * A, 3 * A], axis=-1)
        attn = dilated_attention(q.reshape(B, S, N_HEADS, HEAD_DIM),
                                 k.reshape(B, S, N_HEADS, HEAD_DIM),
                                 v.reshape(B, S, N_HEADS, HEAD_DIM)).reshape(B, S, A)
        pool = multiscale_pool(u, pool_w[l], pool_scale[l])
        mixed = jnp.einsum('bse,ed->bsd', jnp.concatenate([attn, pool], axis=-1), w_out[l])
        x = x + g1 * mixed
        h2 = rmsnorm(x, norm2_g[l]) * (1.0 + sc2) + sh2
        x = x + g2 * peer_ffn(h2, peer_wq[l], peer_subkeys[l], peer_u[l], peer_v[l])
    return rmsnorm(x, final_g)


def setup_inputs(seed=0):
    out = dict(first_inputs(seed))
    for name, value in second_inputs(seed + 1).items():
        if name != "x":
            out[name + "_2"] = value
    return out


def reference(
    x, mem, positions, w_in, hgrn_lb_logits, hgrn_out_norm, mla_q_norm, mla_kv_norm, w_mla_uq,
    w_mla_uk, w_mla_uv, w_mem_k, w_mem_v, w_out, ln_g, ln_b, c_2, w_ada_2, b_ada_2, norm1_g_2,
    w_in_2, pool_w_2, pool_scale_2, w_out_2, norm2_g_2, peer_wq_2, peer_subkeys_2, peer_u_2,
    peer_v_2, final_g_2,
):
    x = first_block(
        x, mem, positions, w_in, hgrn_lb_logits, hgrn_out_norm, mla_q_norm, mla_kv_norm,
        w_mla_uq, w_mla_uk, w_mla_uv, w_mem_k, w_mem_v, w_out, ln_g, ln_b,
    )
    return second_block(
        x, c_2, w_ada_2, b_ada_2, norm1_g_2, w_in_2, pool_w_2, pool_scale_2, w_out_2, norm2_g_2,
        peer_wq_2, peer_subkeys_2, peer_u_2, peer_v_2, final_g_2,
    )


_drawn_inputs = setup_inputs


def setup_inputs(seed=0):
    import zlib

    import numpy as np

    out = dict(_drawn_inputs(seed))
    spreads = {}
    factors = {'mem': 5.214,
     'hgrn_lb_logits': 3.47,
     'hgrn_out_norm': 7.725,
     'mla_q_norm': 8.0,
     'mla_kv_norm': 8.0,
     'w_mla_uq': 3.646,
     'w_mla_uk': 4.003,
     'w_mla_uv': 2.78,
     'w_mem_k': 5.885,
     'w_mem_v': 5.088,
     'b_ada_2': 4.083,
     'norm1_g_2': 3.833,
     'norm2_g_2': 2.785}
    for name, (base, spread) in spreads.items():
        noise = np.random.default_rng([zlib.crc32(name.encode()), seed]).standard_normal(out[name].shape)
        drawn = base * np.exp(spread * noise) if base else spread * noise
        out[name] = __import__('jax').numpy.asarray(drawn.astype(out[name].dtype))
    for name, factor in factors.items():
        out[name] = (out[name] * factor).astype(out[name].dtype)
    return out
```

```python
import numpy as np

P = 128
D_MODEL = 1024
T = 256
TT = T // P
DC = D_MODEL // P
DEPTH = 2
HG_HEADS = 8
MLA_HEADS, NOPE, ROPE, MLA_V = 8, 64, 32, 64
Q_RANK, KV_RANK = 256, 128
MEM_HEADS = 4
IN_WIDTH = 6048
N_LEVELS = 9
ALPHA = (2 * DEPTH) ** 0.25
MLA_SCALE = (NOPE + ROPE) ** -0.5
MEM_SCALE = 128 ** -0.5
RMS_EPS, LN_EPS = 1e-6, 1e-5
NEG_BIG = -1e30
COLS = 512
RING = 3

HEADS2, HD2 = 8, 64
PEER_HEADS, NKEYS, TOPK = 8, 128, 16
PICKS = PEER_HEADS * TOPK
GSLOTS = 16
GHALF = GSLOTS // 2
TURNS = PICKS // GSLOTS

IN_UNITS = [("G0", 3072), ("G1", 3584), ("GM", 4512), ("GE", 5536), ("F0", 1024), ("F1", 1536),
            ("Q0", 0), ("Q1", 512), ("C", 4096), ("I0", 2048), ("I1", 2560), ("MQ", 5024)]
LAYER_UNITS = ["G0", "G1", "GM", "GE", "F0", "F1", "Q0", "Q1", "C", "I0", "UP", "I1", "MQ", "MK", "MV",
               "O0", "O1", "O2", "O3"]
B2 = DEPTH
N_MOD_UNITS = 6 * D_MODEL // COLS
B2_UNITS = ([f"AD{j}" for j in range(N_MOD_UNITS)] + ["BQ", "BK", "BV", "BU", "O0", "O1"]
            + [f"K{j}" for j in range(4)])
STREAM = [(l, n) for l in range(DEPTH) for n in LAYER_UNITS] + [(B2, n) for n in B2_UNITS]
UNIT = {key: n for n, key in enumerate(STREAM)}


def big_uses():
    out, uses, turn = {}, [0, 0], 0
    for l, name in STREAM:
        if name == "O0":
            out[l, "OUT"] = tuple(uses)
            uses = [uses[0] + 1, uses[1] + 1]
            turn = 0
        elif name != "UP" and name[0] != "O":
            out[l, name] = (turn, uses[turn])
            uses[turn] += 1
            turn = 1 - turn
    return out


BIG = big_uses()

TASKS = ["X", "G0", "G1", "GM", "GE", "F0", "F1", "FP", "Q0", "Q1", "C", "Da1", "L0", "Da2", "Db1",
         "N", "I0", "L1", "Da3", "Db2", "UP", "I1", "L2", "Da4", "Db3", "A0", "A1", "MQ", "L3",
         "Da5", "Db4", "A2", "A3", "MK", "L4", "Da6", "Db5", "A4", "A5", "MV", "L5", "Da7", "Db6",
         "A6", "L6", "Da8", "Db7", "A7", "L7", "Db8", "A8", "L8", "A9", "A10", "H0", "H1", "H2",
         "H3", "H4", "A11", "A12", "A13", "OUT", "LN"]
N_ATT = MLA_HEADS + MEM_HEADS
TASKS2 = ([f"AD{j}" for j in range(N_MOD_UNITS)] + ["R1", "X", "BQ", "BK", "BV", "BU", "PL", "SK"]
          + [f"B{i}" for i in range(HEADS2 + 2)] + ["OUT", "R2", "X2"]
          + ["K0", "E0", "K1", "E1", "E2", "K2", "E3", "E4", "K3", "E5", "E6", "E7"])


def bank_uses(task):
    if task in ("X", "X2"):
        return [(task, j) for j in range(4)]
    if task == "SK":
        return [("SK",)]
    if task == "PL":
        return [("PL", j) for j in range(2)]
    if task[0] == "E":
        return [("E", int(task[1:]))]
    if task[0] == "B" and task[1:].isdigit():
        i = int(task[1:])
        out = [("S", i)] if i < HEADS2 else []
        out += [("PT", i - 1)] if 1 <= i <= HEADS2 else []
        return out + ([("AO", i - 2)] if i >= 2 else [])
    if task[0] == "L" and task[1:].isdigit():
        m = int(task[1:])
        return [("L", m, j) for j in range(4 if m < 8 else 2)]
    if task == "N":
        return [("N",), ("KR",)]
    if task == "UP":
        return ([("UQ", j) for j in range(4)] + [("UK", j) for j in range(4)]
                + [("UV", t) for t in range(TT)] + [("QR", j) for j in range(4)])
    if task[0] == "A" and task[1:].isdigit():
        i = int(task[1:])
        out = [("S", i)] if i < N_ATT else []
        out += [("PT", i - 1)] if 1 <= i <= N_ATT else []
        return out + ([("AO", i - 2)] if i >= 2 else [])
    if task[0] == "H":
        i = int(task[1:])
        return ([("HO", i)] if i < 4 else []) + ([("HN", i - 1)] if i >= 1 else [])
    return []


def bank_index():
    out, n = {}, 0
    for j in range(4):
        out["M", j] = n
        n += 1
    out["VEC"] = n
    n += 1
    for l in range(DEPTH + 1):
        for task in TASKS if l < DEPTH else TASKS2:
            for key in bank_uses(task):
                out[l, key] = n
                n += 1
    return out, n


def constants():
    i = np.arange(P)
    level = np.zeros((P, 7, P), np.int32)
    for m in range(1, 8):
        h = 2 ** (m - 1)
        same = (i[:, None] // (2 * h)) == (i[None, :] // (2 * h))
        level[:, m - 1] = same & ((i[:, None] // h) % 2 == 0) & ((i[None, :] // h) % 2 == 1)
    t = np.arange(T)
    causal = np.where(t[None, :] <= t[:, None], 0.0, NEG_BIG).astype(np.float32)
    rot = np.zeros((P, 32), np.float32)
    for j in range(16):
        for base in (0, 64):
            rot[base + j + 16, j] = -1.0
            rot[base + j, j + 16] = 1.0
    inv = np.float32(1.0) / (np.float32(10000.0) ** (np.arange(0, ROPE, 2, dtype=np.float32) / np.float32(ROPE)))
    dist = (t[:, None] - t[None, :])
    count = ((dist >= 0) & (dist <= 128)).astype(np.float32)
    for d in (4, 16):
        count += (dist >= 0) & (dist % d == 0)
    far = np.where(count > 0, dist, 1e30).astype(np.float32)
    inv_count = np.stack([1.0 / np.minimum(t + 1, w) for w in (2, 4, 8, 16)]).astype(np.float32)
    return {
        "c_eye": np.eye(P, dtype=np.float32),
        "c_level": level.reshape(P, 7 * P),
        "c_causal": causal, "c_rot": rot,
        "c_inv_freq": np.tile(inv, P // 16).reshape(1, P).astype(np.float32),
        "c_count": count, "c_dist": far, "c_inv_count": inv_count.reshape(1, 4 * T),
        "c_iota": np.arange(16, dtype=np.float32).reshape(1, 16),
    }


def build(nc, d, out, part="all"):
    import concourse.bass as bass
    from concourse import mybir
    from concourse.alu_op_type import AluOpType as ALU
    from contextlib import ExitStack

    f32, u32, i32, u8 = mybir.dt.float32, mybir.dt.uint32, mybir.dt.int32, mybir.dt.uint8
    ACT = mybir.ActivationFunctionType
    X = mybir.AxisListType.X
    BANK, N_BANK1 = bank_index()

    with ExitStack() as ctx:
        def sb(name, shape, dt=f32):
            return ctx.enter_context(nc.sbuf_tensor(name, shape, dt))

        eye = sb("eye", [P, P])
        ones_mean = sb("ones_mean", [P, P])
        rot = sb("rot", [P, 32])
        level_mask = sb("level_mask", [P, 7, P], u8)
        causal = sb("causal", [P, TT, T])
        vec = sb("vec", [P, 40])
        lower = sb("lower", [P, DEPTH, 2, 8])
        lbt = sb("lbt", [P, 6, 8])
        eps = sb("eps", [P, 3])
        rope = sb("rope", [P, 2, T])
        stat = sb("stat", [P, 16])
        x = sb("x", [P, TT, D_MODEL])
        xT = sb("xT", [P, DC, T])
        memT = sb("memT", [P, DC, T])
        ring = sb("ring", [P, RING, DC * COLS])
        yT = sb("yT", [P, 16, T])
        big = sb("big", [P, 3, HG_HEADS * T])
        vec_rows = big[:, 2, 0:P]
        qT = sb("qT", [P, HG_HEADS, T])
        kT = sb("kT", [P, HG_HEADS, T])
        b = sb("b", [P, HG_HEADS, T])
        pair = sb("pair", [P, HG_HEADS * TT, P])
        hv = sb("hv", [P, TT, D_MODEL])
        cT = sb("cT", [P, 4, T])
        sq = sb("sq", [P, 3, T])
        rstd = sb("rstd", [P, 2, T])
        qM = sb("qM", [96, MLA_HEADS, T])
        kM = sb("kM", [96, MLA_HEADS, T])
        vM = sb("vM", [P, TT, MLA_HEADS * MLA_V])
        qE = sb("qE", [P, MEM_HEADS, T])
        kE = sb("kE", [P, MEM_HEADS, T])
        vE = sb("vE", [P, TT, MEM_HEADS * P])
        sm = sb("sm", [P, 2, TT, T])
        pT = sb("pT", [P, 2, TT, T])
        far_pair = kT
        ln_gb = big[:, 1, :]

        mod = big[:, :, :].rearrange("p a n -> p (a n)")
        gain = hv
        flat_pair = pair[:, :, :].rearrange("p a t -> p (a t)")
        final_g, w_pool, iota = flat_pair[:, 0:D_MODEL], pair[:, 8:12, :], flat_pair[:, 1536:1552]
        q2, k2, v2 = qT[:, 0:4, :], qT[:, 4:8, :], vE
        uT, pool_sum = kT[:, 0:4, :], kT[:, 4:8, :]
        mixed, inv_count = b[:, 0:4, :], b[:, 4:8, :].rearrange("p a t -> p (a t)")
        count, dist = qE[:, 0:2, :], qE[:, 2:4, :]
        normed = memT[:, :, :].rearrange("p a t -> p (a t)").rearrange("p (a n) -> p a n", a=TT)
        silu_c = lbt[:, 4, :]

        def flat(tile):
            return tile[:, :, :].rearrange("p a t -> p (a t)")
        shape5 = dict(t=TT, h=PEER_HEADS, two=2)
        sub_val = flat(cT)[:, 0:512].rearrange("p (t h two k) -> p t h two k", **shape5)
        sub_idf = flat(cT)[:, 512:1024].rearrange("p (t h two k) -> p t h two k", **shape5)
        sub_id = flat(kE)[:, 0:512].bitcast(u32).rearrange("p (t h two k) -> p t h two k", **shape5)
        top_pos = flat(kE)[:, 512:768].bitcast(u32).rearrange("p (t j) -> p t j", t=TT)
        digit = flat(kE)[:, 768:896].bitcast(u32)
        top_val = flat(rstd)[:, 0:PICKS * TT].rearrange("p (t h k) -> p t h k", t=TT, h=PEER_HEADS)
        gate = flat(rstd)[:, PICKS * TT:].rearrange("p (t j) -> p t j", t=TT)
        sub_rows = flat_pair[:, 1552:1552 + 2 * P]
        skT = flat(sq)[:, 512:768].rearrange("p (a k) -> p a k", a=2)
        cand, cand_left = flat(sq)[:, 0:256], flat(sq)[:, 256:512]
        first_of, second_of = flat(vM)[:, 0:PICKS], flat(vM)[:, PICKS:2 * PICKS]
        id_a, id_b = flat(vM)[:, 2 * PICKS:3 * PICKS], flat(vM)[:, 3 * PICKS:4 * PICKS]
        expert = flat(vM)[:, 512:768].bitcast(u32).rearrange("p (t j) -> p t j", t=TT)
        dots = flat(vM)[:, 768:1024].rearrange("p (t j) -> p t j", t=TT)
        onehot = flat(qT).rearrange("p (j i) -> p j i", i=TOPK)
        gslot = ([ring[:, s, g * D_MODEL:(g + 1) * D_MODEL] for s in range(RING) for g in range(4)]
                 + [yT[:, 4 * g:4 * g + 4, :].rearrange("p a t -> p (a t)") for g in range(GSLOTS - 4 * RING)])
        turn_idx = causal[:, 0, 0:GSLOTS].bitcast(u32)
        acc = b[:, :, :].rearrange("p a t -> p (a t)").rearrange("p (a n) -> p a n", a=TT)
        product = flat(kT)[:, 0:D_MODEL]
        pj = [ctx.enter_context(nc.psum_tensor(f"pj{i}", [P, 1024], f32)) for i in range(2)]
        bank = [ctx.enter_context(nc.psum_tensor(f"bank{i}", [P, 512], f32)) for i in range(4)]

        made = {}

        def sem(name):
            if name not in made:
                made[name] = ctx.enter_context(nc.semaphore(name))
            return made[name]

        PER = dict(x_ready=1, xT_ready=4, gates=1, fz=2, f_exp=1, f_pos=1, f_ln=1, k_ready=1, q_ready=2,
                   lvl_sub=8, lvl_exp=8, lvl_ready=8, blended=9, c_ready=1, c_sq=1, c_rstd=1,
                   c_normed=1, kr_ready=1, kr_spread=1, uq_ready=4, qrope_ready=4, uk_ready=4,
                   uv_ready=2, hv_ready=2, qE_ready=1, kE_ready=1, vE_ready=1,
                   sm_ready=12, exp_done=12, p_ready=12, pt_ready=12, y_att=12,
                   ho_sq=4, ho_used=4, ho_rstd=4, y_hg=4, ln_in=2, ln_sq=2, ln_rstd=2, x_next=2)


        def after(eng, name, l, i=0):
            eng.wait_ge(sem(name), l * PER[name] + i + 1)

        def bank_of(key):
            return bank[BANK[key] % 4]

        def bank_filled(eng, key):
            eng.wait_ge(sem("bank_filled"), BANK[key] + 1)

        def bank_empty(eng, key):
            n = BANK[key]
            if n >= 4:
                eng.wait_ge(sem(f"bank_free{n % 4}"), n // 4)

        def bank_free(key):
            n = BANK[key]
            return f"bank_free{n % 4}", n // 4 + 1

        UQ_W = 2 * MLA_HEADS * (NOPE + ROPE)

        def up_weights(slot):
            w = ring[:, slot, :]
            return (w[:, 0:UQ_W].rearrange("p (c n) -> p c n", c=2), w[:, UQ_W:UQ_W + 512],
                    w[:, UQ_W + 512:UQ_W + 1024])

        def ring_loads(n):
            units = range(n % RING, n + 1, RING)
            return 16 * sum(3 if STREAM[k][1] == "UP" else 1 for k in units)

        def unit_done(eng, l, name):
            eng.wait_ge(sem("unit_done"), UNIT[l, name] + 1)

        def steps(eng, own):
            seen = {}

            def step(ins, name=None, value=None):
                name = name or own
                seen[name] = value or seen.get(name, 0) + 1
                ins.then_inc(sem(name), 1)
                eng.wait_ge(sem(name), seen[name])
            return step

        V_LB, V_OUT, V_QN, V_KN, V_INV = 0, 16, 18, 22, 24
        V_C, V_POOL = 25, 33
        N_B2 = 9
        N_CONST = 12

        block = ctx.enter_context(nc.Block())

        @block.sync
        def _(sp):
            def load(dst, src, name="consts_load"):
                sp.dma_start(dst, src).then_inc(sem(name), 16)

            sp.wait_ge(sem("vec_zeroed"), 1)
            load(vec_rows[V_LB:V_LB + 16, :], d["hgrn_lb_logits"].rearrange("l (h p) -> (l h) p", p=P))
            load(vec_rows[V_OUT:V_OUT + 2, :], d["hgrn_out_norm"])
            load(vec_rows[V_QN:V_QN + 4, :], d["mla_q_norm"].rearrange("l (h p) -> (l h) p", p=P))
            load(vec_rows[V_KN:V_KN + 2, :], d["mla_kv_norm"])
            load(vec_rows[V_INV:V_INV + 1, :], d["c_inv_freq"])
            load(vec_rows[V_C:V_C + 8, :], d["c_2"].rearrange("l (h p) -> (l h) p", p=P))
            load(vec_rows[V_POOL:V_POOL + 4, :], d["pool_scale_2"].rearrange("l (h p) -> (l h) p", p=P))
            load(eye[:, :], d["c_eye"])
            load(rot[:, :], d["c_rot"])
            load(big[:, 1, 800:1696].bitcast(i32), d["c_level"])
            load(causal[:, :, :], d["c_causal"].rearrange("(a p) s -> p a s", p=P))
            load(big[:, 1, 0:T].bitcast(i32), d["positions"].to_broadcast([P, T]))
            load(big[:, 0, :].rearrange("p (a n) -> p a n", a=TT), d["mem"].rearrange("o (a p) n -> p (o a) n", p=P), "mem_load")
            load(x[:, :, :], d["x"].rearrange("o (a p) n -> p (o a) n", p=P), "x_load")

            def weights(n):
                if n >= RING:
                    sp.wait_ge(sem("unit_done"), n - RING + 1)
                l, name = STREAM[n]
                slot = n % RING
                arrived = f"ring_load{slot}"
                if name == "UP":
                    w_uq, w_uk, w_uv = up_weights(slot)
                    load(w_uq, d["w_mla_uq"][l].rearrange("(c p) n -> p c n", p=P), arrived)
                    load(w_uk, d["w_mla_uk"][l], arrived)
                    load(w_uv, d["w_mla_uv"][l], arrived)
                    return
                if name[0] == "O":
                    j = int(name[1])
                    src = d["w_out"][l] if l < DEPTH else d["w_out_2"][0]
                    load(ring[:, slot, :].rearrange("p (c n) -> p c n", c=4),
                         src[j * 512:(j + 1) * 512, :].rearrange("(c p) n -> p c n", p=P), arrived)
                    return
                if name == "MK":
                    src = d["w_mem_k"][l]
                elif name == "MV":
                    src = d["w_mem_v"][l]
                elif l < DEPTH:
                    c0 = dict(IN_UNITS)[name]
                    src = d["w_in"][l, :, c0:c0 + (416 if name == "C" else COLS)]
                elif name[:2] == "AD":
                    j = int(name[2:])
                    src = d["w_ada_2"][0, :, j * COLS:(j + 1) * COLS]
                elif name[0] == "B":
                    j = "QKVU".index(name[1])
                    src = d["w_in_2"][0, :, j * COLS:(j + 1) * COLS]
                else:
                    j = int(name[1])
                    src = d["peer_wq_2"][0, :, j * COLS:(j + 1) * COLS]
                w = src.shape[1]
                load(ring[:, slot, :].rearrange("p (c n) -> p c n", c=DC)[:, :, 0:w],
                     src.rearrange("(c p) n -> p c n", p=P), arrived)

            for l in range(DEPTH):
                for name in LAYER_UNITS:
                    weights(UNIT[l, name])
                bank_filled(sp, (l, ("L", 8, 1)))
                load(ln_gb[:, 0:D_MODEL], d["ln_g"][l:l + 1, :].to_broadcast([P, D_MODEL]), "gb_load")
                load(ln_gb[:, D_MODEL:], d["ln_b"][l:l + 1, :].to_broadcast([P, D_MODEL]), "gb_load")
            for n in range(RING):
                weights(UNIT[B2, "AD0"] + n)
            after(sp, "x_next", DEPTH - 1, 1)
            load(mod[:, :], d["b_ada_2"].to_broadcast([P, 6 * D_MODEL]), "mod_load")
            for j, name in enumerate(("norm1_g_2", "norm2_g_2")):
                load(gain[:, j, :], d[name].to_broadcast([P, D_MODEL]), "b2_load")
            load(final_g, d["final_g_2"].rearrange("(o n) -> o n", o=1).to_broadcast([P, D_MODEL]), "b2_load")
            load(count[:, :, :], d["c_count"].rearrange("(a p) s -> p a s", p=P), "b2_load")
            load(dist[:, :, :], d["c_dist"].rearrange("(a p) s -> p a s", p=P), "b2_load")
            load(inv_count, d["c_inv_count"].to_broadcast([P, 4 * T]), "b2_load")
            load(w_pool, d["pool_w_2"].rearrange("o g c e -> c (o g) e"), "b2_load")
            load(sub_rows.rearrange("p (a k) -> p a k", a=2), d["peer_subkeys_2"].rearrange("o a n k -> n (o a) k"),
                 "b2_load")
            load(iota, d["c_iota"].to_broadcast([P, 16]), "b2_load")
            for n in range(UNIT[B2, "AD0"] + RING, len(STREAM)):
                weights(n)
            sp.wait_ge(sem("result"), TT)
            sp.dma_start(out.rearrange("(a p) n -> p a n", p=P), x[:, :, :]).then_inc(sem("out_store"), 16)
            sp.wait_ge(sem("out_store"), 16)

        @block.gpsimd
        def _(pool):
            tables = [d["peer_u_2"].rearrange("o e n -> (o e) n"), d["peer_v_2"].rearrange("o e n -> (o e) n")]
            run = 0
            for table in tables:
                for t in range(TT):
                    if table is tables[0]:
                        pool.wait_ge(sem("experts"), t + 1)
                    with pool.Fori(0, TURNS) as turn:
                        for half in range(2):
                            pool.wait_ge(sem("slots_free"), turn * GSLOTS + (PICKS * run + (half + 1) * GHALF))
                            pool.sem_inc(sem("gather_turn"), 1)
                            idx = turn_idx[:, half * GHALF:(half + 1) * GHALF]
                            nc.gpsimd.tensor_copy(idx, expert[:, t, bass.ds(turn * GSLOTS + half * GHALF, GHALF)])\
                              .then_inc(sem("idx_ready"), 1)
                            pool.wait_ge(sem("idx_ready"), turn * 2 + (2 * TURNS * run + half + 1))
                            pool.sem_inc(sem("gather_turn"), 1)
                            for k in range(GHALF):
                                slot = half * GHALF + k
                                pool.indirect_dma_start(
                                    gslot[slot], None, table,
                                    bass.IndirectOffsetOnAxis(ap=idx[:, k:k + 1], axis=0))\
                                    .then_inc(sem(f"row_load{slot}"), 16)
                    run += 1

        @block.tensor
        def _(pe):
            def last(ins, name="bank_filled"):
                ins.then_inc(sem(name), 1)

            def transposes(key, pairs):
                bank_empty(pe, key)
                for dst, src in pairs:
                    ins = nc.tensor.transpose(dst, src, eye[:, :])
                last(ins)

            def loaded(l, name):
                n = UNIT[l, name]
                pe.wait_ge(sem(f"ring_load{n % RING}"), ring_loads(n))
                return n % RING

            def channel_major(l, name, act, width=COLS):
                slot = loaded(l, name)
                w = ring[:, slot, :].rearrange("p (c n) -> p c n", c=DC)
                s, use = BIG[l, name]
                if use:
                    pe.wait_ge(sem(f"pj_free{s}"), use)
                for m in range(0, width, P):
                    n = min(P, width - m)
                    for c in range(DC):
                        ins = nc.tensor.matmul(pj[s][0:n, 2 * m:2 * m + T], w[:, c, m:m + n], act[:, c, :],
                                               start=(c == 0), stop=(c == DC - 1))
                last(ins, "unit_done")

            def token_major(l, name, act):
                slot = loaded(l, name)
                w = ring[:, slot, :].rearrange("p (c n) -> p c n", c=DC)
                s, use = BIG[l, name]
                if use:
                    pe.wait_ge(sem(f"pj_free{s}"), use)
                for t in range(TT):
                    for c in range(DC):
                        ins = nc.tensor.matmul(pj[s][:, t * COLS:(t + 1) * COLS], act[:, c, t * P:(t + 1) * P],
                                               w[:, c, :], start=(c == 0), stop=(c == DC - 1))
                last(ins, "unit_done")

            pe.wait_ge(sem("consts_load"), 16 * N_CONST)
            pe.wait_ge(sem("mem_load"), 16)
            pe.wait_ge(sem("ones_ready"), 1)
            mem = big[:, 0, :].rearrange("p (a n) -> p a n", a=TT)
            for j in range(4):
                B = bank[BANK["M", j] % 4]
                transposes(("M", j), [(B[:, (cc * TT + a) * P:(cc * TT + a + 1) * P],
                                       mem[:, a, (2 * j + cc) * P:(2 * j + cc + 1) * P])
                                      for cc in range(2) for a in range(TT)])
            transposes("VEC", [(bank_of("VEC")[:, 0:P], vec_rows)])
            def output_product(l, units):
                for s in range(2):
                    pe.wait_ge(sem(f"pj_free{s}"), BIG[l, "OUT"][s])
                for j in range(units):
                    slot = loaded(l, f"O{j}")
                    w = ring[:, slot, :].rearrange("p (c n) -> p c n", c=4)
                    for t in range(TT):
                        for n in range(2):
                            for c in range(4):
                                ins = nc.tensor.matmul(
                                    pj[t][:, n * 512:(n + 1) * 512], yT[:, 4 * j + c, t * P:(t + 1) * P],
                                    w[:, c, n * 512:(n + 1) * 512],
                                    start=(j == 0 and c == 0), stop=(j == units - 1 and c == 3))
                    last(ins, "unit_done")

            def scores(l, i, q, k):
                key = (l, ("S", i))
                bank_empty(pe, key)
                B = bank_of(key)
                for t in range(TT):
                    ins = nc.tensor.matmul(B[:, t * T:(t + 1) * T], q[:, t * P:(t + 1) * P], k, start=True, stop=True)
                last(ins)

            def weights_transposed(l, i):
                key = (l, ("PT", i))
                after(pe, "p_ready", l, i)
                B = bank_of(key)
                transposes(key, [(B[:, s * T + t * P:s * T + (t + 1) * P], sm[:, i % 2, t, s * P:(s + 1) * P])
                                 for s in range(TT) for t in range(TT)])

            def values_summed(l, i, rows, v):
                key = (l, ("AO", i))
                bank_empty(pe, key)
                after(pe, "pt_ready", l, i)
                for s in range(TT):
                    ins = nc.tensor.matmul(bank_of(key)[rows, 0:T], v[s], pT[:, i % 2, s, :],
                                           start=(s == 0), stop=(s == TT - 1))
                last(ins)

            def transposed_x(l, task, src):
                for j in range(4):
                    B = bank_of((l, (task, j)))
                    transposes((l, (task, j)), [(B[:, (cc * TT + a) * P:(cc * TT + a + 1) * P],
                                                 src[:, a, (2 * j + cc) * P:(2 * j + cc + 1) * P])
                                                for cc in range(2) for a in range(TT)])
                after(pe, "xT_ready", l, 3 if task == "X" else 7)

            def attention(l, i):
                if i < N_ATT:
                    if i < MLA_HEADS:
                        after(pe, "qrope_ready", l, i // 2)
                        after(pe, "uk_ready", l, i // 2)
                        after(pe, "kr_spread", l)
                        scores(l, i, qM[:, i, :], kM[:, i, :])
                    else:
                        after(pe, "qE_ready", l)
                        after(pe, "kE_ready", l)
                        scores(l, i, qE[:, i - MLA_HEADS, :], kE[:, i - MLA_HEADS, :])
                if 1 <= i <= N_ATT:
                    weights_transposed(l, i - 1)
                if i >= 2:
                    k = i - 2
                    if k < MLA_HEADS:
                        after(pe, "uv_ready", l, 1)
                        values_summed(l, k, slice(64 * (k % 2), 64 * (k % 2) + 64),
                                      [vM[:, s, k * 64:(k + 1) * 64] for s in range(TT)])
                    else:
                        after(pe, "vE_ready", l)
                        k -= MLA_HEADS
                        values_summed(l, i - 2, slice(0, P), [vE[:, s, k * P:(k + 1) * P] for s in range(TT)])

            def level(l, m):
                if m == 0:
                    after(pe, "k_ready", l)
                    after(pe, "q_ready", l, 1)
                else:
                    after(pe, "lvl_ready", l, m - 1)
                W = big[:, m % 3, :].rearrange("p (h t) -> p h t", t=T)
                for j in range(4 if m < 8 else 2):
                    key = (l, ("L", m, j))
                    bank_empty(pe, key)
                    B = bank_of(key)
                    for g in range(4):
                        if m == 8:
                            k, q = W[:, 4 * j + g, 0:P], W[:, 4 * j + g, P:T]
                        else:
                            h, t = (4 * j + g) // TT, (4 * j + g) % TT
                            q = W[:, h, t * P:(t + 1) * P]
                            k = q
                            if m == 0:
                                q, k = qT[:, h, t * P:(t + 1) * P], kT[:, h, t * P:(t + 1) * P]
                        ins = nc.tensor.matmul(B[:, g * P:(g + 1) * P], k, q, start=True, stop=True)
                    last(ins)

            def readout(l, i):
                if i < 4:
                    key = (l, ("HO", i))
                    bank_empty(pe, key)
                    after(pe, "blended", l, 8)
                    after(pe, "hv_ready", l, 1)
                    B = bank_of(key)
                    for k in range(2):
                        h = 2 * i + k
                        v = [hv[:, t, h * P:(h + 1) * P] for t in range(TT)]
                        o = B[:, k * T:(k + 1) * T]
                        nc.tensor.matmul(o[:, 0:P], v[0], pair[:, h * TT, :], start=True, stop=True)
                        nc.tensor.matmul(o[:, P:T], v[0], far_pair[:, h // 2, (h % 2) * P:(h % 2 + 1) * P],
                                         start=True, stop=False)
                        ins = nc.tensor.matmul(o[:, P:T], v[1], pair[:, h * TT + 1, :], start=False, stop=True)
                    last(ins)
                if i >= 1:
                    key = (l, ("HN", i - 1))
                    bank_empty(pe, key)
                    after(pe, "ho_sq", l, i - 1)
                    last(nc.tensor.matmul(bank_of(key)[:, :], ones_mean[:, :],
                                          sq[:, 0:2, :].rearrange("p a t -> p (a t)"), start=True, stop=True))

            for l in range(DEPTH):
                for task in TASKS:
                    if task == "X":
                        if l:
                            after(pe, "x_next", l - 1, 1)
                        else:
                            pe.wait_ge(sem("x_load"), 16)
                        transposed_x(l, "X", x)
                    elif task in ("G0", "G1", "GM", "GE", "F0", "F1", "Q0", "Q1", "C", "MQ"):
                        channel_major(l, task, xT, 416 if task == "C" else COLS)
                    elif task in ("I0", "I1"):
                        token_major(l, task, xT)
                    elif task == "MK":
                        channel_major(l, task, memT)
                    elif task == "MV":
                        token_major(l, task, memT)
                    elif task[0] == "L" and task != "LN":
                        level(l, int(task[1:]))
                    elif task[0] == "A":
                        attention(l, int(task[1:]))
                    elif task[0] == "H":
                        readout(l, int(task[1:]))
                    elif task == "N":
                        key = (l, ("N",))
                        bank_empty(pe, key)
                        after(pe, "c_sq", l)
                        B = bank_of(key)
                        for c in range(2):
                            nc.tensor.matmul(B[:, 0:T], ones_mean[:, :], sq[:, c, :], start=(c == 0), stop=(c == 1))
                        last(nc.tensor.matmul(B[:, T:2 * T], ones_mean[:, :], sq[:, 2, :], start=True, stop=True))
                        key = (l, ("KR",))
                        bank_empty(pe, key)
                        last(nc.tensor.matmul(bank_of(key)[0:32, 0:T], rot[0:32, :], cT[0:32, 3, :],
                                              start=True, stop=True))
                    elif task == "UP":
                        w_uq, w_uk, w_uv = up_weights(loaded(l, "UP"))
                        after(pe, "c_normed", l)
                        for j in range(4):
                            key = (l, ("UQ", j))
                            bank_empty(pe, key)
                            B = bank_of(key)
                            for k in range(2):
                                h = 2 * j + k
                                for c in range(2):
                                    ins = nc.tensor.matmul(B[0:96, k * T:(k + 1) * T], w_uq[:, c, h * 96:(h + 1) * 96],
                                                           cT[:, c, :], start=(c == 0), stop=(c == 1))
                            last(ins)
                        for j in range(4):
                            key = (l, ("UK", j))
                            bank_empty(pe, key)
                            for k in range(2):
                                h = 2 * j + k
                                ins = nc.tensor.matmul(bank_of(key)[0:64, k * T:(k + 1) * T],
                                                       w_uk[:, h * 64:(h + 1) * 64], cT[:, 2, :], start=True, stop=True)
                            last(ins)
                        for t in range(TT):
                            key = (l, ("UV", t))
                            bank_empty(pe, key)
                            last(nc.tensor.matmul(bank_of(key)[:, :], cT[:, 2, t * P:(t + 1) * P], w_uv,
                                                  start=True, stop=True))
                        pe.wait_ge(sem("bank_filled"), BANK[key] + 1)
                        pe.sem_inc(sem("unit_done"), 1)
                        for j in range(4):
                            key = (l, ("QR", j))
                            bank_empty(pe, key)
                            after(pe, "uq_ready", l, j)
                            last(nc.tensor.matmul(bank_of(key)[64:96, :], rot[64:96, :],
                                                  qM[64:96, 2 * j:2 * j + 2, :].rearrange("p a t -> p (a t)"),
                                                  start=True, stop=True))
                    elif task == "OUT":
                        after(pe, "y_hg", l, 3)
                        after(pe, "y_att", l, N_ATT - 1)
                        output_product(l, 4)
                        continue

            l = B2
            for task in TASKS2:
                if task[:2] == "AD":
                    slot = loaded(l, task)
                    w = ring[:, slot, :].rearrange("p (c n) -> p c n", c=DC)
                    s, use = BIG[l, task]
                    pe.wait_ge(sem(f"pj_free{s}"), use)
                    if task == "AD0":
                        pe.wait_ge(sem("silu_c"), 1)
                    for c in range(DC):
                        ins = nc.tensor.matmul(pj[s][:, 0:COLS], silu_c[:, c:c + 1].to_broadcast([P, P]), w[:, c, :],
                                               start=(c == 0), stop=(c == DC - 1))
                    last(ins, "unit_done")
                elif task in ("X", "X2"):
                    k = 0 if task == "X" else 1
                    pe.wait_ge(sem("h_ready"), k + 1)
                    transposed_x(l, task, normed)
                elif task in ("BQ", "BK", "BU", "K0", "K1", "K2", "K3"):
                    channel_major(l, task, xT)
                elif task == "BV":
                    token_major(l, task, xT)
                elif task == "PL":
                    pe.wait_ge(sem("b2_load"), 16 * N_B2)
                    pe.wait_ge(sem("pool_mixed"), 1)
                    for j in range(2):
                        key = (l, ("PL", j))
                        bank_empty(pe, key)
                        for g in range(2):
                            ins = nc.tensor.matmul(bank_of(key)[:, g * T:(g + 1) * T], w_pool[:, 2 * j + g, :],
                                                   mixed[:, 2 * j + g, :], start=True, stop=True)
                        last(ins)
                elif task == "SK":
                    transposes((l, ("SK",)), [(bank_of((l, ("SK",)))[:, k * P:(k + 1) * P],
                                               sub_rows[:, k * P:(k + 1) * P]) for k in range(2)])
                elif task[0] == "B":
                    i = int(task[1:])
                    if i == 0:
                        pe.wait_ge(sem("qkv2_ready"), 3)
                    if i < HEADS2:
                        r = slice(64 * (i % 2), 64 * (i % 2) + 64)
                        scores(l, i, q2[r, i // 2, :], k2[r, i // 2, :])
                    if 1 <= i <= HEADS2:
                        weights_transposed(l, i - 1)
                    if i >= 2:
                        k = i - 2
                        values_summed(l, k, slice(64 * (k % 2), 64 * (k % 2) + 64),
                                      [v2[:, s, k * 64:(k + 1) * 64] for s in range(TT)])
                elif task == "OUT":
                    pe.wait_ge(sem("y2_ready"), HEADS2 + 2)
                    output_product(l, 2)
                elif task[0] == "E":
                    i = int(task[1:])
                    key = (l, ("E", i))
                    bank_empty(pe, key)
                    pe.wait_ge(sem("skT_ready"), 1)
                    pe.wait_ge(sem("peer_q"), i // 2 + 1)
                    for t in range(TT):
                        for k in range(2):
                            g = 2 * t + k
                            ins = nc.tensor.matmul(bank_of(key)[:, g * P:(g + 1) * P],
                                                   yT[:, 2 * i + k, t * P:(t + 1) * P], skT[:, k, :],
                                                   start=True, stop=True)
                    last(ins)

        @block.scalar
        def _(act):
            a = nc.scalar
            do = steps(act, "act_step")
            for j in range(4):
                act.wait_ge(sem("bank_filled"), BANK["M", j] + 1)
                do(a.copy(memT[:, 2 * j:2 * j + 2, :].rearrange("p a t -> p (a t)"), bank_of(("M", j))[:, :]),
                   *bank_free(("M", j)))
            act.wait_ge(sem("angles"), 1)
            do(a.activation(rope[:, 1, :], big[:, 1, 0:T], ACT.Sin))
            do(a.activation(rope[:, 0, :], big[:, 1, T:2 * T], ACT.Sin), "rope_ready")
            act.wait_ge(sem("lb_centred"), 1)
            do(a.activation(lbt[:, 1:3, :], lbt[:, 1:3, :], ACT.Exp), "lb_exp")

            act.wait_ge(sem("vec_ready"), 1)
            do(a.activation(silu_c, vec[:, V_C:V_C + DC], ACT.Silu), "silu_c")

            def freed(l, name):
                s, use = BIG[l, name]
                return f"pj_free{s}", use + 1

            def transposed_x(l, task):
                for j in range(4):
                    key = (l, (task, j))
                    bank_filled(act, key)
                    do(a.copy(xT[:, 2 * j:2 * j + 2, :].rearrange("p a t -> p (a t)"), bank_of(key)[:, :]),
                       *bank_free(key))
                    act.sem_inc(sem("xT_ready"), 1)

            def exps(l, i):
                after(act, "sm_ready", l, i)
                st = stat[:, 4 * (i % 2):4 * (i % 2) + 4]
                for t in range(TT):
                    do(a.activation(sm[:, i % 2, t, :], sm[:, i % 2, t, :], ACT.Exp, bias=st[:, t:t + 1],
                                    accum_out=st[:, 2 + t:3 + t]), "exp_done" if t == TT - 1 else None)

            def weights_transposed(l, i):
                key = (l, ("PT", i))
                bank_filled(act, key)
                do(a.copy(pT[:, i % 2, :, :].rearrange("p a t -> p (a t)"), bank_of(key)[:, :]), *bank_free(key))
                act.sem_inc(sem("pt_ready"), 1)

            def row_norm(src, t, e, scale, done):
                do(a.activation(sm[:, :, :, :].rearrange("p a b t -> p (a b t)"), src, ACT.Square,
                                accum_out=stat[:, 10 + t:11 + t]))
                do(a.activation(stat[:, 12 + t:13 + t], stat[:, 10 + t:11 + t], ACT.Ln, scale=scale, bias=e))
                do(a.activation(stat[:, 12 + t:13 + t], stat[:, 12 + t:13 + t], ACT.Exp, scale=-0.5), done)

            for l in range(DEPTH):
                for task in TASKS:
                    if (l, task) in BIG and task != "OUT":
                        s, _ = BIG[l, task]
                    if task == "X":
                        if l:
                            unit_done(act, l - 1, "MQ")
                        transposed_x(l, "X")
                    elif task in ("G0", "G1", "GM", "GE"):
                        g = ("G0", "G1", "GM", "GE").index(task)
                        if l and g == 0:
                            unit_done(act, l - 1, "O3")
                        unit_done(act, l, task)
                        do(a.activation(yT[:, 4 * g:4 * g + 4, :].rearrange("p a t -> p (a t)"), pj[s][:, :], ACT.Silu),
                           *freed(l, task))
                        if g == 3:
                            act.sem_inc(sem("gates"), 1)
                    elif task == "FP":
                        after(act, "fz", l, 1)
                        do(a.activation(big[:, 0, :], big[:, 0, :], ACT.Exp, scale=-1.0), "f_exp")
                        do(a.activation(big[:, 2, :], big[:, 0, :], ACT.Ln, bias=1.0))
                        after(act, "f_pos", l)
                        do(a.activation(big[:, 1, :], big[:, 1, :], ACT.Ln, bias=1.0), "f_ln")
                    elif task in ("Q0", "Q1"):
                        q = int(task[1])
                        unit_done(act, l, task)
                        if l:
                            after(act, "blended", l - 1, 8)
                        do(a.copy(qT[:, 4 * q:4 * q + 4, :].rearrange("p a t -> p (a t)"), pj[s][:, :]), *freed(l, task))
                        act.sem_inc(sem("q_ready"), 1)
                    elif task == "C":
                        unit_done(act, l, task)
                        do(a.copy(cT[0:32, 3, :], pj[s][0:32, 3 * T:4 * T]))
                        do(a.copy(cT[:, 0:3, :].rearrange("p a t -> p (a t)"), pj[s][:, 0:3 * T]), *freed(l, task))
                        act.sem_inc(sem("c_ready"), 1)
                        if l:
                            bank_filled(act, (l - 1, ("HN", 3)))
                        do(a.activation(sq[:, :, :], cT[:, 0:3, :], ACT.Square), "c_sq")
                    elif task[:2] == "Da":
                        m = int(task[2])
                        after(act, "lvl_sub", l, m - 1)
                        do(a.activation(big[:, m % 3, :], big[:, m % 3, :], ACT.Exp), "lvl_exp")
                    elif task == "N":
                        key = (l, ("N",))
                        bank_filled(act, key)
                        B = bank_of(key)
                        do(a.activation(rstd[:, 0, :], B[:, 0:T], ACT.Ln, scale=P / Q_RANK, bias=eps[:, 0:1]))
                        do(a.activation(rstd[:, 1, :], B[:, T:2 * T], ACT.Ln, bias=eps[:, 0:1]))
                        do(a.activation(rstd[:, :, :], rstd[:, :, :], ACT.Exp, scale=-0.5), "c_rstd")
                        after(act, "kr_ready", l)
                        do(a.copy(kM[64:96, :, :], cT[0:32, 3:4, :].to_broadcast([32, MLA_HEADS, T])), "kr_spread")
                    elif task == "UP":
                        for j in range(4):
                            key = (l, ("UQ", j))
                            bank_filled(act, key)
                            do(a.copy(qM[:, 2 * j:2 * j + 2, :].rearrange("p a t -> p (a t)"), bank_of(key)[0:96, :]),
                               *bank_free(key))
                            act.sem_inc(sem("uq_ready"), 1)
                        for j in range(4):
                            key = (l, ("UK", j))
                            bank_filled(act, key)
                            do(a.copy(kM[0:64, 2 * j:2 * j + 2, :].rearrange("p a t -> p (a t)"), bank_of(key)[0:64, :]),
                               *bank_free(key))
                            act.sem_inc(sem("uk_ready"), 1)
                        for t in range(TT):
                            key = (l, ("UV", t))
                            bank_filled(act, key)
                            do(a.copy(vM[:, t, :], bank_of(key)[:, :]), *bank_free(key))
                            act.sem_inc(sem("uv_ready"), 1)
                    elif task in ("I0", "I1"):
                        q = int(task[1])
                        unit_done(act, l, task)
                        do(a.copy(hv[:, :, q * COLS:(q + 1) * COLS], pj[s][:, :].rearrange("p (a n) -> p a n", a=TT)),
                           *freed(l, task))
                        act.sem_inc(sem("hv_ready"), 1)
                    elif task in ("MQ", "MK", "MV"):
                        unit_done(act, l, task)
                        dst, done = {"MQ": (qE, "qE_ready"), "MK": (kE, "kE_ready"), "MV": (vE, "vE_ready")}[task]
                        do(a.copy(dst[:, :, :].rearrange("p a t -> p (a t)"), pj[s][:, :]), *freed(l, task))
                        act.sem_inc(sem(done), 1)
                    elif task[0] == "A":
                        i = int(task[1:])
                        if i < N_ATT:
                            exps(l, i)
                        if 1 <= i <= N_ATT:
                            weights_transposed(l, i - 1)
                    elif task[0] == "H":
                        j = int(task[1:])
                        if j >= 1:
                            key = (l, ("HN", j - 1))
                            bank_filled(act, key)
                            if j >= 2:
                                after(act, "y_hg", l, j - 2)
                            do(a.activation(rstd[:, :, :].rearrange("p a t -> p (a t)"), bank_of(key)[:, :], ACT.Ln,
                                            bias=eps[:, 0:1]))
                            do(a.activation(rstd[:, :, :], rstd[:, :, :], ACT.Exp, scale=-0.5), "ho_rstd")
                        if j < 4:
                            key = (l, ("HO", j))
                            bank_filled(act, key)
                            do(a.activation(sq[:, 0:2, :].rearrange("p a t -> p (a t)"), bank_of(key)[:, :], ACT.Square),
                               "ho_sq")
                    elif task == "LN":
                        for t in range(TT):
                            after(act, "ln_in", l, t)
                            row_norm(x[:, t, :], t, eps[:, 1:2], 1.0 / D_MODEL, "ln_rstd")

            l = B2
            pools = 0
            for task in TASKS2:
                if task in ("R1", "R2"):
                    for t in range(TT):
                        if task == "R1":
                            after(act, "x_next", DEPTH - 1, t)
                        else:
                            act.wait_ge(sem("x_mid"), t + 1)
                        row_norm(x[:, t, :], t, eps[:, 0:1], 1.0 / D_MODEL, "row_rstd")
                elif task in ("X", "X2"):
                    if task == "X2":
                        unit_done(act, l, "BU")
                    transposed_x(l, task)
                elif task in ("BQ", "BK", "BV", "BU"):
                    s, _ = BIG[l, task]
                    unit_done(act, l, task)
                    dst = {"BQ": q2, "BK": k2, "BV": v2[:, :, :], "BU": uT}[task]
                    dst = dst.rearrange("p a t -> p (a t)")
                    if task == "BQ":
                        do(a.mul(dst, pj[s][:, :], HD2 ** -0.5), *freed(l, task))
                    else:
                        do(a.copy(dst, pj[s][:, :]), *freed(l, task))
                    act.sem_inc(sem("uT_ready" if task == "BU" else "qkv2_ready"), 1)
                elif task == "PL":
                    for j in range(2):
                        key = (l, ("PL", j))
                        bank_filled(act, key)
                        for g in range(2):
                            c = 2 * j + g
                            do(a.activation(yT[:, 4 + c, :], bank_of(key)[:, g * T:(g + 1) * T], ACT.Copy,
                                            scale=vec[:, V_POOL + c:V_POOL + c + 1]),
                               *(bank_free(key) if g else ()))
                        act.sem_inc(sem("y2_ready"), 1)
                elif task == "SK":
                    key = (l, ("SK",))
                    bank_filled(act, key)
                    do(a.copy(flat(sq)[:, 512:768], bank_of(key)[:, 0:2 * P]), *bank_free(key))
                    act.sem_inc(sem("skT_ready"), 1)
                elif task[0] == "B":
                    i = int(task[1:])
                    if i < HEADS2:
                        exps(l, i)
                    if 1 <= i <= HEADS2:
                        weights_transposed(l, i - 1)
                    if i >= 2:
                        k = i - 2
                        key = (l, ("AO", k))
                        bank_filled(act, key)
                        r = slice(64 * (k % 2), 64 * (k % 2) + 64)
                        do(a.copy(yT[r, k // 2, :], bank_of(key)[r, 0:T]), *bank_free(key))
                        act.sem_inc(sem("y2_ready"), 1)
                elif task[0] == "K":
                    j = int(task[1:])
                    s, _ = BIG[l, task]
                    unit_done(act, l, task)
                    do(a.copy(yT[:, 4 * j:4 * j + 4, :].rearrange("p a t -> p (a t)"), pj[s][:, :]), *freed(l, task))
                    act.sem_inc(sem("peer_q"), 1)
                elif task[0] == "E":
                    i = int(task[1:])
                    key = (l, ("E", i))
                    bank_filled(act, key)
                    if i >= 2:
                        act.wait_ge(sem("sub_best"), i - 1)
                    do(a.copy(sm[:, i % 2, :, :].rearrange("p a t -> p (a t)"), bank_of(key)[:, :]), *bank_free(key))
                    act.sem_inc(sem("sub_scores"), 1)
            for t in range(TT):
                act.wait_ge(sem("top_centred"), t + 1)
                do(a.activation(top_val[:, t], top_val[:, t], ACT.Exp), "top_exp")
            for t in range(TT):
                act.wait_ge(sem("dots_ready"), t + 1)
                do(a.activation(dots[:, t, :], dots[:, t, :], ACT.Gelu), "gelu_done")
            for t in range(TT):
                act.wait_ge(sem("x_last"), t + 1)
                row_norm(x[:, t, :], t, eps[:, 0:1], 1.0 / D_MODEL, "row_rstd")

        @block.vector
        def _(dve):
            v = nc.vector
            do = steps(dve, "dve_step")
            do(v.memset(vec_rows, 0.0), "vec_zeroed")
            do(v.memset(ones_mean[:, :], 1.0 / P), "ones_ready")
            do(v.memset(eps[:, 0:1], RMS_EPS))
            do(v.memset(eps[:, 1:2], LN_EPS))
            dve.wait_ge(sem("bank_filled"), BANK["VEC"] + 1)
            do(v.tensor_copy(vec[:, :], bank_of("VEC")[:, 0:40]), *bank_free("VEC"))
            dve.sem_inc(sem("vec_ready"), 1)
            dve.wait_ge(sem("consts_load"), 16 * N_CONST)
            ang, turns = big[:, 1, T:2 * T], big[:, 1, 2 * T:3 * T]
            do(v.tensor_copy(ang, big[:, 1, 0:T].bitcast(i32)))
            do(v.tensor_scalar(ang, ang, vec[:, V_INV:V_INV + 1], None, ALU.mult))
            MAGIC = 12582912.0
            do(v.tensor_scalar(turns, ang, 1.0 / (2 * np.pi), None, ALU.mult))
            do(v.tensor_scalar(turns, turns, MAGIC, None, ALU.add))
            do(v.tensor_scalar(turns, turns, MAGIC, None, ALU.subtract))
            C1 = 6.28125
            C2 = float(np.float32(int((2 * np.pi - C1) * 2 ** 20) / 2 ** 20))
            C3 = 2 * np.pi - C1 - C2
            for c in (C1, C2, C3):
                do(v.scalar_tensor_tensor(out=ang, in0=turns, scalar=-c, in1=ang, op0=ALU.mult, op1=ALU.add))
            PI = 3.1415925
            do(v.tensor_scalar(big[:, 1, 0:T], ang, PI, -PI, ALU.min, ALU.max))
            do(v.tensor_scalar(turns, ang, float(np.pi / 2), -2 * np.pi, ALU.is_gt, ALU.mult))
            do(v.tensor_tensor(ang, ang, turns, ALU.add))
            do(v.tensor_scalar(ang, ang, float(np.pi / 2), PI, ALU.add, ALU.min))
            do(v.tensor_scalar(ang, ang, -PI, None, ALU.max), "angles")
            do(v.tensor_copy(level_mask[:, :, :].rearrange("p m t -> p (m t)"), big[:, 1, 800:1696].bitcast(i32)))
            l0, l1 = vec[:, V_LB:V_LB + 8], vec[:, V_LB + 8:V_LB + 16]
            do(v.tensor_tensor(lbt[:, 0, :], l0, l1, ALU.max))
            do(v.tensor_tensor(lbt[:, 1, :], l0, lbt[:, 0, :], ALU.subtract))
            do(v.tensor_tensor(lbt[:, 2, :], l1, lbt[:, 0, :], ALU.subtract), "lb_centred")
            dve.wait_ge(sem("lb_exp"), 1)
            do(v.tensor_tensor(lbt[:, 3, :], lbt[:, 1, :], lbt[:, 2, :], ALU.add))
            do(v.reciprocal(lbt[:, 3, :], lbt[:, 3, :]))
            do(v.tensor_tensor(lbt[:, 1:3, :], lbt[:, 1:3, :], lbt[:, 3:4, :].to_broadcast([P, 2, 8]), ALU.mult))
            do(v.tensor_tensor(lower[:, 0, 0, :], lbt[:, 1, :], lbt[:, 1, :], ALU.subtract))
            do(v.tensor_tensor(lower[:, 1, 0, :], lbt[:, 1, :], lbt[:, 2, :], ALU.add))
            do(v.tensor_tensor(lower[:, 1, 0, :], lower[:, 1, 0, :], lbt[:, 1, :], ALU.subtract))
            do(v.tensor_scalar(lower[:, :, 1, :], lower[:, :, 0, :], -1.0, 1.0, ALU.mult, ALU.add))
            dve.wait_ge(sem("rope_ready"), 1)
            cos, sin = rope[:, 0, :], rope[:, 1, :]

            def refine(y, mean, e, tmp, scale=1.0, free=None):
                do(v.tensor_scalar(tmp, mean, scale, e, ALU.mult, ALU.add), *(free or ()))
                do(v.tensor_tensor(tmp, tmp, y, ALU.mult))
                do(v.tensor_tensor(tmp, tmp, y, ALU.mult))
                do(v.tensor_scalar(tmp, tmp, -0.5, 1.5, ALU.mult, ALU.add))
                do(v.tensor_tensor(y, y, tmp, ALU.mult))

            def heads(tile3, j=None):
                return big[:, tile3, :].rearrange("p (h t) -> p h t", t=T)

            def wide(x3):
                return x3.rearrange("p h t -> p (h t)")

            def level_views(l, m):
                if m == 8:
                    W = heads(m % 3)
                    return (b[:, :, 0:P], b[:, :, P:T], W[:, :, 0:P], W[:, :, P:T], kT[:, :, 0:P], qT[:, :, P:T],
                            b[:, :, P - 1:P].to_broadcast([P, HG_HEADS, P]))
                h = 2 ** (m - 1)
                n = HG_HEADS * T // (2 * h)

                def split(y):
                    z = y.rearrange("p (n two m) -> p n two m", two=2, m=h)
                    return z[:, :, 0, :], z[:, :, 1, :]
                b0, b1 = split(wide(b[:, :, :]))
                w0, w1 = split(big[:, m % 3, :])
                return (b0, b1, w0, w1, split(wide(kT[:, :, :]))[0], split(wide(qT[:, :, :]))[1],
                        b0[:, :, h - 1:h].to_broadcast([P, n, h]))

            for l in range(DEPTH):
                for task in TASKS:
                    if task in ("F0", "F1"):
                        q = int(task[1])
                        s, use = BIG[l, task]
                        unit_done(dve, l, task)
                        do(v.tensor_scalar(big[:, 0, q * 1024:(q + 1) * 1024], pj[s][:, :], -44.0, None, ALU.max),
                           f"pj_free{s}", use + 1)
                        dve.sem_inc(sem("fz"), 1)
                    elif task == "FP":
                        after(dve, "f_exp", l)
                        lb = lower[:, l, 0, :].unsqueeze(2).to_broadcast([P, HG_HEADS, T])
                        omlb = lower[:, l, 1, :].unsqueeze(2).to_broadcast([P, HG_HEADS, T])
                        do(v.tensor_tensor(heads(1), heads(0), lb, ALU.mult), "f_pos")
                        after(dve, "f_ln", l)
                        do(v.tensor_tensor(big[:, 2, :], big[:, 1, :], big[:, 2, :], ALU.subtract))
                        for g in range(HG_HEADS * TT):
                            seg = big[:, 2, g * P:(g + 1) * P]
                            do(v.tensor_tensor_scan(wide(b[:, :, :])[:, g * P:(g + 1) * P], seg, seg, 0.0,
                                                    ALU.add, ALU.bypass))
                        do(v.tensor_scalar(big[:, 1, :], big[:, 0, :], 1.0, None, ALU.add))
                        do(v.reciprocal(big[:, 1, :], big[:, 1, :]))
                        do(v.tensor_tensor(big[:, 0, :], big[:, 0, :], big[:, 1, :], ALU.mult))
                        if l:
                            bank_filled(dve, (l - 1, ("HO", 3)))
                        do(v.tensor_tensor(kT[:, :, :], heads(0), omlb, ALU.mult), "k_ready")
                    elif task[:2] == "Da":
                        m = int(task[2])
                        if m >= 4:
                            bank_filled(dve, (l, ("L", m - 3, 3)))
                        b0, b1, w0, w1, _, _, mid = level_views(l, m)
                        do(v.tensor_tensor(w0, mid, b0, ALU.subtract))
                        if m == 8:
                            do(v.tensor_copy(w1, b1), "lvl_sub")
                        else:
                            do(v.tensor_tensor(w1, b1, mid, ALU.subtract), "lvl_sub")
                    elif task[:2] == "Db":
                        m = int(task[2])
                        after(dve, "lvl_exp", l, m - 1)
                        _, _, w0, w1, k0, q1, _ = level_views(l, m)
                        if m == 1:
                            after(dve, "q_ready", l, 1)
                        do(v.tensor_tensor(w0, w0, k0, ALU.mult))
                        do(v.tensor_tensor(w1, w1, q1, ALU.mult), "lvl_ready")
                    elif task[0] == "L" and task != "LN":
                        m = int(task[1:])
                        for j in range(4 if m < 8 else 2):
                            key = (l, ("L", m, j))
                            bank_filled(dve, key)
                            B = bank_of(key)[:, :].rearrange("p (g t) -> p g t", t=P)
                            dst = pair[:, 4 * j:4 * j + 4, :]
                            if m == 0:
                                do(v.tensor_tensor(dst, B, eye[:, :].unsqueeze(1).to_broadcast([P, 4, P]), ALU.mult),
                                   *bank_free(key))
                            elif m < 8:
                                do(v.copy_predicated(dst, level_mask[:, m - 1:m, :].to_broadcast([P, 4, P]), B),
                                   *bank_free(key))
                            else:
                                do(v.tensor_copy(far_pair[:, 2 * j:2 * j + 2, :].rearrange("p a t -> p (a t)"),
                                                 bank_of(key)[:, :]), *bank_free(key))
                        dve.sem_inc(sem("blended"), 1)
                    elif task == "N":
                        after(dve, "c_rstd", l)
                        B = bank_of((l, ("N",)))
                        refine(rstd[:, 0, :], B[:, 0:T], RMS_EPS, sm[:, 0, 0, :], P / Q_RANK)
                        refine(rstd[:, 1, :], B[:, T:2 * T], RMS_EPS, sm[:, 0, 0, :], 1.0, bank_free((l, ("N",))))
                        for c in range(3):
                            g = V_QN + 2 * l + c if c < 2 else V_KN + l
                            do(v.scalar_tensor_tensor(out=cT[:, c, :], in0=cT[:, c, :], scalar=vec[:, g:g + 1],
                                                      in1=rstd[:, c // 2, :], op0=ALU.mult, op1=ALU.mult),
                               "c_normed" if c == 2 else None)
                        key = (l, ("KR",))
                        bank_filled(dve, key)
                        tmp = sm[0:32, 0, 0, :]
                        do(v.tensor_tensor(tmp, bank_of(key)[0:32, 0:T], sin[0:32, :], ALU.mult), *bank_free(key))
                        do(v.tensor_tensor(cT[0:32, 3, :], cT[0:32, 3, :], cos[0:32, :], ALU.mult))
                        do(v.tensor_tensor(cT[0:32, 3, :], cT[0:32, 3, :], tmp, ALU.add), "kr_ready")
                    elif task == "UP":
                        for j in range(4):
                            key = (l, ("QR", j))
                            bank_filled(dve, key)
                            r = slice(64, 96)
                            q = qM[r, 2 * j:2 * j + 2, :]
                            tmp = sm[r, 0, :, :]
                            B = bank_of(key)[r, :].rearrange("p (a t) -> p a t", a=2)
                            do(v.tensor_tensor(tmp, B, sin[r, :].unsqueeze(1).to_broadcast([32, 2, T]), ALU.mult),
                               *bank_free(key))
                            do(v.tensor_tensor(q, q, cos[r, :].unsqueeze(1).to_broadcast([32, 2, T]), ALU.mult))
                            do(v.tensor_tensor(q, q, tmp, ALU.add), "qrope_ready")
                    elif task[0] == "A":
                        i = int(task[1:])
                        st = stat[:, 4 * (i % 2):4 * (i % 2) + 4]
                        if i < N_ATT:
                            key = (l, ("S", i))
                            bank_filled(dve, key)
                            if i >= 2:
                                bank_filled(dve, (l, ("PT", i - 2)))
                            B = bank_of(key)[:, :].rearrange("p (a t) -> p a t", a=TT)
                            if i < MLA_HEADS:
                                do(v.scalar_tensor_tensor(out=sm[:, i % 2, :, :], in0=B, scalar=MLA_SCALE,
                                                          in1=causal[:, :, :], op0=ALU.mult, op1=ALU.add),
                                   *bank_free(key))
                            else:
                                do(v.tensor_scalar(sm[:, i % 2, :, :], B, MEM_SCALE, None, ALU.mult), *bank_free(key))
                            do(v.tensor_reduce(st[:, 0:2], sm[:, i % 2, :, :], X, ALU.max, negate=True), "sm_ready")
                        if i >= 2:
                            h = i - 2
                            key = (l, ("AO", h))
                            bank_filled(dve, key)
                            if h < MLA_HEADS:
                                r = slice(64 * (h % 2), 64 * (h % 2) + 64)
                                g = yT[r, 8 + h // 2, :]
                            else:
                                r = slice(0, P)
                                g = yT[:, 12 + h - MLA_HEADS, :]
                            after(dve, "gates", l)
                            do(v.tensor_tensor(g, bank_of(key)[r, 0:T], g, ALU.mult), *bank_free(key))
                            dve.sem_inc(sem("y_att"), 1)
                        if i < N_ATT:
                            after(dve, "exp_done", l, i)
                            do(v.reciprocal(st[:, 2:4], st[:, 2:4]))
                            P3 = sm[:, i % 2, :, :]
                            do(v.tensor_tensor(P3, P3, st[:, 2:4].unsqueeze(2).to_broadcast([P, TT, T]), ALU.mult),
                               "p_ready")
                    elif task[0] == "H":
                        j = int(task[1:])
                        if j < 4:
                            key = (l, ("HO", j))
                            after(dve, "ho_sq", l, j)
                            y = wide(yT[:, 2 * j:2 * j + 2, :])
                            do(v.scalar_tensor_tensor(out=y, in0=bank_of(key)[:, :], scalar=vec[:, V_OUT + l:V_OUT + l + 1],
                                                      in1=y, op0=ALU.mult, op1=ALU.mult), *bank_free(key))
                        if j >= 1:
                            after(dve, "ho_rstd", l, j - 1)
                            key = (l, ("HN", j - 1))
                            refine(wide(rstd[:, :, :]), bank_of(key)[:, :], RMS_EPS, big[:, 0, 0:2 * T], 1.0, bank_free(key))
                            y = wide(yT[:, 2 * j - 2:2 * j, :])
                            do(v.tensor_tensor(y, y, wide(rstd[:, :, :]), ALU.mult), "y_hg")
                    elif task == "LN":
                        unit_done(dve, l, "O3")
                        for t in range(TT):
                            do(v.scalar_tensor_tensor(out=x[:, t, :], in0=x[:, t, :], scalar=ALPHA, in1=pj[t][:, :],
                                                      op0=ALU.mult, op1=ALU.add, accum_out=stat[:, 8 + t:9 + t]),
                               f"pj_free{t}", BIG[l, "OUT"][t] + 1)
                            do(v.tensor_scalar(stat[:, 8 + t:9 + t], stat[:, 8 + t:9 + t], 1.0 / D_MODEL, None, ALU.mult))
                            do(v.tensor_scalar(x[:, t, :], x[:, t, :], stat[:, 8 + t:9 + t], None, ALU.subtract), "ln_in")
                        dve.wait_ge(sem("gb_load"), (l + 1) * 32)
                        for t in range(TT):
                            after(dve, "ln_rstd", l, t)
                            refine(stat[:, 12 + t:13 + t], stat[:, 10 + t:11 + t], LN_EPS, stat[:, 14:15], 1.0 / D_MODEL)
                            do(v.scalar_tensor_tensor(out=x[:, t, :], in0=x[:, t, :], scalar=stat[:, 12 + t:13 + t],
                                                      in1=ln_gb[:, 0:D_MODEL], op0=ALU.mult, op1=ALU.mult))
                            do(v.tensor_tensor(x[:, t, :], x[:, t, :], ln_gb[:, D_MODEL:], ALU.add), "x_next")


            l = B2
            shift1, scale1, gate1, shift2, scale2, gate2 = (mod[:, j * D_MODEL:(j + 1) * D_MODEL] for j in range(6))

            def norm_rows(part, scale_row, shift_row):
                for t in range(TT):
                    dve.wait_ge(sem("row_rstd"), TT * part + t + 1)
                    refine(stat[:, 12 + t:13 + t], stat[:, 10 + t:11 + t], RMS_EPS, stat[:, 14:15], 1.0 / D_MODEL)
                    do(v.scalar_tensor_tensor(out=normed[:, t, :], in0=x[:, t, :], scalar=stat[:, 12 + t:13 + t],
                                              in1=scale_row, op0=ALU.mult, op1=ALU.mult))
                    do(v.tensor_tensor(normed[:, t, :], normed[:, t, :], shift_row, ALU.add))
                dve.sem_inc(sem("h_ready"), 1)

            def best16(values, left, out_val, out_id, done=None):
                do(v.max(out_val[:, 0:8], values))
                do(v.match_replace(left, out_val[:, 0:8], values, -3e38))
                do(v.max(out_val[:, 8:16], left))
                do(v.max_index(out_id[:, 0:8], out_val[:, 0:8], values))
                do(v.max_index(out_id[:, 8:16], out_val[:, 8:16], left))

            for task in TASKS2:
                if task[:2] == "AD":
                    j = int(task[2:])
                    s, use = BIG[l, task]
                    unit_done(dve, l, task)
                    if j == 0:
                        dve.wait_ge(sem("mod_load"), 16)
                    m = mod[:, j * COLS:(j + 1) * COLS]
                    do(v.tensor_tensor(m, m, pj[s][:, 0:COLS], ALU.add), f"pj_free{s}", use + 1)
                elif task == "R1":
                    dve.wait_ge(sem("b2_load"), 16 * N_B2)
                    for k, row in enumerate((scale1, scale2)):
                        do(v.scalar_tensor_tensor(out=row, in0=row, scalar=1.0, in1=gain[:, k, :],
                                                  op0=ALU.add, op1=ALU.mult))
                    norm_rows(0, scale1, shift1)
                elif task == "PL":
                    dve.wait_ge(sem("uT_ready"), 1)
                    do(v.tensor_copy(pool_sum, uT))
                    for g in range(4):
                        for k in range(g + 1):
                            n = 2 ** k
                            spare = mixed[:, g, :]
                            do(v.tensor_copy(spare, pool_sum[:, g, :]))
                            do(v.tensor_tensor(pool_sum[:, g, n:T], spare[:, n:T], spare[:, 0:T - n], ALU.add))
                    do(v.tensor_tensor(mixed, pool_sum, inv_count.rearrange("p (a t) -> p a t", a=4), ALU.mult))
                    do(v.tensor_tensor(mixed, mixed, uT, ALU.subtract), "pool_mixed")
                elif task[0] == "B" and task[1:].isdigit():
                    i = int(task[1:])
                    if i < HEADS2:
                        st = stat[:, 4 * (i % 2):4 * (i % 2) + 4]
                        key = (l, ("S", i))
                        bank_filled(dve, key)
                        if i >= 2:
                            bank_filled(dve, (l, ("PT", i - 2)))
                        do(v.scalar_tensor_tensor(out=sm[:, i % 2, :, :], in0=dist, scalar=-2.0 ** -(i + 1),
                                                  in1=bank_of(key)[:, :].rearrange("p (a t) -> p a t", a=TT),
                                                  op0=ALU.mult, op1=ALU.add), *bank_free(key))
                        do(v.tensor_reduce(st[:, 0:2], sm[:, i % 2, :, :], X, ALU.max, negate=True), "sm_ready")
                        after(dve, "exp_done", l, i)
                        for t in range(TT):
                            do(v.scalar_tensor_tensor(out=sm[:, i % 2, t, :], in0=sm[:, i % 2, t, :], scalar=1.0,
                                                      in1=count[:, t, :], op0=ALU.mult, op1=ALU.mult,
                                                      accum_out=st[:, 2 + t:3 + t]))
                        do(v.reciprocal(st[:, 2:4], st[:, 2:4]))
                        P3 = sm[:, i % 2, :, :]
                        do(v.tensor_tensor(P3, P3, st[:, 2:4].unsqueeze(2).to_broadcast([P, TT, T]), ALU.mult),
                           "p_ready")
                elif task == "OUT":
                    unit_done(dve, l, "O1")
                    for t in range(TT):
                        tmp = sm[:, :, :, :].rearrange("p a b t -> p (a b t)")
                        if t:
                            dve.wait_ge(sem("row_rstd"), TT + t)
                        do(v.tensor_tensor(tmp, pj[t][:, :], gate1, ALU.mult), f"pj_free{t}", BIG[l, "OUT"][t] + 1)
                        do(v.tensor_tensor(x[:, t, :], x[:, t, :], tmp, ALU.add), "x_mid")
                elif task == "R2":
                    norm_rows(1, scale2, shift2)
                elif task[0] == "E":
                    i = int(task[1:])
                    dve.wait_ge(sem("sub_scores"), i + 1)
                    for t in range(TT):
                        for k in range(2):
                            best16(sm[:, i % 2, t, k * P:(k + 1) * P], cand_left[:, 0:P],
                                   sub_val[:, t, i, k, :], sub_id[:, t, i, k, :])
                    dve.sem_inc(sem("sub_best"), 1)
            for t in range(TT):
                do(v.tensor_copy(sub_idf[:, t], sub_id[:, t]))
                for e in range(PEER_HEADS):
                    do(v.tensor_tensor(cand.rearrange("p (i j) -> p i j", i=TOPK),
                                       sub_val[:, t, e, 0, :].unsqueeze(2).to_broadcast([P, TOPK, TOPK]),
                                       sub_val[:, t, e, 1, :].unsqueeze(1).to_broadcast([P, TOPK, TOPK]), ALU.add))
                    best16(cand, cand_left, top_val[:, t, e, :], top_pos[:, t, e * TOPK:(e + 1) * TOPK])
                for k, (op, arg, place, found) in enumerate(((ALU.logical_shift_right, 4, first_of, id_a),
                                                             (ALU.bitwise_and, 15, second_of, id_b))):
                    do(v.tensor_scalar(digit, top_pos[:, t, :], arg, None, op))
                    do(v.tensor_copy(place, digit))
                    do(v.tensor_tensor(onehot, iota.unsqueeze(1).to_broadcast([P, PICKS, TOPK]),
                                       place.unsqueeze(2).to_broadcast([P, PICKS, TOPK]), ALU.is_equal))
                    oh4 = onehot.rearrange("p (e j) i -> p e j i", e=PEER_HEADS)
                    do(v.tensor_tensor(oh4, oh4, sub_idf[:, t, :, k, :].unsqueeze(2)
                                       .to_broadcast([P, PEER_HEADS, TOPK, TOPK]), ALU.mult))
                    do(v.tensor_reduce(found, onehot, X, ALU.add))
                do(v.scalar_tensor_tensor(out=id_a, in0=id_a, scalar=float(NKEYS), in1=id_b,
                                          op0=ALU.mult, op1=ALU.add))
                do(v.tensor_copy(expert[:, t, :], id_a), "experts")
                if t == 0:
                    unit_done(dve, l, "K3")
                    bank_filled(dve, (l, ("E", PEER_HEADS - 1)))
                    dve.sem_inc(sem("slots_free"), GSLOTS)
                do(v.tensor_copy(stat[:, 0:8].unsqueeze(2), top_val[:, t, :, 0:1]))
                do(v.tensor_tensor(top_val[:, t], top_val[:, t],
                                   stat[:, 0:8].unsqueeze(2).to_broadcast([P, PEER_HEADS, TOPK]), ALU.subtract),
                   "top_centred")
                dve.wait_ge(sem("top_exp"), t + 1)
                do(v.tensor_reduce(stat[:, 0:8], top_val[:, t], X, ALU.add))
                do(v.reciprocal(stat[:, 0:8], stat[:, 0:8]))
                do(v.tensor_tensor(gate[:, t, :].rearrange("p (e j) -> p e j", e=PEER_HEADS), top_val[:, t],
                                   stat[:, 0:8].unsqueeze(2).to_broadcast([P, PEER_HEADS, TOPK]), ALU.mult))

            def rows(run, consume):
                with dve.Fori(0, TURNS) as turn:
                    for k in range(GSLOTS):
                        dve.wait_ge(sem(f"row_load{k}"), turn * 16 + (16 * TURNS * run + 16))
                        consume(k, turn * GSLOTS + k).then_inc(sem("slots_free"), 1)
                        dve.wait_ge(sem("slots_free"), turn * GSLOTS + (GSLOTS + PICKS * run + k + 1))

            for t in range(TT):
                rows(t, lambda k, j: v.scalar_tensor_tensor(
                    out=product, in0=gslot[k], scalar=1.0, in1=normed[:, t, :], op0=ALU.mult, op1=ALU.mult,
                    accum_out=dots[:, t, bass.ds(j, 1)]))
                dve.sem_inc(sem("dots_ready"), 1)
            do(v.memset(acc, 0.0))
            for t in range(TT):
                dve.wait_ge(sem("gelu_done"), t + 1)
                do(v.tensor_tensor(gate[:, t, :], gate[:, t, :], dots[:, t, :], ALU.mult))
                rows(TT + t, lambda k, j: v.scalar_tensor_tensor(
                    out=acc[:, t, :], in0=gslot[k], scalar=gate[:, t, bass.ds(j, 1)], in1=acc[:, t, :],
                    op0=ALU.mult, op1=ALU.add))
                do(v.tensor_tensor(acc[:, t, :], acc[:, t, :], gate2, ALU.mult))
                do(v.tensor_tensor(x[:, t, :], x[:, t, :], acc[:, t, :], ALU.add), "x_last")
                dve.wait_ge(sem("row_rstd"), 2 * TT + t + 1)
                refine(stat[:, 12 + t:13 + t], stat[:, 10 + t:11 + t], RMS_EPS, stat[:, 14:15], 1.0 / D_MODEL)
                do(v.scalar_tensor_tensor(out=x[:, t, :], in0=x[:, t, :], scalar=stat[:, 12 + t:13 + t],
                                          in1=final_g, op0=ALU.mult, op1=ALU.mult), "result")


_NAMES = ["x", "mem", "positions", "w_in", "hgrn_lb_logits", "hgrn_out_norm", "mla_q_norm", "mla_kv_norm",
          "w_mla_uq", "w_mla_uk", "w_mla_uv", "w_mem_k", "w_mem_v", "w_out", "ln_g", "ln_b", "c_2", "pool_scale_2",
          "w_ada_2", "b_ada_2", "norm1_g_2", "w_in_2", "pool_w_2", "w_out_2", "norm2_g_2", "peer_wq_2",
          "peer_subkeys_2", "peer_u_2", "peer_v_2", "final_g_2"]


def kernel(**inputs):
    import concourse.bacc as bacc
    from concourse import mybir
    from concourse.bass_utils import run_bass_kernel_spmd

    nc = bacc.Bacc("TRN2", target_bir_lowering=False, num_devices=1)
    arrays = {n: np.ascontiguousarray(inputs[n]) for n in _NAMES}
    arrays.update(constants())
    d = {n: nc.dram_tensor(f"in_{n}", a.shape, mybir.dt.from_np(a.dtype), kind="ExternalInput").ap()
         for n, a in arrays.items()}
    out = nc.dram_tensor("out", (T, D_MODEL), mybir.dt.float32, kind="ExternalOutput").ap()
    build(nc, d, out)
    got = run_bass_kernel_spmd(nc, [{f"in_{n}": a for n, a in arrays.items()}], core_ids=[0])
    return got.results[0]["out"].reshape(1, T, D_MODEL)
```

```python
import numpy as np

P = 128
D_MODEL = 1024
T = 256
TT = T // P
DC = D_MODEL // P
DEPTH = 2
HG_HEADS = 8
GROUPS, GH = 2, 4
MLA_HEADS, NOPE, ROPE, MLA_V = 8, 64, 32, 64
Q_RANK, KV_RANK = 256, 128
MEM_HEADS = 4
IN_WIDTH = 6048
N_LEVELS = 9
ALPHA = (2 * DEPTH) ** 0.25
MLA_SCALE = (NOPE + ROPE) ** -0.5
MEM_SCALE = 128 ** -0.5
RMS_EPS, LN_EPS = 1e-6, 1e-5
NEG_BIG = -1e30
COLS = 512
RING = 3

HEADS2, HD2 = 8, 64
PEER_HEADS, NKEYS, TOPK = 8, 128, 16
PICKS = PEER_HEADS * TOPK
GSLOTS = 16
GHALF = GSLOTS // 2
TURNS = PICKS // GSLOTS

IN_UNITS = [("G0", 3072), ("G1", 3584), ("GM", 4512), ("GE", 5536), ("F0", 1024), ("F1", 1536),
            ("Q0", 0), ("Q1", 512), ("C", 4096), ("I0", 2048), ("I1", 2560), ("MQ", 5024)]
B2 = DEPTH
N_MOD = 6
N_MOD_UNITS = N_MOD * D_MODEL // COLS

LAYER = """MK X C F0 N Q0 FP0 UP F1 Da01 L00 Da02 Db01 A0 L01 Da03 Db02 GM A1 L02 Da04 Db03 A2 AD L03
    Da05 Db04 Q1 A3 L04 Da06 Db05 A4 AD L05 Da07 Db06 I0 A5 L06 Da08 Db07 A6 AD L07 Db08 MV A7 L08 FP1 MQ AD A8
    G0 H00 Da11 H01 L10 Da12 Db11 A9 L11 Da13 Db12 GE A10 H02 L12 Da14 Db13 A11 L13 Da15 Db14 I1 A12
    L14 Da16 Db15 A13 G1 L15 Da17 Db16 A14 L16 Da18 Db17 O0 L17 Db18 O2 L18 H10 O3 AD H11 AD H12 O1 LN"""
BLOCK2 = """R1 X MB BQ BK B0 BV B1 BU PL B2 B3 B4 PM B5 SK B6 O1 B7 B8 B9 B10 O0
    OUT R2 X2 K0 K1 E0 E1 K2 E2 E3 K3 E4 E5 E6 E7"""


def all_tasks():
    out, n = [], 0
    for text in [LAYER] * DEPTH + [BLOCK2]:
        tasks = []
        for task in text.split():
            if task == "AD":
                task, n = f"AD{n}", n + 1
            tasks.append(task)
        out.append(tasks)
    assert n == N_MOD_UNITS
    return out


TASKS = all_tasks()
ONE_SLOT = {"MK", "MV", "C", "F0", "F1", "Q0", "Q1", "G0", "G1", "GM", "GE", "I0", "I1", "MQ",
            "BQ", "BK", "BV", "BU", "K0", "K1", "K2", "K3"}


def output_unit(task):
    return task[0] == "O" and task[1:].isdigit()


OUT_UNITS = [[task for task in tasks if output_unit(task)] for tasks in TASKS]


def stream():
    out = []
    for l, tasks in enumerate(TASKS):
        for task in tasks:
            if task in ONE_SLOT or task == "UP" or task[:2] == "AD" or output_unit(task):
                out.append((l, task))
    return out


STREAM = stream()
UNIT = {key: n for n, key in enumerate(STREAM)}


def big_uses():
    out, uses, turn = {}, [0, 0], 0
    for l, name in STREAM:
        if name == OUT_UNITS[l][0]:
            out[l, "OUT"] = tuple(uses)
            uses = [uses[0] + 1, uses[1] + 1]
            turn = 0
        elif name in ONE_SLOT:
            out[l, name] = (turn, uses[turn])
            uses[turn] += 1
            turn = 1 - turn
    return out


BIG = big_uses()
N_ATT = MLA_HEADS + MEM_HEADS


def bank_uses(task):
    if task in ("X", "X2"):
        return [(task, j) for j in range(4)]
    if task == "SK":
        return [("SK",)]
    if task == "PM":
        return [("PL", j) for j in range(2)]
    if task[0] == "E":
        return [("E", int(task[1:]))]
    if task[0] == "B" and task[1:].isdigit():
        i = int(task[1:])
        out = [("S", i)] if i < HEADS2 else []
        out += [("PT", i - 2)] if 2 <= i <= HEADS2 + 1 else []
        return out + ([("AO", i - 3)] if i >= 3 else [])
    if task[0] == "L" and task[1:].isdigit():
        g, m = int(task[1]), int(task[2])
        return [("L", g, m, j) for j in range(2 if m < 8 else 1)]
    if task[:2] == "AD":
        return [(task,)]
    if task == "MB":
        return [("MB", v, k) for v in range(4) for k in range(2)]
    if task == "N":
        return [("N",), ("KR",)]
    if task == "UP":
        return ([("UQ", j) for j in range(4)] + [("UK", j) for j in range(4)]
                + [("UV", t) for t in range(TT)] + [("QR", j) for j in range(4)])
    if task[0] == "A" and task[1:].isdigit():
        i = int(task[1:])
        out = [("S", i)] if i < N_ATT else []
        out += [("PT", i - 2)] if 2 <= i <= N_ATT + 1 else []
        return out + ([("AO", i - 3)] if i >= 3 else [])
    if task[0] == "H":
        g, i = int(task[1]), int(task[2])
        return ([("HO", 2 * g + i)] if i < 2 else []) + ([("HN", 2 * g + i - 1)] if i >= 1 else [])
    return []


def bank_index():
    out, n = {}, 0
    for j in range(4):
        out["M", j] = n
        n += 1
    out["VEC"] = n
    n += 1
    for l in range(DEPTH + 1):
        for task in TASKS[l]:
            for key in bank_uses(task):
                out[l, key] = n
                n += 1
    return out, n


def constants():
    i = np.arange(P)
    level = np.zeros((P, 7, P), np.int32)
    for m in range(1, 8):
        h = 2 ** (m - 1)
        same = (i[:, None] // (2 * h)) == (i[None, :] // (2 * h))
        level[:, m - 1] = same & ((i[:, None] // h) % 2 == 0) & ((i[None, :] // h) % 2 == 1)
    t = np.arange(T)
    causal = np.where(t[None, :] <= t[:, None], 0.0, NEG_BIG).astype(np.float32)
    rot = np.zeros((P, 32), np.float32)
    for j in range(16):
        for base in (0, 64):
            rot[base + j + 16, j] = -1.0
            rot[base + j, j + 16] = 1.0
    inv = np.float32(1.0) / (np.float32(10000.0) ** (np.arange(0, ROPE, 2, dtype=np.float32) / np.float32(ROPE)))
    dist = (t[:, None] - t[None, :])
    count = ((dist >= 0) & (dist <= 128)).astype(np.float32)
    for d in (4, 16):
        count += (dist >= 0) & (dist % d == 0)
    far = np.where(count > 0, dist, 1e30).astype(np.float32)
    inv_count = np.stack([1.0 / np.minimum(t + 1, w) for w in (2, 4, 8, 16)]).astype(np.float32)
    return {
        "c_eye": np.eye(P, dtype=np.float32),
        "c_level": level.reshape(P, 7 * P),
        "c_causal": causal, "c_rot": rot,
        "c_inv_freq": np.tile(inv, P // 16).reshape(1, P).astype(np.float32),
        "c_count": count, "c_dist": far, "c_inv_count": inv_count.reshape(1, 4 * T),
        "c_iota": np.arange(16, dtype=np.float32).reshape(1, 16),
    }


def build(nc, d, out, part="all"):
    import concourse.bass as bass
    from concourse import mybir
    from concourse.alu_op_type import AluOpType as ALU
    from contextlib import ExitStack

    f32, u32, i32, u8 = mybir.dt.float32, mybir.dt.uint32, mybir.dt.int32, mybir.dt.uint8
    ACT = mybir.ActivationFunctionType
    X = mybir.AxisListType.X
    BANK, N_BANK1 = bank_index()

    with ExitStack() as ctx:
        def sb(name, shape, dt=f32):
            return ctx.enter_context(nc.sbuf_tensor(name, shape, dt))

        eye = sb("eye", [P, P])
        ones_mean = sb("ones_mean", [P, P])
        rot = sb("rot", [P, 32])
        level_mask = sb("level_mask", [P, 7, P], u8)
        causal = sb("causal", [P, TT, T])
        vec = sb("vec", [P, 104])
        mod_part = sb("mod_part", [P, 2, COLS])
        modc = sb("modc", [P, N_MOD, DC])
        lower = sb("lower", [P, DEPTH, 2, 8])
        lbt = sb("lbt", [P, 6, 8])
        eps = sb("eps", [P, 3])
        rope = sb("rope", [P, 2, T])
        stat = sb("stat", [P, 16])
        x = sb("x", [P, TT, D_MODEL])
        xT = sb("xT", [P, DC, T])
        memT = sb("memT", [P, DC, T])
        ring = sb("ring", [P, RING, DC * COLS])
        yT = sb("yT", [P, 16, T])
        big = sb("big", [P, 3, GH * T])
        qT = sb("qT", [P, HG_HEADS, T])
        kT = sb("kT", [P, HG_HEADS, T])
        b = sb("b", [P, HG_HEADS, T])
        pair = sb("pair", [P, GH * TT, P])
        far_pair = sb("far_pair", [P, GH, P])
        hv = sb("hv", [P, TT, D_MODEL])
        cT = sb("cT", [P, 4, T])
        sq = sb("sq", [P, 3, T])
        rstd = sb("rstd", [P, 2, T])
        qM = sb("qM", [96, MLA_HEADS, T])
        kM = sb("kM", [96, MLA_HEADS, T])
        vM = sb("vM", [P, TT, MLA_HEADS * MLA_V])
        qE = sb("qE", [P, MEM_HEADS, T])
        kE = sb("kE", [P, MEM_HEADS, T])
        vE = sb("vE", [P, TT, MEM_HEADS * P])
        sm = sb("sm", [P, 2, TT, T])
        pT = sb("pT", [P, 2, TT, T])
        flat_b = b[:, :, :].rearrange("p a t -> p (a t)")
        vec_rows = flat_b[:, 1700:1700 + P]
        ln_gb = big[:, 0:2, :].rearrange("p a n -> p (a n)")

        flat_pair = pair[:, :, :].rearrange("p a t -> p (a t)")
        w_pool, iota = pair[:, 0:4, :], flat_pair[:, 512:528]
        sub_rows = flat_pair[:, 528:528 + 2 * P]
        row_gate1, row_scale2 = hv[:, 0, :], hv[:, 1, :]
        row_shift2, row_gate2, final_g = big[:, 0, :], big[:, 1, :], big[:, 2, :]
        q2, k2, v2 = qT[:, 0:4, :], qT[:, 4:8, :], vE
        uT, pool_sum = kT[:, 0:4, :], kT[:, 4:8, :]
        mixed, inv_count = b[:, 0:4, :], b[:, 4:8, :].rearrange("p a t -> p (a t)")
        count, dist = qE[:, 0:2, :], qE[:, 2:4, :]
        normed = memT[:, :, :].rearrange("p a t -> p (a t)").rearrange("p (a n) -> p a n", a=TT)
        silu_c = lbt[:, 4, :]

        def flat(tile):
            return tile[:, :, :].rearrange("p a t -> p (a t)")
        shape5 = dict(t=TT, h=PEER_HEADS, two=2)
        sub_val = flat(cT)[:, 0:512].rearrange("p (t h two k) -> p t h two k", **shape5)
        sub_idf = flat(cT)[:, 512:1024].rearrange("p (t h two k) -> p t h two k", **shape5)
        sub_id = flat(kE)[:, 0:512].bitcast(u32).rearrange("p (t h two k) -> p t h two k", **shape5)
        top_pos = flat(kE)[:, 512:768].bitcast(u32).rearrange("p (t j) -> p t j", t=TT)
        digit = flat(kE)[:, 768:896].bitcast(u32)
        top_val = flat(rstd)[:, 0:PICKS * TT].rearrange("p (t h k) -> p t h k", t=TT, h=PEER_HEADS)
        gate = flat(rstd)[:, PICKS * TT:].rearrange("p (t j) -> p t j", t=TT)
        skT = flat(sq)[:, 512:768].rearrange("p (a k) -> p a k", a=2)
        cand, cand_left = flat(sq)[:, 0:256], flat(sq)[:, 256:512]
        first_of, second_of = flat(vM)[:, 0:PICKS], flat(vM)[:, PICKS:2 * PICKS]
        id_a, id_b = flat(vM)[:, 2 * PICKS:3 * PICKS], flat(vM)[:, 3 * PICKS:4 * PICKS]
        expert = flat(vM)[:, 512:768].bitcast(u32).rearrange("p (t j) -> p t j", t=TT)
        dots = flat(vM)[:, 768:1024].rearrange("p (t j) -> p t j", t=TT)
        onehot = flat(qT).rearrange("p (j i) -> p j i", i=TOPK)
        gslot = ([ring[:, (UNIT[B2, "K3"] + s) % RING, g * D_MODEL:(g + 1) * D_MODEL]
                  for s in (1, 2, 0) for g in range(4)]
                 + [yT[:, 4 * g:4 * g + 4, :].rearrange("p a t -> p (a t)") for g in range(GSLOTS - 4 * RING)])
        turn_idx = causal[:, 0, 0:GSLOTS].bitcast(u32)
        acc = b[:, :, :].rearrange("p a t -> p (a t)").rearrange("p (a n) -> p a n", a=TT)
        product = pT[:, :, :, :].rearrange("p a b t -> p (a b t)")
        spare_product = hv[:, 0, :]
        later_scores = kT
        pj = [ctx.enter_context(nc.psum_tensor(f"pj{i}", [P, 1024], f32)) for i in range(2)]
        bank = [ctx.enter_context(nc.psum_tensor(f"bank{i}", [P, 512], f32)) for i in range(4)]

        made = {}

        def sem(name):
            if name not in made:
                made[name] = ctx.enter_context(nc.semaphore(name))
            return made[name]

        PER = dict(xT_ready=4, gates=4, fz=2, f_exp=2, f_pos=2, f_ln=2, k_ready=2, q_ready=2,
                   lvl_sub=16, lvl_exp=16, lvl_ready=16, blended=18, out_tile=1, c_ready=1, c_sq=1, c_rstd=1,
                   c_normed=1, kr_ready=1, kr_spread=1, uq_ready=4, qrope_ready=4, uk_ready=4,
                   uv_ready=2, hv_ready=2, qE_ready=1, kE_ready=1, vE_ready=1,
                   sm_ready=12, exp_done=12, p_ready=12, pt_ready=12, y_att=12,
                   ho_sq=4, ho_used=4, ho_rstd=4, y_hg=4, ln_in=2, ln_sq=2, ln_rstd=2, x_next=2)


        def after(eng, name, l, i=0):
            eng.wait_ge(sem(name), l * PER[name] + i + 1)

        GATE_OF = {name: n for n, name in enumerate(t for t in TASKS[0] if t in ("G0", "G1", "GM", "GE"))}

        def bank_of(key):
            return bank[BANK[key] % 4]

        def bank_filled(eng, key):
            eng.wait_ge(sem("bank_filled"), BANK[key] + 1)

        def bank_empty(eng, key):
            n = BANK[key]
            if n >= 4:
                eng.wait_ge(sem(f"bank_free{n % 4}"), n // 4)

        def bank_free(key):
            n = BANK[key]
            return f"bank_free{n % 4}", n // 4 + 1

        UQ_W = 2 * MLA_HEADS * (NOPE + ROPE)

        def up_weights(slot):
            w = ring[:, slot, :]
            return (w[:, 0:UQ_W].rearrange("p (c n) -> p c n", c=2), w[:, UQ_W:UQ_W + 512],
                    w[:, UQ_W + 512:UQ_W + 1024])

        def ring_loads(n):
            units = range(n % RING, n + 1, RING)
            return 16 * sum(3 if STREAM[k][1] == "UP" else 1 for k in units)

        def unit_done(eng, l, name):
            eng.wait_ge(sem("unit_done"), UNIT[l, name] + 1)

        def steps(eng, own):
            seen = {}

            def step(ins, name=None, value=None):
                name = name or own
                seen[name] = value or seen.get(name, 0) + 1
                ins.then_inc(sem(name), 1)
                eng.wait_ge(sem(name), seen[name])
            return step

        V_LB, V_OUT, V_QN, V_KN, V_INV = 0, 16, 18, 22, 24
        V_C, V_POOL, V_N1, V_N2, V_BADA = 25, 33, 37, 45, 53
        N_B2 = 5
        N_CONST = 15

        block = ctx.enter_context(nc.Block())

        @block.sync
        def _(sp):
            def load(dst, src, name="consts_load"):
                sp.dma_start(dst, src).then_inc(sem(name), 16)

            sp.wait_ge(sem("vec_zeroed"), 1)
            load(vec_rows[V_LB:V_LB + 16, :], d["hgrn_lb_logits"].rearrange("l (h p) -> (l h) p", p=P))
            load(vec_rows[V_OUT:V_OUT + 2, :], d["hgrn_out_norm"])
            load(vec_rows[V_QN:V_QN + 4, :], d["mla_q_norm"].rearrange("l (h p) -> (l h) p", p=P))
            load(vec_rows[V_KN:V_KN + 2, :], d["mla_kv_norm"])
            load(vec_rows[V_INV:V_INV + 1, :], d["c_inv_freq"])
            load(vec_rows[V_C:V_C + 8, :], d["c_2"].rearrange("l (h p) -> (l h) p", p=P))
            load(vec_rows[V_POOL:V_POOL + 4, :], d["pool_scale_2"].rearrange("l (h p) -> (l h) p", p=P))
            load(vec_rows[V_N1:V_N1 + 8, :], d["norm1_g_2"].rearrange("l (h p) -> (l h) p", p=P))
            load(vec_rows[V_N2:V_N2 + 8, :], d["norm2_g_2"].rearrange("l (h p) -> (l h) p", p=P))
            load(vec_rows[V_BADA:V_BADA + 48, :], d["b_ada_2"].rearrange("l (h p) -> (l h) p", p=P))
            load(eye[:, :], d["c_eye"])
            load(rot[:, :], d["c_rot"])
            load(flat_b[:, 800:1696].bitcast(i32), d["c_level"])
            load(causal[:, :, :], d["c_causal"].rearrange("(a p) s -> p a s", p=P))
            load(flat_b[:, 0:T].bitcast(i32), d["positions"].to_broadcast([P, T]))
            load(big[:, 0:2, :], d["mem"].rearrange("o (a p) n -> p (o a) n", p=P), "mem_load")
            load(x[:, :, :], d["x"].rearrange("o (a p) n -> p (o a) n", p=P), "x_load")

            def weights(n):
                if n >= RING:
                    sp.wait_ge(sem("unit_done"), n - RING + 1)
                l, name = STREAM[n]
                slot = n % RING
                arrived = f"ring_load{slot}"
                if name == "UP":
                    w_uq, w_uk, w_uv = up_weights(slot)
                    load(w_uq, d["w_mla_uq"][l].rearrange("(c p) n -> p c n", p=P), arrived)
                    load(w_uk, d["w_mla_uk"][l], arrived)
                    load(w_uv, d["w_mla_uv"][l], arrived)
                    return
                if name[0] == "O":
                    j = int(name[1])
                    src = d["w_out"][l] if l < DEPTH else d["w_out_2"][0]
                    load(ring[:, slot, :].rearrange("p (c n) -> p c n", c=4),
                         src[j * 512:(j + 1) * 512, :].rearrange("(c p) n -> p c n", p=P), arrived)
                    return
                if name == "MK":
                    src = d["w_mem_k"][l]
                elif name == "MV":
                    src = d["w_mem_v"][l]
                elif name[:2] == "AD":
                    j = int(name[2:])
                    src = d["w_ada_2"][0, :, j * COLS:(j + 1) * COLS]
                elif l < DEPTH:
                    c0 = dict(IN_UNITS)[name]
                    src = d["w_in"][l, :, c0:c0 + (416 if name == "C" else COLS)]
                elif name[0] == "B":
                    j = "QKVU".index(name[1])
                    src = d["w_in_2"][0, :, j * COLS:(j + 1) * COLS]
                else:
                    j = int(name[1])
                    src = d["peer_wq_2"][0, :, j * COLS:(j + 1) * COLS]
                w = src.shape[1]
                load(ring[:, slot, :].rearrange("p (c n) -> p c n", c=DC)[:, :, 0:w],
                     src.rearrange("(c p) n -> p c n", p=P), arrived)

            for l in range(DEPTH + 1):
                units = [name for k, name in STREAM if k == l]
                for name in units:
                    if l < DEPTH and name == OUT_UNITS[l][-1]:
                        bank_filled(sp, (l, ("L", 1, 7, 1)))
                        load(ln_gb[:, 0:D_MODEL], d["ln_g"][l:l + 1, :].to_broadcast([P, D_MODEL]), "gb_load")
                        load(ln_gb[:, D_MODEL:], d["ln_b"][l:l + 1, :].to_broadcast([P, D_MODEL]), "gb_load")
                    weights(UNIT[l, name])
                    if name == "BV":
                        after(sp, "x_next", DEPTH - 1, 1)
                        load(count[:, :, :], d["c_count"].rearrange("(a p) s -> p a s", p=P), "table_load")
                        load(dist[:, :, :], d["c_dist"].rearrange("(a p) s -> p a s", p=P), "table_load")
                        load(final_g, d["final_g_2"].rearrange("(o n) -> o n", o=1).to_broadcast([P, D_MODEL]), "b2_load")
                        load(inv_count, d["c_inv_count"].to_broadcast([P, 4 * T]), "b2_load")
                        load(w_pool, d["pool_w_2"].rearrange("o g c e -> c (o g) e"), "b2_load")
                        load(sub_rows.rearrange("p (a k) -> p a k", a=2),
                             d["peer_subkeys_2"].rearrange("o a n k -> n (o a) k"), "b2_load")
                        load(iota, d["c_iota"].to_broadcast([P, 16]), "b2_load")
            sp.wait_ge(sem("result"), TT)
            sp.dma_start(out.rearrange("(a p) n -> p a n", p=P), x[:, :, :]).then_inc(sem("out_store"), 16)
            sp.wait_ge(sem("out_store"), 16)

        @block.gpsimd
        def _(pool):
            g = nc.gpsimd
            do = steps(pool, "pool_step")
            pool.wait_ge(sem("silu_c"), 1)
            for l in range(DEPTH + 1):
                for task in TASKS[l]:
                    if task[:2] == "AD":
                        j, n = int(task[2:]), UNIT[l, task]
                        pool.wait_ge(sem(f"ring_load{n % RING}"), ring_loads(n))
                        if j >= 2:
                            key = (l, (f"AD{j - 2}",)) if (l, (f"AD{j - 2}",)) in BANK else (l - 1, (f"AD{j - 2}",))
                            bank_filled(pool, key)
                        w = ring[:, n % RING, :].rearrange("p (c n) -> p c n", c=DC)
                        part = mod_part[:, j % 2, :]
                        do(g.tensor_tensor(w, w, silu_c.unsqueeze(2).to_broadcast([P, DC, COLS]), ALU.mult))
                        do(g.tensor_tensor(w[:, 0:4, :], w[:, 0:4, :], w[:, 4:8, :], ALU.add))
                        do(g.tensor_tensor(w[:, 0:2, :], w[:, 0:2, :], w[:, 2:4, :], ALU.add))
                        do(g.tensor_tensor(part, w[:, 0, :], w[:, 1, :], ALU.add), "mod_partial")
            pool.wait_ge(sem("uT_ready"), 1)
            pool.wait_ge(sem("b2_load"), 16 * N_B2)
            do(g.tensor_copy(pool_sum, uT))
            for w in range(4):
                for k in range(w + 1):
                    n = 2 ** k
                    spare = mixed[:, w, :]
                    do(g.tensor_copy(spare, pool_sum[:, w, :]))
                    do(g.tensor_tensor(pool_sum[:, w, n:T], spare[:, n:T], spare[:, 0:T - n], ALU.add))
            do(g.tensor_tensor(mixed, pool_sum, inv_count.rearrange("p (a t) -> p a t", a=4), ALU.mult))
            do(g.tensor_tensor(mixed, mixed, uT, ALU.subtract), "pool_mixed")
            tables = [d["peer_u_2"].rearrange("o e n -> (o e) n"), d["peer_v_2"].rearrange("o e n -> (o e) n")]
            turns = 0
            for table in tables:
                for part in range(2 * TT):
                    if table is tables[0]:
                        pool.wait_ge(sem("experts"), part + 1)
                    t, first = part // 2, part % 2 * (PICKS // 2)
                    with pool.Fori(0, TURNS // 2) as turn:
                        for half in range(2):
                            pool.wait_ge(sem("slots_free"), turn * GSLOTS + (turns * GSLOTS + (half + 1) * GHALF))
                            pool.sem_inc(sem("gather_turn"), 1)
                            idx = turn_idx[:, half * GHALF:(half + 1) * GHALF]
                            src = expert[:, t, bass.ds(turn * GSLOTS + (first + half * GHALF), GHALF)]
                            g.tensor_copy(idx, src).then_inc(sem("idx_ready"), 1)
                            pool.wait_ge(sem("idx_ready"), turn * 2 + (2 * turns + half + 1))
                            pool.sem_inc(sem("gather_turn"), 1)
                            for k in range(GHALF):
                                slot = half * GHALF + k
                                pool.indirect_dma_start(
                                    gslot[slot], None, table,
                                    bass.IndirectOffsetOnAxis(ap=idx[:, k:k + 1], axis=0))\
                                    .then_inc(sem(f"row_load{slot}"), 16)
                    turns += TURNS // 2

        @block.tensor
        def _(pe):
            def last(ins, name="bank_filled"):
                ins.then_inc(sem(name), 1)

            def transposes(key, pairs):
                bank_empty(pe, key)
                for dst, src in pairs:
                    ins = nc.tensor.transpose(dst, src, eye[:, :])
                last(ins)

            def loaded(l, name):
                n = UNIT[l, name]
                pe.wait_ge(sem(f"ring_load{n % RING}"), ring_loads(n))
                return n % RING

            def channel_major(l, name, act, width=COLS):
                slot = loaded(l, name)
                w = ring[:, slot, :].rearrange("p (c n) -> p c n", c=DC)
                s, use = BIG[l, name]
                if use:
                    pe.wait_ge(sem(f"pj_free{s}"), use)
                for m in range(0, width, P):
                    n = min(P, width - m)
                    for c in range(DC):
                        ins = nc.tensor.matmul(pj[s][0:n, 2 * m:2 * m + T], w[:, c, m:m + n], act[:, c, :],
                                               start=(c == 0), stop=(c == DC - 1))
                last(ins, "unit_done")

            def token_major(l, name, act):
                slot = loaded(l, name)
                w = ring[:, slot, :].rearrange("p (c n) -> p c n", c=DC)
                s, use = BIG[l, name]
                if use:
                    pe.wait_ge(sem(f"pj_free{s}"), use)
                for t in range(TT):
                    for c in range(DC):
                        ins = nc.tensor.matmul(pj[s][:, t * COLS:(t + 1) * COLS], act[:, c, t * P:(t + 1) * P],
                                               w[:, c, :], start=(c == 0), stop=(c == DC - 1))
                last(ins, "unit_done")

            pe.wait_ge(sem("consts_load"), 16 * N_CONST)
            pe.wait_ge(sem("mem_load"), 16)
            pe.wait_ge(sem("ones_ready"), 1)
            mem = big[:, 0:2, :]
            for j in range(4):
                B = bank[BANK["M", j] % 4]
                transposes(("M", j), [(B[:, (cc * TT + a) * P:(cc * TT + a + 1) * P],
                                       mem[:, a, (2 * j + cc) * P:(2 * j + cc + 1) * P])
                                      for cc in range(2) for a in range(TT)])
            transposes("VEC", [(bank_of("VEC")[:, 0:P], vec_rows)])

            def output_product(l, name):
                j = int(name[1:])
                first, stop = name == OUT_UNITS[l][0], name == OUT_UNITS[l][-1]
                if first:
                    for s in range(2):
                        pe.wait_ge(sem(f"pj_free{s}"), BIG[l, "OUT"][s])
                slot = loaded(l, name)
                w = ring[:, slot, :].rearrange("p (c n) -> p c n", c=4)
                for t in range(TT):
                    for n in range(2):
                        for c in range(4):
                            ins = nc.tensor.matmul(
                                pj[t][:, n * 512:(n + 1) * 512], yT[:, 4 * j + c, t * P:(t + 1) * P],
                                w[:, c, n * 512:(n + 1) * 512],
                                start=(first and c == 0), stop=(stop and c == 3))
                    if t == 0 and stop:
                        last(ins, "out_tile")
                last(ins, "unit_done")

            def scores(l, i, q, k):
                key = (l, ("S", i))
                bank_empty(pe, key)
                B = bank_of(key)
                for t in range(TT):
                    ins = nc.tensor.matmul(B[:, t * T:(t + 1) * T], q[:, t * P:(t + 1) * P], k, start=True, stop=True)
                last(ins)

            def weights_transposed(l, i):
                key = (l, ("PT", i))
                after(pe, "p_ready", l, i)
                B = bank_of(key)
                transposes(key, [(B[:, s * T + t * P:s * T + (t + 1) * P], sm[:, i % 2, t, s * P:(s + 1) * P])
                                 for s in range(TT) for t in range(TT)])

            def values_summed(l, i, rows, v):
                key = (l, ("AO", i))
                bank_empty(pe, key)
                after(pe, "pt_ready", l, i)
                for s in range(TT):
                    ins = nc.tensor.matmul(bank_of(key)[rows, 0:T], v[s], pT[:, i % 2, s, :],
                                           start=(s == 0), stop=(s == TT - 1))
                last(ins)

            def transposed_x(l, task, src, ready):
                for j in range(4):
                    a, c0 = j // 2, 4 * (j % 2)
                    if j % 2 == 0:
                        ready(a)
                    B = bank_of((l, (task, j)))
                    transposes((l, (task, j)), [(B[:, c * P:(c + 1) * P], src[:, a, (c0 + c) * P:(c0 + c + 1) * P])
                                                for c in range(4)])
                after(pe, "xT_ready", l, 3 if task == "X" else 7)

            def attention(l, i):
                if i < N_ATT:
                    if i < MLA_HEADS:
                        after(pe, "qrope_ready", l, i // 2)
                        after(pe, "uk_ready", l, i // 2)
                        after(pe, "kr_spread", l)
                        scores(l, i, qM[:, i, :], kM[:, i, :])
                    else:
                        after(pe, "qE_ready", l)
                        after(pe, "kE_ready", l)
                        scores(l, i, qE[:, i - MLA_HEADS, :], kE[:, i - MLA_HEADS, :])
                if 2 <= i <= N_ATT + 1:
                    weights_transposed(l, i - 2)
                if i >= 3:
                    k = i - 3
                    if k < MLA_HEADS:
                        after(pe, "uv_ready", l, 1)
                        values_summed(l, k, slice(64 * (k % 2), 64 * (k % 2) + 64),
                                      [vM[:, s, k * 64:(k + 1) * 64] for s in range(TT)])
                    else:
                        after(pe, "vE_ready", l)
                        k -= MLA_HEADS
                        values_summed(l, i - 3, slice(0, P), [vE[:, s, k * P:(k + 1) * P] for s in range(TT)])

            def level(l, g, m):
                if m == 0:
                    after(pe, "k_ready", l, g)
                    after(pe, "q_ready", l, g)
                else:
                    after(pe, "lvl_ready", l, 8 * g + m - 1)
                W = big[:, m % 3, :].rearrange("p (h t) -> p h t", t=T)
                for j in range(2 if m < 8 else 1):
                    key = (l, ("L", g, m, j))
                    bank_empty(pe, key)
                    B = bank_of(key)
                    for n in range(4):
                        if m == 8:
                            k, q = W[:, n, 0:P], W[:, n, P:T]
                        else:
                            hd, t = (4 * j + n) // TT, (4 * j + n) % TT
                            q = W[:, hd, t * P:(t + 1) * P]
                            k = q
                            if m == 0:
                                q = qT[:, GH * g + hd, t * P:(t + 1) * P]
                                k = kT[:, GH * g + hd, t * P:(t + 1) * P]
                        ins = nc.tensor.matmul(B[:, n * P:(n + 1) * P], k, q, start=True, stop=True)
                    last(ins)

            def readout(l, g, i):
                if i < 2:
                    key = (l, ("HO", 2 * g + i))
                    bank_empty(pe, key)
                    after(pe, "blended", l, 9 * g + 8)
                    after(pe, "hv_ready", l, g)
                    B = bank_of(key)
                    for k in range(2):
                        hd = 2 * i + k
                        c = (GH * g + hd) * P
                        v = [hv[:, t, c:c + P] for t in range(TT)]
                        o = B[:, k * T:(k + 1) * T]
                        nc.tensor.matmul(o[:, 0:P], v[0], pair[:, hd * TT, :], start=True, stop=True)
                        nc.tensor.matmul(o[:, P:T], v[0], far_pair[:, hd, :], start=True, stop=False)
                        ins = nc.tensor.matmul(o[:, P:T], v[1], pair[:, hd * TT + 1, :], start=False, stop=True)
                    last(ins)
                if i >= 1:
                    n = 2 * g + i - 1
                    key = (l, ("HN", n))
                    bank_empty(pe, key)
                    after(pe, "ho_sq", l, n)
                    last(nc.tensor.matmul(bank_of(key)[:, :], ones_mean[:, :],
                                          sq[:, 0:2, :].rearrange("p a t -> p (a t)"), start=True, stop=True))

            def modulation(l, task):
                j = int(task[2:])
                key = (l, (task,))
                bank_empty(pe, key)
                pe.wait_ge(sem("mod_partial"), j + 1)
                for m in range(COLS // P):
                    ins = nc.tensor.matmul(bank_of(key)[:, m:m + 1], mod_part[:, j % 2, m * P:(m + 1) * P],
                                           ones_mean[:, 0:1], start=True, stop=True)
                last(ins)
                pe.wait_ge(sem("bank_filled"), BANK[key] + 1)
                pe.sem_inc(sem("unit_done"), 1)

            for l in range(DEPTH):
                for task in TASKS[l]:
                    if task == "X":
                        if l:
                            transposed_x(l, "X", x, lambda a: after(pe, "x_next", l - 1, a))
                        else:
                            transposed_x(l, "X", x, lambda a: pe.wait_ge(sem("x_load"), 16))
                    elif task in ("G0", "G1", "GM", "GE", "F0", "F1", "Q0", "Q1", "C", "MQ"):
                        channel_major(l, task, xT, 416 if task == "C" else COLS)
                    elif task in ("I0", "I1"):
                        token_major(l, task, xT)
                    elif task == "MK":
                        pe.wait_ge(sem("memT_ready"), 4)
                        channel_major(l, task, memT)
                    elif task == "MV":
                        token_major(l, task, memT)
                    elif task[0] == "L" and task != "LN":
                        level(l, int(task[1]), int(task[2]))
                    elif task[:2] == "AD":
                        modulation(l, task)
                    elif task[0] == "A":
                        attention(l, int(task[1:]))
                    elif task[0] == "H":
                        readout(l, int(task[1]), int(task[2]))
                    elif task == "N":
                        key = (l, ("N",))
                        bank_empty(pe, key)
                        after(pe, "c_sq", l)
                        B = bank_of(key)
                        for c in range(2):
                            nc.tensor.matmul(B[:, 0:T], ones_mean[:, :], sq[:, c, :], start=(c == 0), stop=(c == 1))
                        last(nc.tensor.matmul(B[:, T:2 * T], ones_mean[:, :], sq[:, 2, :], start=True, stop=True))
                        key = (l, ("KR",))
                        bank_empty(pe, key)
                        last(nc.tensor.matmul(bank_of(key)[0:32, 0:T], rot[0:32, :], cT[0:32, 3, :],
                                              start=True, stop=True))
                    elif task == "UP":
                        w_uq, w_uk, w_uv = up_weights(loaded(l, "UP"))
                        after(pe, "c_normed", l)
                        for j in range(4):
                            key = (l, ("UQ", j))
                            bank_empty(pe, key)
                            B = bank_of(key)
                            for k in range(2):
                                h = 2 * j + k
                                for c in range(2):
                                    ins = nc.tensor.matmul(B[0:96, k * T:(k + 1) * T], w_uq[:, c, h * 96:(h + 1) * 96],
                                                           cT[:, c, :], start=(c == 0), stop=(c == 1))
                            last(ins)
                        for j in range(4):
                            key = (l, ("UK", j))
                            bank_empty(pe, key)
                            for k in range(2):
                                h = 2 * j + k
                                ins = nc.tensor.matmul(bank_of(key)[0:64, k * T:(k + 1) * T],
                                                       w_uk[:, h * 64:(h + 1) * 64], cT[:, 2, :], start=True, stop=True)
                            last(ins)
                        for t in range(TT):
                            key = (l, ("UV", t))
                            bank_empty(pe, key)
                            last(nc.tensor.matmul(bank_of(key)[:, :], cT[:, 2, t * P:(t + 1) * P], w_uv,
                                                  start=True, stop=True))
                        pe.wait_ge(sem("bank_filled"), BANK[key] + 1)
                        pe.sem_inc(sem("unit_done"), 1)
                        for j in range(4):
                            key = (l, ("QR", j))
                            bank_empty(pe, key)
                            after(pe, "uq_ready", l, j)
                            last(nc.tensor.matmul(bank_of(key)[64:96, :], rot[64:96, :],
                                                  qM[64:96, 2 * j:2 * j + 2, :].rearrange("p a t -> p (a t)"),
                                                  start=True, stop=True))
                    elif output_unit(task):
                        signal, i = (("y_hg", 1), ("y_hg", 3), ("y_att", MLA_HEADS - 1), ("y_att", N_ATT - 1))[int(task[1])]
                        after(pe, signal, l, i)
                        output_product(l, task)

            l = B2
            for task in TASKS[l]:
                if task in ("X", "X2"):
                    k = 0 if task == "X" else TT
                    transposed_x(l, task, normed, lambda a: pe.wait_ge(sem("row_normed"), k + a + 1))
                elif task == "MB":
                    pe.wait_ge(sem("mod_ready"), 1)
                    for v, c in enumerate((2, 4, 3, 5)):
                        for k in range(2):
                            key = (l, ("MB", v, k))
                            bank_empty(pe, key)
                            for j in range(4):
                                n = 4 * k + j
                                ins = nc.tensor.matmul(bank_of(key)[:, j * P:(j + 1) * P],
                                                       modc[:, c, n:n + 1].to_broadcast([P, P]), eye[:, :],
                                                       start=True, stop=True)
                            last(ins)
                elif task in ("BQ", "BK", "BU", "K0", "K1", "K2", "K3"):
                    channel_major(l, task, xT)
                elif task == "BV":
                    token_major(l, task, xT)
                elif task == "PM":
                    pe.wait_ge(sem("b2_load"), 16 * N_B2)
                    pe.wait_ge(sem("pool_mixed"), 1)
                    for j in range(2):
                        key = (l, ("PL", j))
                        bank_empty(pe, key)
                        for g in range(2):
                            ins = nc.tensor.matmul(bank_of(key)[:, g * T:(g + 1) * T], w_pool[:, 2 * j + g, :],
                                                   mixed[:, 2 * j + g, :], start=True, stop=True)
                        last(ins)
                elif task == "SK":
                    pe.wait_ge(sem("b2_load"), 16 * N_B2)
                    transposes((l, ("SK",)), [(bank_of((l, ("SK",)))[:, k * P:(k + 1) * P],
                                               sub_rows[:, k * P:(k + 1) * P]) for k in range(2)])
                elif task[0] == "B" and task[1:].isdigit():
                    i = int(task[1:])
                    if i in (0, 3):
                        pe.wait_ge(sem("qkv2_ready"), 3 if i == 3 else 2)
                    if i < HEADS2:
                        r = slice(64 * (i % 2), 64 * (i % 2) + 64)
                        scores(l, i, q2[r, i // 2, :], k2[r, i // 2, :])
                    if 2 <= i <= HEADS2 + 1:
                        weights_transposed(l, i - 2)
                    if i >= 3:
                        k = i - 3
                        values_summed(l, k, slice(64 * (k % 2), 64 * (k % 2) + 64),
                                      [v2[:, s, k * 64:(k + 1) * 64] for s in range(TT)])
                elif task[:2] == "AD":
                    modulation(l, task)
                elif output_unit(task):
                    if task == "O1":
                        pe.wait_ge(sem("pool_out"), 2)
                    else:
                        pe.wait_ge(sem("y2_ready"), HEADS2)
                    output_product(l, task)
                elif task[0] == "E":
                    i = int(task[1:])
                    key = (l, ("E", i))
                    bank_empty(pe, key)
                    pe.wait_ge(sem("skT_ready"), 1)
                    pe.wait_ge(sem("peer_q"), i // 2 + 1)
                    for t in range(TT):
                        for k in range(2):
                            g = 2 * t + k
                            ins = nc.tensor.matmul(bank_of(key)[:, g * P:(g + 1) * P],
                                                   yT[:, 2 * i + k, t * P:(t + 1) * P], skT[:, k, :],
                                                   start=True, stop=True)
                    last(ins)

        @block.scalar
        def _(act):
            a = nc.scalar
            do = steps(act, "act_step")

            def log_exp_tables():
                a.preload_act_table_set("natural_log_exp_and_others")

            for j in range(4):
                act.wait_ge(sem("bank_filled"), BANK["M", j] + 1)
                do(a.copy(memT[:, 2 * j:2 * j + 2, :].rearrange("p a t -> p (a t)"), bank_of(("M", j))[:, :]),
                   *bank_free(("M", j)))
                act.sem_inc(sem("memT_ready"), 1)
            act.wait_ge(sem("angles"), 1)
            do(a.activation(rope[:, 1, :], flat_b[:, 0:T], ACT.Sin))
            do(a.activation(rope[:, 0, :], flat_b[:, T:2 * T], ACT.Sin), "rope_ready")
            act.wait_ge(sem("lb_centred"), 1)
            do(a.activation(lbt[:, 1:3, :], lbt[:, 1:3, :], ACT.Exp), "lb_exp")

            act.wait_ge(sem("vec_ready"), 1)
            do(a.activation(silu_c, vec[:, V_C:V_C + DC], ACT.Silu), "silu_c")
            log_exp_tables()

            def freed(l, name):
                s, use = BIG[l, name]
                return f"pj_free{s}", use + 1

            def transposed_x(l, task, scale=None, shift=None):
                for j in range(4):
                    key = (l, (task, j))
                    bank_filled(act, key)
                    t, c0 = j // 2, 4 * (j % 2)
                    dst = xT[:, c0:c0 + 4, t * P:(t + 1) * P]
                    src = bank_of(key)[:, :].rearrange("p (c n) -> p c n", c=4)
                    if scale is None:
                        do(a.copy(dst, src), *bank_free(key))
                    else:
                        for c in range(4):
                            do(a.activation(dst[:, c, :], src[:, c, :], ACT.Identity, scale=scale[:, c0 + c:c0 + c + 1],
                                            bias=shift[:, c0 + c:c0 + c + 1]), *(bank_free(key) if c == 3 else ()))
                    act.sem_inc(sem("xT_ready"), 1)

            def exps(l, i):
                after(act, "sm_ready", l, i)
                st = stat[:, 4 * (i % 2):4 * (i % 2) + 4]
                for t in range(TT):
                    do(a.activation(sm[:, i % 2, t, :], sm[:, i % 2, t, :], ACT.Exp, bias=st[:, t:t + 1],
                                    accum_out=st[:, 2 + t:3 + t]), "exp_done" if t == TT - 1 else None)

            def weights_transposed(l, i):
                key = (l, ("PT", i))
                bank_filled(act, key)
                do(a.copy(pT[:, i % 2, :, :].rearrange("p a t -> p (a t)"), bank_of(key)[:, :]), *bank_free(key))
                act.sem_inc(sem("pt_ready"), 1)

            def row_norm(src, t, e, scale, done):
                do(a.activation(sm[:, :, :, :].rearrange("p a b t -> p (a b t)"), src, ACT.Square,
                                accum_out=stat[:, 10 + t:11 + t]))
                do(a.activation(stat[:, 12 + t:13 + t], stat[:, 10 + t:11 + t], ACT.Ln, scale=scale, bias=e))
                do(a.activation(stat[:, 12 + t:13 + t], stat[:, 12 + t:13 + t], ACT.Exp, scale=-0.5), done)

            for l in range(DEPTH):
                for task in TASKS[l]:
                    if (l, task) in BIG and task != "OUT":
                        s, _ = BIG[l, task]
                    if task == "X":
                        if l:
                            unit_done(act, l - 1, "G1")
                        transposed_x(l, "X")
                    elif task in ("G0", "G1", "GM", "GE"):
                        g = ("G0", "G1", "GM", "GE").index(task)
                        if l and task == "GM":
                            unit_done(act, l - 1, OUT_UNITS[l - 1][-1])
                        unit_done(act, l, task)
                        do(a.activation(yT[:, 4 * g:4 * g + 4, :].rearrange("p a t -> p (a t)"), pj[s][:, :], ACT.Silu),
                           *freed(l, task))
                        act.sem_inc(sem("gates"), 1)
                        log_exp_tables()
                    elif task[:2] == "FP":
                        g = int(task[2])
                        z = flat(b)[:, g * GH * T:(g + 1) * GH * T]
                        after(act, "fz", l, g)
                        if g:
                            bank_filled(act, (l, ("L", 0, 8, 0)))
                        do(a.activation(flat(kT)[:, g * GH * T:(g + 1) * GH * T], z, ACT.Sigmoid, scale=-1.0))
                        log_exp_tables()
                        do(a.activation(big[:, 0, :], z, ACT.Exp, scale=-1.0), "f_exp")
                        do(a.activation(big[:, 2, :], big[:, 0, :], ACT.Ln, bias=1.0))
                        after(act, "f_pos", l, g)
                        do(a.activation(big[:, 1, :], big[:, 1, :], ACT.Ln, bias=1.0), "f_ln")
                    elif task in ("Q0", "Q1"):
                        q = int(task[1])
                        unit_done(act, l, task)
                        do(a.copy(qT[:, 4 * q:4 * q + 4, :].rearrange("p a t -> p (a t)"), pj[s][:, :]), *freed(l, task))
                        act.sem_inc(sem("q_ready"), 1)
                    elif task == "C":
                        unit_done(act, l, task)
                        do(a.copy(cT[0:32, 3, :], pj[s][0:32, 3 * T:4 * T]))
                        do(a.copy(cT[:, 0:3, :].rearrange("p a t -> p (a t)"), pj[s][:, 0:3 * T]), *freed(l, task))
                        act.sem_inc(sem("c_ready"), 1)
                        if l:
                            bank_filled(act, (l - 1, ("HN", 3)))
                        do(a.activation(sq[:, :, :], cT[:, 0:3, :], ACT.Square), "c_sq")
                    elif task[:2] == "Da":
                        m = int(task[3])
                        after(act, "lvl_sub", l, 8 * int(task[2]) + m - 1)
                        do(a.activation(big[:, m % 3, :], big[:, m % 3, :], ACT.Exp), "lvl_exp")
                    elif task == "N":
                        key = (l, ("N",))
                        bank_filled(act, key)
                        B = bank_of(key)
                        do(a.activation(rstd[:, 0, :], B[:, 0:T], ACT.Ln, scale=P / Q_RANK, bias=eps[:, 0:1]))
                        do(a.activation(rstd[:, 1, :], B[:, T:2 * T], ACT.Ln, bias=eps[:, 0:1]))
                        do(a.activation(rstd[:, :, :], rstd[:, :, :], ACT.Exp, scale=-0.5), "c_rstd")
                        after(act, "kr_ready", l)
                        do(a.copy(kM[64:96, :, :], cT[0:32, 3:4, :].to_broadcast([32, MLA_HEADS, T])), "kr_spread")
                    elif task == "UP":
                        for j in range(4):
                            key = (l, ("UQ", j))
                            bank_filled(act, key)
                            do(a.copy(qM[:, 2 * j:2 * j + 2, :].rearrange("p a t -> p (a t)"), bank_of(key)[0:96, :]),
                               *bank_free(key))
                            act.sem_inc(sem("uq_ready"), 1)
                        for j in range(4):
                            key = (l, ("UK", j))
                            bank_filled(act, key)
                            do(a.copy(kM[0:64, 2 * j:2 * j + 2, :].rearrange("p a t -> p (a t)"), bank_of(key)[0:64, :]),
                               *bank_free(key))
                            act.sem_inc(sem("uk_ready"), 1)
                        for t in range(TT):
                            key = (l, ("UV", t))
                            bank_filled(act, key)
                            do(a.copy(vM[:, t, :], bank_of(key)[:, :]), *bank_free(key))
                            act.sem_inc(sem("uv_ready"), 1)
                    elif task in ("I0", "I1"):
                        q = int(task[1])
                        unit_done(act, l, task)
                        do(a.copy(hv[:, :, q * COLS:(q + 1) * COLS], pj[s][:, :].rearrange("p (a n) -> p a n", a=TT)),
                           *freed(l, task))
                        act.sem_inc(sem("hv_ready"), 1)
                    elif task in ("MQ", "MK", "MV"):
                        unit_done(act, l, task)
                        dst, done = {"MQ": (qE, "qE_ready"), "MK": (kE, "kE_ready"), "MV": (vE, "vE_ready")}[task]
                        do(a.copy(dst[:, :, :].rearrange("p a t -> p (a t)"), pj[s][:, :]), *freed(l, task))
                        act.sem_inc(sem(done), 1)
                    elif task[0] == "A" and task[1:].isdigit():
                        i = int(task[1:])
                        if i < N_ATT:
                            exps(l, i)
                        if 2 <= i <= N_ATT + 1:
                            weights_transposed(l, i - 2)
                    elif task[0] == "H":
                        g, i = int(task[1]), int(task[2])
                        if i >= 1:
                            n = 2 * g + i - 1
                            key = (l, ("HN", n))
                            bank_filled(act, key)
                            if n:
                                after(act, "y_hg", l, n - 1)
                            do(a.activation(rstd[:, :, :].rearrange("p a t -> p (a t)"), bank_of(key)[:, :], ACT.Ln,
                                            bias=eps[:, 0:1]))
                            do(a.activation(rstd[:, :, :], rstd[:, :, :], ACT.Exp, scale=-0.5), "ho_rstd")
                        if i < 2:
                            key = (l, ("HO", 2 * g + i))
                            bank_filled(act, key)
                            do(a.activation(sq[:, 0:2, :].rearrange("p a t -> p (a t)"), bank_of(key)[:, :], ACT.Square),
                               "ho_sq")
                    elif task == "LN":
                        for t in range(TT):
                            after(act, "ln_in", l, t)
                            row_norm(x[:, t, :], t, eps[:, 1:2], 1.0 / D_MODEL, "ln_rstd")

            l = B2
            for task in TASKS[l]:
                if task in ("R1", "R2"):
                    for t in range(TT):
                        if task == "R1":
                            after(act, "x_next", DEPTH - 1, t)
                        else:
                            act.wait_ge(sem("x_mid"), t + 1)
                        row_norm(x[:, t, :], t, eps[:, 0:1], 1.0 / D_MODEL, "row_rstd")
                elif task == "X":
                    transposed_x(l, task, modc[:, 1, :], modc[:, 0, :])
                elif task == "X2":
                    transposed_x(l, task, modc[:, 4, :], modc[:, 3, :])
                elif task == "MB":
                    for v, row in enumerate((row_gate1, row_scale2, row_shift2, row_gate2)):
                        for k in range(2):
                            key = (l, ("MB", v, k))
                            bank_filled(act, key)
                            do(a.copy(row[:, k * COLS:(k + 1) * COLS], bank_of(key)[:, :]), *bank_free(key))
                    act.sem_inc(sem("rows_ready"), 1)
                elif task in ("BQ", "BK", "BV", "BU"):
                    s, _ = BIG[l, task]
                    unit_done(act, l, task)
                    dst = {"BQ": q2, "BK": k2, "BV": v2[:, :, :], "BU": uT}[task]
                    dst = dst.rearrange("p a t -> p (a t)")
                    if task == "BQ":
                        do(a.mul(dst, pj[s][:, :], HD2 ** -0.5), *freed(l, task))
                    else:
                        do(a.copy(dst, pj[s][:, :]), *freed(l, task))
                    act.sem_inc(sem("uT_ready" if task == "BU" else "qkv2_ready"), 1)
                elif task == "PM":
                    for j in range(2):
                        key = (l, ("PL", j))
                        bank_filled(act, key)
                        for g in range(2):
                            c = 2 * j + g
                            do(a.activation(yT[:, 4 + c, :], bank_of(key)[:, g * T:(g + 1) * T], ACT.Copy,
                                            scale=vec[:, V_POOL + c:V_POOL + c + 1]),
                               *(bank_free(key) if g else ()))
                        act.sem_inc(sem("pool_out"), 1)
                elif task == "SK":
                    key = (l, ("SK",))
                    bank_filled(act, key)
                    do(a.copy(flat(sq)[:, 512:768], bank_of(key)[:, 0:2 * P]), *bank_free(key))
                    act.sem_inc(sem("skT_ready"), 1)
                elif task[0] == "B" and task[1:].isdigit():
                    i = int(task[1:])
                    if i < HEADS2:
                        exps(l, i)
                    if 2 <= i <= HEADS2 + 1:
                        weights_transposed(l, i - 2)
                    if i >= 3:
                        k = i - 3
                        key = (l, ("AO", k))
                        bank_filled(act, key)
                        r = slice(64 * (k % 2), 64 * (k % 2) + 64)
                        do(a.copy(yT[r, k // 2, :], bank_of(key)[r, 0:T]), *bank_free(key))
                        act.sem_inc(sem("y2_ready"), 1)
                elif task[0] == "K":
                    j = int(task[1:])
                    s, _ = BIG[l, task]
                    unit_done(act, l, task)
                    do(a.copy(yT[:, 4 * j:4 * j + 4, :].rearrange("p a t -> p (a t)"), pj[s][:, :]), *freed(l, task))
                    act.sem_inc(sem("peer_q"), 1)
                elif task[0] == "E":
                    i = int(task[1:])
                    key = (l, ("E", i))
                    bank_filled(act, key)
                    if i >= 2:
                        act.wait_ge(sem("sub_best"), i - 1)
                    do(a.copy(sm[:, i % 2, 0, :], bank_of(key)[:, 0:T]))
                    act.sem_inc(sem("sub_scores"), 1)
                    do(a.copy(later_scores[:, i, :], bank_of(key)[:, T:2 * T]), *bank_free(key))
            for t in range(TT):
                act.wait_ge(sem("top_centred"), t + 1)
                do(a.activation(top_val[:, t], top_val[:, t], ACT.Exp), "top_exp")
            for t in range(TT):
                act.wait_ge(sem("dots_ready"), t + 1)
                do(a.activation(dots[:, t, :], dots[:, t, :], ACT.Gelu), "gelu_done")
            for t in range(TT):
                act.wait_ge(sem("x_last"), t + 1)
                row_norm(x[:, t, :], t, eps[:, 0:1], 1.0 / D_MODEL, "row_rstd")

        @block.vector
        def _(dve):
            v = nc.vector
            do = steps(dve, "dve_step")
            do(v.memset(vec_rows, 0.0), "vec_zeroed")
            do(v.memset(ones_mean[:, :], 1.0 / P), "ones_ready")
            do(v.memset(eps[:, 0:1], RMS_EPS))
            do(v.memset(eps[:, 1:2], LN_EPS))
            dve.wait_ge(sem("bank_filled"), BANK["VEC"] + 1)
            do(v.tensor_copy(vec[:, :], bank_of("VEC")[:, 0:104]), *bank_free("VEC"))
            dve.sem_inc(sem("vec_ready"), 1)
            dve.wait_ge(sem("consts_load"), 16 * N_CONST)
            ang, turns = flat_b[:, T:2 * T], flat_b[:, 2 * T:3 * T]
            do(v.tensor_copy(ang, flat_b[:, 0:T].bitcast(i32)))
            do(v.tensor_scalar(ang, ang, vec[:, V_INV:V_INV + 1], None, ALU.mult))
            MAGIC = 12582912.0
            do(v.tensor_scalar(turns, ang, 1.0 / (2 * np.pi), None, ALU.mult))
            do(v.tensor_scalar(turns, turns, MAGIC, None, ALU.add))
            do(v.tensor_scalar(turns, turns, MAGIC, None, ALU.subtract))
            C1 = 6.28125
            C2 = float(np.float32(int((2 * np.pi - C1) * 2 ** 20) / 2 ** 20))
            C3 = 2 * np.pi - C1 - C2
            for c in (C1, C2, C3):
                do(v.scalar_tensor_tensor(out=ang, in0=turns, scalar=-c, in1=ang, op0=ALU.mult, op1=ALU.add))
            PI = 3.1415925
            do(v.tensor_scalar(flat_b[:, 0:T], ang, PI, -PI, ALU.min, ALU.max))
            do(v.tensor_scalar(turns, ang, float(np.pi / 2), -2 * np.pi, ALU.is_gt, ALU.mult))
            do(v.tensor_tensor(ang, ang, turns, ALU.add))
            do(v.tensor_scalar(ang, ang, float(np.pi / 2), PI, ALU.add, ALU.min))
            do(v.tensor_scalar(ang, ang, -PI, None, ALU.max), "angles")
            do(v.tensor_copy(level_mask[:, :, :].rearrange("p m t -> p (m t)"), flat_b[:, 800:1696].bitcast(i32)))
            l0, l1 = vec[:, V_LB:V_LB + 8], vec[:, V_LB + 8:V_LB + 16]
            do(v.tensor_tensor(lbt[:, 0, :], l0, l1, ALU.max))
            do(v.tensor_tensor(lbt[:, 1, :], l0, lbt[:, 0, :], ALU.subtract))
            do(v.tensor_tensor(lbt[:, 2, :], l1, lbt[:, 0, :], ALU.subtract), "lb_centred")
            dve.wait_ge(sem("lb_exp"), 1)
            do(v.tensor_tensor(lbt[:, 3, :], lbt[:, 1, :], lbt[:, 2, :], ALU.add))
            do(v.reciprocal(lbt[:, 3, :], lbt[:, 3, :]))
            do(v.tensor_tensor(lbt[:, 1:3, :], lbt[:, 1:3, :], lbt[:, 3:4, :].to_broadcast([P, 2, 8]), ALU.mult))
            do(v.tensor_tensor(lower[:, 0, 0, :], lbt[:, 1, :], lbt[:, 1, :], ALU.subtract))
            do(v.tensor_tensor(lower[:, 1, 0, :], lbt[:, 1, :], lbt[:, 2, :], ALU.add))
            do(v.tensor_tensor(lower[:, 1, 0, :], lower[:, 1, 0, :], lbt[:, 1, :], ALU.subtract))
            do(v.tensor_scalar(lower[:, :, 1, :], lower[:, :, 0, :], -1.0, 1.0, ALU.mult, ALU.add))
            dve.wait_ge(sem("rope_ready"), 1)
            cos, sin = rope[:, 0, :], rope[:, 1, :]

            def refine(y, mean, e, tmp, scale=1.0, free=None):
                do(v.tensor_scalar(tmp, mean, scale, e, ALU.mult, ALU.add))
                do(v.tensor_tensor(tmp, tmp, y, ALU.mult))
                do(v.tensor_tensor(tmp, tmp, y, ALU.mult))
                do(v.tensor_scalar(tmp, tmp, -0.5, 1.5, ALU.mult, ALU.add))
                do(v.tensor_tensor(y, y, tmp, ALU.mult), *(free or ()))

            def heads(k):
                return big[:, k, :].rearrange("p (h t) -> p h t", t=T)

            def wide(x3):
                return x3.rearrange("p h t -> p (h t)")

            def level_views(g, m):
                s = slice(GH * g, GH * (g + 1))
                if m == 8:
                    W = heads(m % 3)
                    return (b[:, s, 0:P], b[:, s, P:T], W[:, :, 0:P], W[:, :, P:T], kT[:, s, 0:P], qT[:, s, P:T],
                            b[:, s, P - 1:P].to_broadcast([P, GH, P]))
                n = 2 ** (m - 1)

                def split(y):
                    z = y.rearrange("p (n two m) -> p n two m", two=2, m=n)
                    return z[:, :, 0, :], z[:, :, 1, :]
                b0, b1 = split(wide(b[:, s, :]))
                w0, w1 = split(big[:, m % 3, :])
                return (b0, b1, w0, w1, split(wide(kT[:, s, :]))[0], split(wide(qT[:, s, :]))[1],
                        b0[:, :, n - 1:n].to_broadcast([P, GH * T // (2 * n), n]))

            def modulation(l, task):
                j = int(task[2:])
                key = (l, (task,))
                bank_filled(dve, key)
                n = COLS // P
                do(v.scalar_tensor_tensor(out=modc[:, :, :].rearrange("p a c -> p (a c)")[:, j * n:(j + 1) * n],
                                          in0=bank_of(key)[:, 0:n], scalar=float(P),
                                          in1=vec[:, V_BADA + j * n:V_BADA + (j + 1) * n], op0=ALU.mult, op1=ALU.add),
                   *bank_free(key))

            def normalise(i):
                st = stat[:, 4 * (i % 2):4 * (i % 2) + 4]
                do(v.reciprocal(st[:, 2:4], st[:, 2:4]))
                P3 = sm[:, i % 2, :, :]
                do(v.tensor_tensor(P3, P3, st[:, 2:4].unsqueeze(2).to_broadcast([P, TT, T]), ALU.mult), "p_ready")

            for l in range(DEPTH):
                for task in TASKS[l]:
                    if task in ("F0", "F1"):
                        q = int(task[1])
                        s, use = BIG[l, task]
                        unit_done(dve, l, task)
                        do(v.tensor_scalar(wide(b[:, GH * q:GH * (q + 1), :]), pj[s][:, :], -44.0, None, ALU.max),
                           f"pj_free{s}", use + 1)
                        dve.sem_inc(sem("fz"), 1)
                    elif task[:2] == "AD":
                        modulation(l, task)
                    elif task[:2] == "FP":
                        g = int(task[2])
                        s = slice(GH * g, GH * (g + 1))
                        after(dve, "f_exp", l, g)
                        lb = lower[:, l, 0, s].unsqueeze(2).to_broadcast([P, GH, T])
                        omlb = lower[:, l, 1, s].unsqueeze(2).to_broadcast([P, GH, T])
                        do(v.tensor_tensor(heads(1), heads(0), lb, ALU.mult), "f_pos")
                        do(v.tensor_tensor(kT[:, s, :], kT[:, s, :], omlb, ALU.mult), "k_ready")
                        after(dve, "f_ln", l, g)
                        do(v.tensor_tensor(big[:, 2, :], big[:, 1, :], big[:, 2, :], ALU.subtract))
                        sums = wide(b[:, s, :])
                        for n in range(GH * TT):
                            seg = big[:, 2, n * P:(n + 1) * P]
                            do(v.tensor_tensor_scan(sums[:, n * P:(n + 1) * P], seg, seg, 0.0, ALU.add, ALU.bypass))
                    elif task[:2] == "Da":
                        g, m = int(task[2]), int(task[3])
                        if m >= 3:
                            bank_filled(dve, (l, ("L", g, m - 3, 1)))
                        b0, b1, w0, w1, _, _, mid = level_views(g, m)
                        do(v.tensor_tensor(w0, mid, b0, ALU.subtract))
                        if m == 8:
                            do(v.tensor_copy(w1, b1), "lvl_sub")
                        else:
                            do(v.tensor_tensor(w1, b1, mid, ALU.subtract), "lvl_sub")
                    elif task[:2] == "Db":
                        g, m = int(task[2]), int(task[3])
                        after(dve, "lvl_exp", l, 8 * g + m - 1)
                        _, _, w0, w1, k0, q1, _ = level_views(g, m)
                        if m == 1:
                            after(dve, "q_ready", l, g)
                        do(v.tensor_tensor(w0, w0, k0, ALU.mult))
                        do(v.tensor_tensor(w1, w1, q1, ALU.mult), "lvl_ready")
                    elif task[0] == "L" and task != "LN":
                        g, m = int(task[1]), int(task[2])
                        if g and m == 0:
                            bank_filled(dve, (l, ("HO", 1)))
                        for j in range(2 if m < 8 else 1):
                            key = (l, ("L", g, m, j))
                            bank_filled(dve, key)
                            B = bank_of(key)[:, :].rearrange("p (g t) -> p g t", t=P)
                            dst = pair[:, 4 * j:4 * j + 4, :]
                            if m == 0:
                                do(v.tensor_tensor(dst, B, eye[:, :].unsqueeze(1).to_broadcast([P, 4, P]), ALU.mult),
                                   *bank_free(key))
                            elif m < 8:
                                do(v.copy_predicated(dst, level_mask[:, m - 1:m, :].to_broadcast([P, 4, P]), B),
                                   *bank_free(key))
                            else:
                                do(v.tensor_copy(far_pair[:, :, :], B), *bank_free(key))
                        dve.sem_inc(sem("blended"), 1)
                    elif task == "N":
                        after(dve, "c_rstd", l)
                        B = bank_of((l, ("N",)))
                        refine(rstd[:, 0, :], B[:, 0:T], RMS_EPS, sm[:, 0, 0, :], P / Q_RANK)
                        refine(rstd[:, 1, :], B[:, T:2 * T], RMS_EPS, sm[:, 0, 0, :], 1.0, bank_free((l, ("N",))))
                        for c in range(3):
                            g = V_QN + 2 * l + c if c < 2 else V_KN + l
                            do(v.scalar_tensor_tensor(out=cT[:, c, :], in0=cT[:, c, :], scalar=vec[:, g:g + 1],
                                                      in1=rstd[:, c // 2, :], op0=ALU.mult, op1=ALU.mult),
                               "c_normed" if c == 2 else None)
                        key = (l, ("KR",))
                        bank_filled(dve, key)
                        tmp = sm[0:32, 0, 0, :]
                        do(v.tensor_tensor(tmp, bank_of(key)[0:32, 0:T], sin[0:32, :], ALU.mult), *bank_free(key))
                        do(v.tensor_tensor(cT[0:32, 3, :], cT[0:32, 3, :], cos[0:32, :], ALU.mult))
                        do(v.tensor_tensor(cT[0:32, 3, :], cT[0:32, 3, :], tmp, ALU.add), "kr_ready")
                    elif task == "UP":
                        for j in range(4):
                            key = (l, ("QR", j))
                            bank_filled(dve, key)
                            r = slice(64, 96)
                            q = qM[r, 2 * j:2 * j + 2, :]
                            tmp = sm[r, 0, :, :]
                            B = bank_of(key)[r, :].rearrange("p (a t) -> p a t", a=2)
                            do(v.tensor_tensor(tmp, B, sin[r, :].unsqueeze(1).to_broadcast([32, 2, T]), ALU.mult),
                               *bank_free(key))
                            do(v.tensor_tensor(q, q, cos[r, :].unsqueeze(1).to_broadcast([32, 2, T]), ALU.mult))
                            do(v.tensor_tensor(q, q, tmp, ALU.add), "qrope_ready")
                    elif task[0] == "A" and task[1:].isdigit():
                        i = int(task[1:])
                        st = stat[:, 4 * (i % 2):4 * (i % 2) + 4]
                        if i < N_ATT:
                            key = (l, ("S", i))
                            bank_filled(dve, key)
                            if i >= 2:
                                bank_filled(dve, (l, ("PT", i - 2)))
                            B = bank_of(key)[:, :].rearrange("p (a t) -> p a t", a=TT)
                            if i < MLA_HEADS:
                                do(v.scalar_tensor_tensor(out=sm[:, i % 2, :, :], in0=B, scalar=MLA_SCALE,
                                                          in1=causal[:, :, :], op0=ALU.mult, op1=ALU.add),
                                   *bank_free(key))
                            else:
                                do(v.tensor_scalar(sm[:, i % 2, :, :], B, MEM_SCALE, None, ALU.mult), *bank_free(key))
                            do(v.tensor_reduce(st[:, 0:2], sm[:, i % 2, :, :], X, ALU.max, negate=True), "sm_ready")
                        if 1 <= i <= N_ATT:
                            after(dve, "exp_done", l, i - 1)
                            normalise(i - 1)
                        if i >= 3:
                            h = i - 3
                            key = (l, ("AO", h))
                            bank_filled(dve, key)
                            if h < MLA_HEADS:
                                r = slice(64 * (h % 2), 64 * (h % 2) + 64)
                                g = yT[r, 8 + h // 2, :]
                            else:
                                r = slice(0, P)
                                g = yT[:, 12 + h - MLA_HEADS, :]
                            if h in (0, MLA_HEADS):
                                after(dve, "gates", l, GATE_OF["GM" if h == 0 else "GE"])
                            do(v.tensor_tensor(g, bank_of(key)[r, 0:T], g, ALU.mult), *bank_free(key))
                            dve.sem_inc(sem("y_att"), 1)
                    elif task[0] == "H":
                        g, i = int(task[1]), int(task[2])
                        if i < 2:
                            n = 2 * g + i
                            key = (l, ("HO", n))
                            after(dve, "ho_sq", l, n)
                            after(dve, "gates", l, GATE_OF[f"G{g}"])
                            y = wide(yT[:, 2 * n:2 * n + 2, :])
                            do(v.scalar_tensor_tensor(out=y, in0=bank_of(key)[:, :], scalar=vec[:, V_OUT + l:V_OUT + l + 1],
                                                      in1=y, op0=ALU.mult, op1=ALU.mult), *bank_free(key))
                        if i >= 1:
                            n = 2 * g + i - 1
                            after(dve, "ho_rstd", l, n)
                            key = (l, ("HN", n))
                            B = bank_of(key)[:, :]
                            refine(wide(rstd[:, :, :]), B, RMS_EPS, B, 1.0, bank_free(key))
                            y = wide(yT[:, 2 * n:2 * n + 2, :])
                            do(v.tensor_tensor(y, y, wide(rstd[:, :, :]), ALU.mult), "y_hg")
                    elif task == "LN":
                        for t in range(TT):
                            if t == 0:
                                after(dve, "out_tile", l)
                            else:
                                unit_done(dve, l, OUT_UNITS[l][-1])
                            do(v.scalar_tensor_tensor(out=x[:, t, :], in0=x[:, t, :], scalar=ALPHA, in1=pj[t][:, :],
                                                      op0=ALU.mult, op1=ALU.add, accum_out=stat[:, 8 + t:9 + t]),
                               f"pj_free{t}", BIG[l, "OUT"][t] + 1)
                            do(v.tensor_scalar(stat[:, 8 + t:9 + t], stat[:, 8 + t:9 + t], 1.0 / D_MODEL, None, ALU.mult))
                            do(v.tensor_scalar(x[:, t, :], x[:, t, :], stat[:, 8 + t:9 + t], None, ALU.subtract), "ln_in")
                            if t == 0:
                                dve.wait_ge(sem("gb_load"), (l + 1) * 32)
                            after(dve, "ln_rstd", l, t)
                            refine(stat[:, 12 + t:13 + t], stat[:, 10 + t:11 + t], LN_EPS, stat[:, 14:15], 1.0 / D_MODEL)
                            do(v.scalar_tensor_tensor(out=x[:, t, :], in0=x[:, t, :], scalar=stat[:, 12 + t:13 + t],
                                                      in1=ln_gb[:, 0:D_MODEL], op0=ALU.mult, op1=ALU.mult))
                            do(v.tensor_tensor(x[:, t, :], x[:, t, :], ln_gb[:, D_MODEL:], ALU.add), "x_next")


            l = B2

            def norm_rows(part):
                for t in range(TT):
                    dve.wait_ge(sem("row_rstd"), TT * part + t + 1)
                    refine(stat[:, 12 + t:13 + t], stat[:, 10 + t:11 + t], RMS_EPS, stat[:, 14:15], 1.0 / D_MODEL)
                    do(v.tensor_scalar(normed[:, t, :], x[:, t, :], stat[:, 12 + t:13 + t], None, ALU.mult), "row_normed")

            def scale_gain(c, gain, done=None):
                do(v.scalar_tensor_tensor(out=modc[:, c, :], in0=modc[:, c, :], scalar=1.0,
                                          in1=vec[:, gain:gain + DC], op0=ALU.add, op1=ALU.mult), done)

            def best16(values, left, out_val, out_id, done=None):
                do(v.max(out_val[:, 0:8], values))
                do(v.match_replace(left, out_val[:, 0:8], values, -3e38))
                do(v.max(out_val[:, 8:16], left))
                do(v.max_index(out_id[:, 0:8], out_val[:, 0:8], values))
                do(v.max_index(out_id[:, 8:16], out_val[:, 8:16], left))

            def best_keys(t, e, values):
                for k in range(2):
                    best16(values[:, k * P:(k + 1) * P], cand_left[:, 0:P], sub_val[:, t, e, k, :], sub_id[:, t, e, k, :])

            def best_sums(t, e):
                do(v.tensor_tensor(cand.rearrange("p (i j) -> p i j", i=TOPK),
                                   sub_val[:, t, e, 0, :].unsqueeze(2).to_broadcast([P, TOPK, TOPK]),
                                   sub_val[:, t, e, 1, :].unsqueeze(1).to_broadcast([P, TOPK, TOPK]), ALU.add))
                best16(cand, cand_left, top_val[:, t, e, :], top_pos[:, t, e * TOPK:(e + 1) * TOPK])

            def experts_of(t, half):
                n, H = PICKS // 2, PEER_HEADS // 2
                js, es = slice(half * n, (half + 1) * n), slice(half * H, (half + 1) * H)
                do(v.tensor_copy(sub_idf[:, t, es], sub_id[:, t, es]))
                oh = onehot[:, 0:n, :]
                for k, (op, arg, place, found) in enumerate(((ALU.logical_shift_right, 4, first_of, id_a),
                                                             (ALU.bitwise_and, 15, second_of, id_b))):
                    do(v.tensor_scalar(digit[:, 0:n], top_pos[:, t, js], arg, None, op))
                    do(v.tensor_copy(place[:, 0:n], digit[:, 0:n]))
                    do(v.tensor_tensor(oh, iota.unsqueeze(1).to_broadcast([P, n, TOPK]),
                                       place[:, 0:n].unsqueeze(2).to_broadcast([P, n, TOPK]), ALU.is_equal))
                    oh4 = oh.rearrange("p (e j) i -> p e j i", e=H)
                    do(v.tensor_tensor(oh4, oh4, sub_idf[:, t, es, k, :].unsqueeze(2)
                                       .to_broadcast([P, H, TOPK, TOPK]), ALU.mult))
                    do(v.tensor_reduce(found[:, 0:n], oh, X, ALU.add))
                do(v.scalar_tensor_tensor(out=id_a[:, 0:n], in0=id_a[:, 0:n], scalar=float(NKEYS), in1=id_b[:, 0:n],
                                          op0=ALU.mult, op1=ALU.add))
                do(v.tensor_copy(expert[:, t, js], id_a[:, 0:n]), "experts")

            def gates_of(t):
                do(v.tensor_copy(stat[:, 0:8].unsqueeze(2), top_val[:, t, :, 0:1]))
                do(v.tensor_tensor(top_val[:, t], top_val[:, t],
                                   stat[:, 0:8].unsqueeze(2).to_broadcast([P, PEER_HEADS, TOPK]), ALU.subtract),
                   "top_centred")
                dve.wait_ge(sem("top_exp"), t + 1)
                do(v.tensor_reduce(stat[:, 0:8], top_val[:, t], X, ALU.add))
                do(v.reciprocal(stat[:, 0:8], stat[:, 0:8]))
                do(v.tensor_tensor(gate[:, t, :].rearrange("p (e j) -> p e j", e=PEER_HEADS), top_val[:, t],
                                   stat[:, 0:8].unsqueeze(2).to_broadcast([P, PEER_HEADS, TOPK]), ALU.mult))

            for task in TASKS[l]:
                if task == "R1":
                    scale_gain(1, V_N1)
                    norm_rows(0)
                elif task[:2] == "AD":
                    modulation(l, task)
                elif task == "MB":
                    scale_gain(4, V_N2, "mod_ready")
                elif task[0] == "B" and task[1:].isdigit():
                    i = int(task[1:])
                    if i < HEADS2:
                        st = stat[:, 4 * (i % 2):4 * (i % 2) + 4]
                        key = (l, ("S", i))
                        bank_filled(dve, key)
                        if i >= 2:
                            bank_filled(dve, (l, ("PT", i - 2)))
                        if i == 0:
                            dve.wait_ge(sem("table_load"), 32)
                        do(v.scalar_tensor_tensor(out=sm[:, i % 2, :, :], in0=dist, scalar=-2.0 ** -(i + 1),
                                                  in1=bank_of(key)[:, :].rearrange("p (a t) -> p a t", a=TT),
                                                  op0=ALU.mult, op1=ALU.add), *bank_free(key))
                        do(v.tensor_reduce(st[:, 0:2], sm[:, i % 2, :, :], X, ALU.max, negate=True), "sm_ready")
                    if 1 <= i <= HEADS2:
                        st = stat[:, 4 * ((i - 1) % 2):4 * ((i - 1) % 2) + 4]
                        after(dve, "exp_done", l, i - 1)
                        for t in range(TT):
                            p = sm[:, (i - 1) % 2, t, :]
                            do(v.scalar_tensor_tensor(out=p, in0=p, scalar=1.0, in1=count[:, t, :], op0=ALU.mult,
                                                      op1=ALU.mult, accum_out=st[:, 2 + t:3 + t]))
                        normalise(i - 1)
                elif task == "OUT":
                    for t in range(TT):
                        if t == 0:
                            dve.wait_ge(sem("rows_ready"), 1)
                            after(dve, "out_tile", l)
                        else:
                            unit_done(dve, l, OUT_UNITS[l][-1])
                        tmp = product
                        do(v.tensor_tensor(tmp, pj[t][:, :], row_gate1, ALU.mult), f"pj_free{t}", BIG[l, "OUT"][t] + 1)
                        do(v.tensor_tensor(x[:, t, :], x[:, t, :], tmp, ALU.add), "x_mid")
                elif task == "R2":
                    norm_rows(1)
                elif task == "K0":
                    bank_filled(dve, (l, ("X2", 3)))
                    for t in range(TT):
                        do(v.tensor_tensor(normed[:, t, :], normed[:, t, :], row_scale2, ALU.mult))
                        do(v.tensor_tensor(normed[:, t, :], normed[:, t, :], row_shift2, ALU.add))
                elif task[0] == "E":
                    e = int(task[1:])
                    if e == PEER_HEADS // 2:
                        unit_done(dve, l, "K2")
                        dve.sem_inc(sem("slots_free"), GHALF)
                    if e == PEER_HEADS // 2 + 1:
                        unit_done(dve, l, "K3")
                        bank_filled(dve, (l, ("E", PEER_HEADS - 1)))
                        dve.sem_inc(sem("slots_free"), GHALF)
                    dve.wait_ge(sem("sub_scores"), e + 1)
                    best_keys(0, e, sm[:, e % 2, 0, :])
                    dve.sem_inc(sem("sub_best"), 1)
                    best_sums(0, e)
                    if e == PEER_HEADS // 2 - 1:
                        experts_of(0, 0)
                    if e == PEER_HEADS - 1:
                        experts_of(0, 1)
            gates_of(0)

            def row(run, k, turn, consume):
                dve.wait_ge(sem(f"row_load{k}"), turn * 16 + (16 * TURNS * run + 16))
                dve.wait_ge(sem("slots_free"), turn * GSLOTS + (GSLOTS + PICKS * run + k - 1))
                consume(k, turn * GSLOTS + k).then_inc(sem("slots_free"), 1)

            def rows(run, consume):
                with dve.Fori(0, TURNS) as turn:
                    for k in range(GSLOTS):
                        row(run, k, turn, consume)
                dve.wait_ge(sem("slots_free"), GSLOTS + PICKS * (run + 1))

            def dot(t):
                return lambda k, j: v.scalar_tensor_tensor(
                    out=product[:, :] if k % 2 else spare_product, in0=gslot[k], scalar=1.0, in1=normed[:, t, :],
                    op0=ALU.mult, op1=ALU.mult, accum_out=dots[:, t, j:j + 1] if isinstance(j, int)
                    else dots[:, t, bass.ds(j, 1)])

            for turn in range(TURNS):
                for k in range(GSLOTS):
                    row(0, k, turn, dot(0))
                if turn < 4:
                    for e in (2 * turn, 2 * turn + 1):
                        best_keys(1, e, later_scores[:, e, :])
                        best_sums(1, e)
                if turn in (1, 3):
                    experts_of(1, turn // 2)
                if turn == 4:
                    gates_of(1)
            dve.wait_ge(sem("slots_free"), GSLOTS + PICKS)
            dve.sem_inc(sem("dots_ready"), 1)
            rows(1, dot(1))
            dve.sem_inc(sem("dots_ready"), 1)
            do(v.memset(acc, 0.0))
            for t in range(TT):
                dve.wait_ge(sem("gelu_done"), t + 1)
                do(v.tensor_tensor(gate[:, t, :], gate[:, t, :], dots[:, t, :], ALU.mult))
                do(v.memset(spare_product, 0.0))
                rows(TT + t, lambda k, j: v.scalar_tensor_tensor(
                    out=spare_product if k % 2 else acc[:, t, :], in0=gslot[k], scalar=gate[:, t, bass.ds(j, 1)],
                    in1=spare_product if k % 2 else acc[:, t, :], op0=ALU.mult, op1=ALU.add))
                do(v.tensor_tensor(acc[:, t, :], acc[:, t, :], spare_product, ALU.add))
                do(v.tensor_tensor(acc[:, t, :], acc[:, t, :], row_gate2, ALU.mult))
                do(v.tensor_tensor(x[:, t, :], x[:, t, :], acc[:, t, :], ALU.add), "x_last")
                dve.wait_ge(sem("row_rstd"), 2 * TT + t + 1)
                refine(stat[:, 12 + t:13 + t], stat[:, 10 + t:11 + t], RMS_EPS, stat[:, 14:15], 1.0 / D_MODEL)
                do(v.scalar_tensor_tensor(out=x[:, t, :], in0=x[:, t, :], scalar=stat[:, 12 + t:13 + t],
                                          in1=final_g, op0=ALU.mult, op1=ALU.mult), "result")


_NAMES = ["x", "mem", "positions", "w_in", "hgrn_lb_logits", "hgrn_out_norm", "mla_q_norm", "mla_kv_norm",
          "w_mla_uq", "w_mla_uk", "w_mla_uv", "w_mem_k", "w_mem_v", "w_out", "ln_g", "ln_b", "c_2", "pool_scale_2",
          "w_ada_2", "b_ada_2", "norm1_g_2", "w_in_2", "pool_w_2", "w_out_2", "norm2_g_2", "peer_wq_2",
          "peer_subkeys_2", "peer_u_2", "peer_v_2", "final_g_2"]


def kernel(**inputs):
    import concourse.bacc as bacc
    from concourse import mybir
    from concourse.bass_utils import run_bass_kernel_spmd

    nc = bacc.Bacc("TRN2", target_bir_lowering=False, num_devices=1)
    arrays = {n: np.ascontiguousarray(inputs[n]) for n in _NAMES}
    arrays.update(constants())
    d = {n: nc.dram_tensor(f"in_{n}", a.shape, mybir.dt.from_np(a.dtype), kind="ExternalInput").ap()
         for n, a in arrays.items()}
    out = nc.dram_tensor("out", (T, D_MODEL), mybir.dt.float32, kind="ExternalOutput").ap()
    build(nc, d, out)
    got = run_bass_kernel_spmd(nc, [{f"in_{n}": a for n, a in arrays.items()}], core_ids=[0])
    return got.results[0]["out"].reshape(1, T, D_MODEL)
```

```python
import numpy as np

P = 128
D_MODEL = 1024
T = 256
TT = T // P
DC = D_MODEL // P
DEPTH = 2
HG_HEADS = 8
GH = HG_HEADS // 2
MLA_HEADS, NOPE, ROPE, MLA_V = 8, 64, 32, 64
Q_RANK = 256
MEM_HEADS = 4
ALPHA = (2 * DEPTH) ** 0.25
MLA_SCALE = (NOPE + ROPE) ** -0.5
MEM_SCALE = 128 ** -0.5
RMS_EPS, LN_EPS = 1e-6, 1e-5
NEG_BIG = -1e30
COLS = 512
RING = 3

HEADS2, HD2 = 8, 64
PEER_HEADS, NKEYS, TOPK = 8, 128, 16
PICKS = PEER_HEADS * TOPK
GSLOTS = 16
GHALF = GSLOTS // 2
TURNS = PICKS // GSLOTS

IN_UNITS = [("G0", 3072), ("G1", 3584), ("GM", 4512), ("GE", 5536), ("F0", 1024), ("F1", 1536),
            ("Q0", 0), ("Q1", 512), ("C", 4096), ("I0", 2048), ("I1", 2560), ("MQ", 5024)]
B2 = DEPTH
N_MOD = 6
N_MOD_UNITS = N_MOD * D_MODEL // COLS

LAYER = """MK X C F0 N Q0 FP0 UP F1 Da01 Da02 Db01 L00 A0 Da03 Db02 L01 GM A1 Da04 Db03 L02 A2 AD
    Da05 Db04 L03 Q1 A3 Da06 Db05 L04 A4 AD Da07 Db06 L05 I0 A5 Da08 Db07 L06 A6 AD Db08 L07 MV A7 L08 FP1
    MQ AD A8 G0 H00 Da11 Da12 Db11 H01 L10 A9 Da13 Db12 L11 GE A10 H02 Da14 Db13 L12 A11 Da15 Db14 L13 I1
    A12 Da16 Db15 L14 A13 G1 Da17 Db16 L15 A14 Da18 Db17 L16 O0 Db18 L17 O2 L18 H10 AD H11 AD H12 O3 O1 LN"""
BLOCK2 = """X BV MB BQ BK B0 BU B1 B2 B3 B4 B5 SK B6 B7 PM B8 O1 B9 B10 O0
    OUT X2 K0 E0 E1 K1 E2 E3 K2 K3 E4 E5 E6 E7"""


def all_tasks():
    out, n = [], 0
    for text in [LAYER] * DEPTH + [BLOCK2]:
        tasks = []
        for task in text.split():
            if task == "AD":
                task, n = f"AD{n}", n + 1
            tasks.append(task)
            if task == "X" and not out:
                tasks.append("VEC")
        out.append(tasks)
    assert n == N_MOD_UNITS
    return out


TASKS = all_tasks()
ONE_SLOT = {"MK", "MV", "C", "F0", "F1", "Q0", "Q1", "G0", "G1", "GM", "GE", "I0", "I1", "MQ",
            "BQ", "BK", "BV", "BU", "K0", "K1", "K2", "K3"}


def output_unit(task):
    return task[0] == "O" and task[1:].isdigit()


OUT_UNITS = [[task for task in tasks if output_unit(task)] for tasks in TASKS]


def stream():
    out = []
    for l, tasks in enumerate(TASKS):
        for task in tasks:
            if task in ONE_SLOT or task == "UP" or task[:2] == "AD" or output_unit(task):
                out.append((l, task))
    return out


STREAM = stream()
UNIT = {key: n for n, key in enumerate(STREAM)}


def big_uses():
    out, uses, turn = {}, [0, 0], 0
    for l, name in STREAM:
        if name == OUT_UNITS[l][0]:
            out[l, "OUT"] = tuple(uses)
            uses = [uses[0] + 1, uses[1] + 1]
            turn = 0
        elif name in ONE_SLOT:
            out[l, name] = (turn, uses[turn])
            uses[turn] += 1
            turn = 1 - turn
    return out


BIG = big_uses()
N_ATT = MLA_HEADS + MEM_HEADS


def bank_uses(task):
    if task in ("X", "X2"):
        return [(task, j) for j in range(4)]
    if task == "VEC":
        return [("VEC",)]
    if task == "SK":
        return [("SK",)]
    if task == "PM":
        return [("PL", j) for j in range(2)]
    if task[0] == "E":
        return [("E", int(task[1:]))]
    if task[0] == "B" and task[1:].isdigit():
        i = int(task[1:])
        out = [("S", i)] if i < HEADS2 else []
        out += [("PT", i - 2)] if 2 <= i <= HEADS2 + 1 else []
        return out + ([("AO", i - 3)] if i >= 3 else [])
    if task[0] == "L" and task[1:].isdigit():
        g, m = int(task[1]), int(task[2])
        return [("L", g, m, j) for j in range(2 if m < 8 else 1)]
    if task[:2] == "AD":
        return [(task,)]
    if task == "MB":
        return [("MB", v, k) for v in range(4) for k in range(2)]
    if task == "N":
        return [("N",), ("KR",)]
    if task == "UP":
        return ([("UQ", j) for j in range(4)] + [("UK", j) for j in range(4)]
                + [("UV", t) for t in range(TT)] + [("QR", j) for j in range(4)])
    if task[0] == "A" and task[1:].isdigit():
        i = int(task[1:])
        out = [("S", i)] if i < N_ATT else []
        out += [("PT", i - 2)] if 2 <= i <= N_ATT + 1 else []
        return out + ([("AO", i - 3)] if i >= 3 else [])
    if task[0] == "H":
        g, i = int(task[1]), int(task[2])
        return ([("HO", 2 * g + i)] if i < 2 else []) + ([("HN", 2 * g + i - 1)] if i >= 1 else [])
    return []


EXPERT_PARTS = [(0, 0, 2), (0, 2, 4), (0, 4, 8), (1, 0, 4), (1, 4, 8)]


def expert_rows(t):
    out = [(0, (last - first) * TOPK // GSLOTS, n + 1)
           for n, (tile, first, last) in enumerate(EXPERT_PARTS) if tile == t]
    return out + [(1, TURNS, 0)]


def bank_index():
    out, n = {}, 0
    for j in range(4):
        out["M", j] = n
        n += 1
    for l in range(DEPTH + 1):
        for task in TASKS[l]:
            for key in bank_uses(task):
                out[l, key] = n
                n += 1
    return out


def constants():
    i = np.arange(P)
    level = np.zeros((P, 7, P), np.int32)
    for m in range(1, 8):
        h = 2 ** (m - 1)
        same = (i[:, None] // (2 * h)) == (i[None, :] // (2 * h))
        level[:, m - 1] = same & ((i[:, None] // h) % 2 == 0) & ((i[None, :] // h) % 2 == 1)
    t = np.arange(T)
    causal = np.where(t[None, :] <= t[:, None], 0.0, NEG_BIG).astype(np.float32)
    rot = np.zeros((P, 32), np.float32)
    for j in range(16):
        for base in (0, 64):
            rot[base + j + 16, j] = -1.0
            rot[base + j, j + 16] = 1.0
    inv = np.float32(1.0) / (np.float32(10000.0) ** (np.arange(0, ROPE, 2, dtype=np.float32) / np.float32(ROPE)))
    dist = (t[:, None] - t[None, :])
    count = ((dist >= 0) & (dist <= 128)).astype(np.float32)
    for d in (4, 16):
        count += (dist >= 0) & (dist % d == 0)
    far = np.where(count > 0, dist, 1e30).astype(np.float32)
    inv_count = np.stack([1.0 / np.minimum(t + 1, w) for w in (2, 4, 8, 16)]).astype(np.float32)
    return {
        "c_eye": np.eye(P, dtype=np.float32),
        "c_level": level.reshape(P, 7 * P),
        "c_causal": causal, "c_rot": rot,
        "c_inv_freq": np.tile(inv, P // 16).reshape(1, P).astype(np.float32),
        "c_count": count, "c_dist": far, "c_inv_count": inv_count.reshape(1, 4 * T),
        "c_iota": np.arange(16, dtype=np.float32).reshape(1, 16),
    }


def build(nc, d, out):
    import concourse.bass as bass
    from concourse import mybir
    from concourse.alu_op_type import AluOpType as ALU
    from contextlib import ExitStack

    f32, u32, i32, u8 = mybir.dt.float32, mybir.dt.uint32, mybir.dt.int32, mybir.dt.uint8
    ACT = mybir.ActivationFunctionType
    X = mybir.AxisListType.X
    BANK = bank_index()

    with ExitStack() as ctx:
        def sb(name, shape, dt=f32):
            return ctx.enter_context(nc.sbuf_tensor(name, shape, dt))

        eye = sb("eye", [P, P])
        ones_mean = sb("ones_mean", [P, P])
        rot = sb("rot", [P, 32])
        level_mask = sb("level_mask", [P, 7, P], u8)
        causal = sb("causal", [P, TT, T])
        vec = sb("vec", [P, 104])
        mod_part = sb("mod_part", [P, 2, COLS])
        more_rows = sb("more_rows", [P, 2, D_MODEL])
        modc = sb("modc", [P, N_MOD, DC])
        lower = sb("lower", [P, DEPTH, 2, 8])
        lbt = sb("lbt", [P, 6, 8])
        eps = sb("eps", [P, 3])
        rope = sb("rope", [P, 2, T])
        stat = sb("stat", [P, 16])
        x = sb("x", [P, TT, D_MODEL])
        xT = sb("xT", [P, DC, T])
        memT = sb("memT", [P, DC, T])
        ring = sb("ring", [P, RING, DC * COLS])
        yT = sb("yT", [P, 16, T])
        big = sb("big", [P, 3, GH * T])
        qT = sb("qT", [P, HG_HEADS, T])
        kT = sb("kT", [P, HG_HEADS, T])
        b = sb("b", [P, HG_HEADS, T])
        pair = sb("pair", [P, GH * TT, P])
        far_pair = sb("far_pair", [P, GH, P])
        hv = sb("hv", [P, TT, D_MODEL])
        cT = sb("cT", [P, 4, T])
        sq = sb("sq", [P, 3, T])
        rstd = sb("rstd", [P, 2, T])
        qM = sb("qM", [96, MLA_HEADS, T])
        kM = sb("kM", [96, MLA_HEADS, T])
        vM = sb("vM", [P, TT, MLA_HEADS * MLA_V])
        qE = sb("qE", [P, MEM_HEADS, T])
        kE = sb("kE", [P, MEM_HEADS, T])
        vE = sb("vE", [P, TT, MEM_HEADS * P])
        sm = sb("sm", [P, 2, TT, T])
        pT = sb("pT", [P, 2, TT, T])
        flat_b = b[:, :, :].rearrange("p a t -> p (a t)")
        vec_rows = flat_b[:, 1700:1700 + P]
        ln_gb = big[:, 0:2, :].rearrange("p a n -> p (a n)")

        flat_pair = pair[:, :, :].rearrange("p a t -> p (a t)")
        w_pool, iota = pair[:, 0:4, :], mod_part[:, 1, 0:TOPK]
        sub_rows = flat_pair[:, 528:528 + 2 * P]
        row_gate1, row_scale2 = hv[:, 0, :], hv[:, 1, :]
        row_shift2, row_gate2, final_g = big[:, 0, :], big[:, 1, :], big[:, 2, :]
        q2, k2, v2 = qT[:, 0:4, :], qT[:, 4:8, :], vE
        uT, pool_sum = kT[:, 0:4, :], kT[:, 4:8, :]
        mixed, inv_count = b[:, 0:4, :], b[:, 4:8, :].rearrange("p a t -> p (a t)")
        count, dist = qE[:, 0:2, :], qE[:, 2:4, :]
        normed = memT[:, :, :].rearrange("p a t -> p (a t)").rearrange("p (a n) -> p a n", a=TT)
        silu_c = lbt[:, 4, :]
        keys_left = mod_part[:, 0, 0:2 * P]

        def flat(tile):
            return tile[:, :, :].rearrange("p a t -> p (a t)")

        shape5 = dict(t=TT, h=PEER_HEADS, two=2)
        sub_val = flat(cT)[:, 0:512].rearrange("p (t h two k) -> p t h two k", **shape5)
        sub_idf = flat(cT)[:, 512:1024].rearrange("p (t h two k) -> p t h two k", **shape5)
        sub_id = flat(kE)[:, 0:512].bitcast(u32).rearrange("p (t h two k) -> p t h two k", **shape5)
        top_pos = flat(kE)[:, 512:768].bitcast(u32).rearrange("p (t j) -> p t j", t=TT)
        digit = flat(kE)[:, 768:896].bitcast(u32)
        top_val = flat(rstd)[:, 0:PICKS * TT].rearrange("p (t h k) -> p t h k", t=TT, h=PEER_HEADS)
        gate = flat(rstd)[:, PICKS * TT:].rearrange("p (t j) -> p t j", t=TT)
        skT = flat(sq)[:, 512:768].rearrange("p (a k) -> p a k", a=2)
        cand, cand_left = flat(sq)[:, 0:256], flat(sq)[:, 256:512]
        first_of, second_of = flat(vM)[:, 0:PICKS], flat(vM)[:, PICKS:2 * PICKS]
        id_a, id_b = flat(vM)[:, 2 * PICKS:3 * PICKS], flat(vM)[:, 3 * PICKS:4 * PICKS]
        expert = flat(vM)[:, 512:768].bitcast(u32).rearrange("p (t j) -> p t j", t=TT)
        dots = flat(vM)[:, 768:1024].rearrange("p (t j) -> p t j", t=TT)
        onehot = flat(qT).rearrange("p (j i) -> p j i", i=TOPK)
        k1_slot, k2_slot = ([ring[:, UNIT[B2, unit] % RING, g * D_MODEL:(g + 1) * D_MODEL] for g in range(4)]
                            for unit in ("K1", "K2"))
        gslot = ([more_rows[:, g, :] for g in range(2)] + [flat(qE), flat(vE)] + k1_slot
                 + k2_slot + [flat(b)[:, g * D_MODEL:(g + 1) * D_MODEL] for g in range(2)] + [hv[:, 1, :], flat_pair])
        turn_idx = causal[:, 0, 0:GSLOTS].bitcast(u32)
        acc = ring[:, UNIT[B2, "K3"] % RING, 0:TT * D_MODEL].rearrange("p (a n) -> p a n", a=TT)
        product = pT[:, :, :, :].rearrange("p a b t -> p (a b t)")
        spare_product = hv[:, 0, :]
        later_scores = kT
        pj = [ctx.enter_context(nc.psum_tensor(f"pj{i}", [P, 1024], f32)) for i in range(2)]
        bank = [ctx.enter_context(nc.psum_tensor(f"bank{i}", [P, 512], f32)) for i in range(4)]

        made = {}

        def sem(name):
            if name not in made:
                made[name] = ctx.enter_context(nc.semaphore(name))
            return made[name]

        PER = dict(xT_ready=4, gates=4, fz=2, f_exp=2, f_pos=2, f_ln=2, k_ready=2, q_ready=2,
                   lvl_sub=16, lvl_exp=16, lvl_ready=16, blended=18, out_tile=1, c_ready=1, c_sq=1, c_rstd=1,
                   c_normed=1, kr_ready=1, kr_spread=1, uq_ready=4, qrope_ready=4, uk_ready=4,
                   uv_ready=2, hv_ready=2, qE_ready=1, kE_ready=1, vE_ready=1,
                   sm_ready=12, exp_done=12, p_ready=12, pt_ready=12, y_att=12,
                   ho_sq=4, ho_rstd=4, y_hg=4, ln_in=2, ln_rstd=2, x_next=2)

        def after(eng, name, l, i=0):
            eng.wait_ge(sem(name), l * PER[name] + i + 1)

        GATE_OF = {name: n for n, name in enumerate(t for t in TASKS[0] if t in ("G0", "G1", "GM", "GE"))}

        def bank_of(key):
            return bank[BANK[key] % 4]

        def bank_filled(eng, key):
            eng.wait_ge(sem("bank_filled"), BANK[key] + 1)

        def bank_empty(eng, key):
            n = BANK[key]
            if n >= 4:
                eng.wait_ge(sem(f"bank_free{n % 4}"), n // 4)

        def bank_free(key):
            n = BANK[key]
            return f"bank_free{n % 4}", n // 4 + 1

        UQ_W = 2 * MLA_HEADS * (NOPE + ROPE)

        def up_weights(slot):
            w = ring[:, slot, :]
            return (w[:, 0:UQ_W].rearrange("p (c n) -> p c n", c=2), w[:, UQ_W:UQ_W + 512],
                    w[:, UQ_W + 512:UQ_W + 1024])

        def ring_loads(n):
            units = range(n % RING, n + 1, RING)
            return 16 * sum(3 if STREAM[k][1] == "UP" else 1 for k in units)

        def unit_done(eng, l, name):
            eng.wait_ge(sem("unit_done"), UNIT[l, name] + 1)

        def steps(eng, own):
            seen = {}

            def step(ins, name=None, value=None, behind=0):
                name = name or own
                seen[name] = value or seen.get(name, 0) + 1
                ins.then_inc(sem(name), 1)
                eng.wait_ge(sem(name), seen[name] - behind)
            return step

        V_LB, V_OUT, V_QN, V_KN, V_INV = 0, 16, 18, 22, 24
        V_C, V_POOL, V_N1, V_N2, V_BADA = 25, 33, 37, 45, 53
        N_B2 = 5
        N_CONST = 14

        block = ctx.enter_context(nc.Block())

        @block.sync
        def _(sp):
            def load(dst, src, name="consts_load"):
                sp.dma_start(dst, src).then_inc(sem(name), 16)

            load(eye[:, :], d["c_eye"], "eye_load")
            load(big[:, 0:2, :], d["mem"].rearrange("o (a p) n -> p (o a) n", p=P), "mem_load")

            def weights(n):
                if n >= RING:
                    sp.wait_ge(sem("unit_done"), n - RING + 1)
                l, name = STREAM[n]
                slot = n % RING
                arrived = f"ring_load{slot}"
                if name == "UP":
                    w_uq, w_uk, w_uv = up_weights(slot)
                    load(w_uq, d["w_mla_uq"][l].rearrange("(c p) n -> p c n", p=P), arrived)
                    load(w_uk, d["w_mla_uk"][l], arrived)
                    load(w_uv, d["w_mla_uv"][l], arrived)
                    return
                if name[0] == "O":
                    j = int(name[1])
                    src = d["w_out"][l] if l < DEPTH else d["w_out_2"][0]
                    load(ring[:, slot, :].rearrange("p (c n) -> p c n", c=4),
                         src[j * 512:(j + 1) * 512, :].rearrange("(c p) n -> p c n", p=P), arrived)
                    return
                if name == "MK":
                    src = d["w_mem_k"][l]
                elif name == "MV":
                    src = d["w_mem_v"][l]
                elif name[:2] == "AD":
                    j = int(name[2:])
                    src = d["w_ada_2"][0, :, j * COLS:(j + 1) * COLS]
                elif l < DEPTH:
                    c0 = dict(IN_UNITS)[name]
                    src = d["w_in"][l, :, c0:c0 + (416 if name == "C" else COLS)]
                elif name[0] == "B":
                    j = "QKVU".index(name[1])
                    src = d["w_in_2"][0, :, j * COLS:(j + 1) * COLS]
                else:
                    j = int(name[1])
                    src = d["peer_wq_2"][0, :, j * COLS:(j + 1) * COLS]
                w = src.shape[1]
                load(ring[:, slot, :].rearrange("p (c n) -> p c n", c=DC)[:, :, 0:w],
                     src.rearrange("(c p) n -> p c n", p=P), arrived)

            weights(0)
            load(x[:, :, :], d["x"].rearrange("o (a p) n -> p (o a) n", p=P), "x_load")
            sp.wait_ge(sem("vec_zeroed"), 1)
            load(vec_rows[V_LB:V_LB + 16, :], d["hgrn_lb_logits"].rearrange("l (h p) -> (l h) p", p=P))
            load(vec_rows[V_OUT:V_OUT + 2, :], d["hgrn_out_norm"])
            load(vec_rows[V_QN:V_QN + 4, :], d["mla_q_norm"].rearrange("l (h p) -> (l h) p", p=P))
            load(vec_rows[V_KN:V_KN + 2, :], d["mla_kv_norm"])
            load(vec_rows[V_INV:V_INV + 1, :], d["c_inv_freq"])
            load(vec_rows[V_C:V_C + 8, :], d["c_2"].rearrange("l (h p) -> (l h) p", p=P))
            load(vec_rows[V_POOL:V_POOL + 4, :], d["pool_scale_2"].rearrange("l (h p) -> (l h) p", p=P))
            load(vec_rows[V_N1:V_N1 + 8, :], d["norm1_g_2"].rearrange("l (h p) -> (l h) p", p=P))
            load(vec_rows[V_N2:V_N2 + 8, :], d["norm2_g_2"].rearrange("l (h p) -> (l h) p", p=P))
            load(vec_rows[V_BADA:V_BADA + 48, :], d["b_ada_2"].rearrange("l (h p) -> (l h) p", p=P))
            load(rot[:, :], d["c_rot"])
            load(flat_b[:, 800:1696].bitcast(i32), d["c_level"])
            load(causal[:, :, :], d["c_causal"].rearrange("(a p) s -> p a s", p=P))
            load(flat_b[:, 0:T].bitcast(i32), d["positions"].to_broadcast([P, T]))

            for l in range(DEPTH + 1):
                units = [name for k, name in STREAM if k == l]
                for name in units:
                    if l < DEPTH and name == OUT_UNITS[l][-1]:
                        bank_filled(sp, (l, ("L", 1, 7, 1)))
                        load(ln_gb[:, 0:D_MODEL], d["ln_g"][l:l + 1, :].to_broadcast([P, D_MODEL]), "gb_load")
                        load(ln_gb[:, D_MODEL:], d["ln_b"][l:l + 1, :].to_broadcast([P, D_MODEL]), "gb_load")
                    if UNIT[l, name]:
                        weights(UNIT[l, name])
                    if name == units[2] and l == B2:
                        after(sp, "x_next", DEPTH - 1, 1)
                        load(count[:, :, :], d["c_count"].rearrange("(a p) s -> p a s", p=P), "table_load")
                        load(dist[:, :, :], d["c_dist"].rearrange("(a p) s -> p a s", p=P), "table_load")
                        load(final_g, d["final_g_2"].rearrange("(o n) -> o n", o=1).to_broadcast([P, D_MODEL]), "b2_load")
                        load(inv_count, d["c_inv_count"].to_broadcast([P, 4 * T]), "b2_load")
                        load(w_pool, d["pool_w_2"].rearrange("o g c e -> c (o g) e"), "b2_load")
                        load(sub_rows.rearrange("p (a k) -> p a k", a=2),
                             d["peer_subkeys_2"].rearrange("o a n k -> n (o a) k"), "b2_load")
                        load(iota, d["c_iota"].to_broadcast([P, 16]), "b2_load")
            for t in range(TT):
                sp.wait_ge(sem("result"), t + 1)
                sp.dma_start(out[t * P:(t + 1) * P, :], x[:, t, :]).then_inc(sem("out_store"), 16)
            sp.wait_ge(sem("out_store"), 16 * TT)

        @block.gpsimd
        def _(pool):
            g = nc.gpsimd
            do = steps(pool, "pool_step")
            pool.wait_ge(sem("silu_c"), 1)
            for l in range(DEPTH + 1):
                for task in TASKS[l]:
                    if task[:2] == "AD":
                        j, n = int(task[2:]), UNIT[l, task]
                        pool.wait_ge(sem(f"ring_load{n % RING}"), ring_loads(n))
                        if j >= 2:
                            key = (l, (f"AD{j - 2}",)) if (l, (f"AD{j - 2}",)) in BANK else (l - 1, (f"AD{j - 2}",))
                            bank_filled(pool, key)
                        w = ring[:, n % RING, :].rearrange("p (c n) -> p c n", c=DC)
                        part = mod_part[:, j % 2, :]
                        do(g.tensor_tensor(w, w, silu_c.unsqueeze(2).to_broadcast([P, DC, COLS]), ALU.mult))
                        do(g.tensor_tensor(w[:, 0:4, :], w[:, 0:4, :], w[:, 4:8, :], ALU.add))
                        do(g.tensor_tensor(w[:, 0:2, :], w[:, 0:2, :], w[:, 2:4, :], ALU.add))
                        do(g.tensor_tensor(part, w[:, 0, :], w[:, 1, :], ALU.add), "mod_partial")
            pool.wait_ge(sem("uT_ready"), 1)
            pool.wait_ge(sem("b2_load"), 16 * N_B2)
            do(g.tensor_copy(pool_sum, uT))
            for w in range(4):
                for k in range(w + 1):
                    n = 2 ** k
                    spare = mixed[:, w, :]
                    do(g.tensor_copy(spare, pool_sum[:, w, :]))
                    do(g.tensor_tensor(pool_sum[:, w, n:T], spare[:, n:T], spare[:, 0:T - n], ALU.add))
            do(g.tensor_tensor(mixed, pool_sum, inv_count.rearrange("p (a t) -> p a t", a=4), ALU.mult))
            do(g.tensor_tensor(mixed, mixed, uT, ALU.subtract), "pool_mixed")
            tables = [d["peer_u_2"].rearrange("o e n -> (o e) n"), d["peer_v_2"].rearrange("o e n -> (o e) n")]
            turns, before = 0, None
            for t in range(TT):
                for table, n_turns, found in expert_rows(t):
                    first = 0 if table != before else first
                    before = table
                    if found:
                        pool.wait_ge(sem("experts"), found)
                    with pool.Fori(0, n_turns) as turn:
                        for half in range(2):
                            pool.wait_ge(sem("slots_free"), turn * GSLOTS + (turns * GSLOTS + (half + 1) * GHALF))
                            pool.sem_inc(sem("gather_turn"), 1)
                            idx = turn_idx[:, half * GHALF:(half + 1) * GHALF]
                            src = expert[:, t, bass.ds(turn * GSLOTS + (first * GSLOTS + half * GHALF), GHALF)]
                            g.tensor_copy(idx, src).then_inc(sem("idx_ready"), 1)
                            pool.wait_ge(sem("idx_ready"), turn * 2 + (2 * turns + half + 1))
                            pool.sem_inc(sem("gather_turn"), 1)
                            for k in range(GHALF):
                                slot = half * GHALF + k
                                pool.indirect_dma_start(
                                    gslot[slot], None, tables[table],
                                    bass.IndirectOffsetOnAxis(ap=idx[:, k:k + 1], axis=0))\
                                    .then_inc(sem(f"row_load{slot}"), 16)
                    turns += n_turns
                    first += n_turns

        @block.tensor
        def _(pe):
            def last(ins, name="bank_filled"):
                ins.then_inc(sem(name), 1)

            def transposes(key, pairs):
                bank_empty(pe, key)
                for dst, src in pairs:
                    ins = nc.tensor.transpose(dst, src, eye[:, :])
                last(ins)

            def loaded(l, name):
                n = UNIT[l, name]
                pe.wait_ge(sem(f"ring_load{n % RING}"), ring_loads(n))
                return n % RING

            def channel_major(l, name, act, width=COLS):
                slot = loaded(l, name)
                w = ring[:, slot, :].rearrange("p (c n) -> p c n", c=DC)
                s, use = BIG[l, name]
                if use:
                    pe.wait_ge(sem(f"pj_free{s}"), use)
                for m in range(0, width, P):
                    n = min(P, width - m)
                    for c in range(DC):
                        ins = nc.tensor.matmul(pj[s][0:n, 2 * m:2 * m + T], w[:, c, m:m + n], act[:, c, :],
                                               start=(c == 0), stop=(c == DC - 1))
                last(ins, "unit_done")

            def token_major(l, name, act):
                slot = loaded(l, name)
                w = ring[:, slot, :].rearrange("p (c n) -> p c n", c=DC)
                s, use = BIG[l, name]
                if use:
                    pe.wait_ge(sem(f"pj_free{s}"), use)
                for t in range(TT):
                    for c in range(DC):
                        ins = nc.tensor.matmul(pj[s][:, t * COLS:(t + 1) * COLS], act[:, c, t * P:(t + 1) * P],
                                               w[:, c, :], start=(c == 0), stop=(c == DC - 1))
                last(ins, "unit_done")

            pe.wait_ge(sem("eye_load"), 16)
            pe.wait_ge(sem("mem_load"), 16)
            mem = big[:, 0:2, :]
            for j in range(4):
                B = bank[BANK["M", j] % 4]
                transposes(("M", j), [(B[:, (cc * TT + a) * P:(cc * TT + a + 1) * P],
                                       mem[:, a, (2 * j + cc) * P:(2 * j + cc + 1) * P])
                                      for cc in range(2) for a in range(TT)])
            def output_product(l, name):
                j = int(name[1:])
                first, stop = name == OUT_UNITS[l][0], name == OUT_UNITS[l][-1]
                if first:
                    for s in range(2):
                        pe.wait_ge(sem(f"pj_free{s}"), BIG[l, "OUT"][s])
                slot = loaded(l, name)
                w = ring[:, slot, :].rearrange("p (c n) -> p c n", c=4)
                for t in range(TT):
                    for n in range(2):
                        for c in range(4):
                            ins = nc.tensor.matmul(
                                pj[t][:, n * 512:(n + 1) * 512], yT[:, 4 * j + c, t * P:(t + 1) * P],
                                w[:, c, n * 512:(n + 1) * 512],
                                start=(first and c == 0), stop=(stop and c == 3))
                    if t == 0 and stop:
                        last(ins, "out_tile")
                last(ins, "unit_done")

            def scores(l, i, q, k):
                key = (l, ("S", i))
                bank_empty(pe, key)
                B = bank_of(key)
                for t in range(TT):
                    ins = nc.tensor.matmul(B[:, t * T:(t + 1) * T], q[:, t * P:(t + 1) * P], k, start=True, stop=True)
                last(ins)

            def weights_transposed(l, i):
                key = (l, ("PT", i))
                after(pe, "p_ready", l, i)
                B = bank_of(key)
                transposes(key, [(B[:, s * T + t * P:s * T + (t + 1) * P], sm[:, i % 2, t, s * P:(s + 1) * P])
                                 for s in range(TT) for t in range(TT)])

            def values_summed(l, i, rows, v):
                key = (l, ("AO", i))
                bank_empty(pe, key)
                after(pe, "pt_ready", l, i)
                for s in range(TT):
                    ins = nc.tensor.matmul(bank_of(key)[rows, 0:T], v[s], pT[:, i % 2, s, :],
                                           start=(s == 0), stop=(s == TT - 1))
                last(ins)

            def transposed_x(l, task, src, ready):
                for j in range(4):
                    a, c0 = j // 2, 4 * (j % 2)
                    if j % 2 == 0:
                        ready(a)
                    B = bank_of((l, (task, j)))
                    transposes((l, (task, j)), [(B[:, c * P:(c + 1) * P], src[:, a, (c0 + c) * P:(c0 + c + 1) * P])
                                                for c in range(4)])
                after(pe, "xT_ready", l, 3)

            def transposed_with_unit(l, task, src, rows, name):
                slot = loaded(l, name)
                w = ring[:, slot, :].rearrange("p (c n) -> p c n", c=DC)
                s, use = BIG[l, name]
                for a in range(TT):
                    tile = slice(a * P, (a + 1) * P)
                    pe.wait_ge(sem("row_normed"), rows + a + 1)
                    for j in (2 * a, 2 * a + 1):
                        B = bank_of((l, (task, j)))
                        c0 = 4 * (j % 2)
                        transposes((l, (task, j)), [(B[:, c * P:(c + 1) * P], src[:, a, (c0 + c) * P:(c0 + c + 1) * P])
                                                    for c in range(4)])
                    after(pe, "xT_ready", l, (0 if task == "X" else 4) + 2 * a + 1)
                    if use and a == 0:
                        pe.wait_ge(sem(f"pj_free{s}"), use)
                    if name == "BV":
                        for c in range(DC):
                            ins = nc.tensor.matmul(pj[s][:, a * COLS:(a + 1) * COLS], xT[:, c, tile], w[:, c, :],
                                                   start=(c == 0), stop=(c == DC - 1))
                    else:
                        for m in range(0, COLS, P):
                            for c in range(DC):
                                ins = nc.tensor.matmul(pj[s][:, 2 * m + a * P:2 * m + (a + 1) * P], w[:, c, m:m + P],
                                                       xT[:, c, tile], start=(c == 0), stop=(c == DC - 1))
                last(ins, "unit_done")

            def attention(l, i):
                if i < N_ATT:
                    if i < MLA_HEADS:
                        after(pe, "qrope_ready", l, i // 2)
                        after(pe, "uk_ready", l, i // 2)
                        after(pe, "kr_spread", l)
                        scores(l, i, qM[:, i, :], kM[:, i, :])
                    else:
                        after(pe, "qE_ready", l)
                        after(pe, "kE_ready", l)
                        scores(l, i, qE[:, i - MLA_HEADS, :], kE[:, i - MLA_HEADS, :])
                if 2 <= i <= N_ATT + 1:
                    weights_transposed(l, i - 2)
                if i >= 3:
                    k = i - 3
                    if k < MLA_HEADS:
                        after(pe, "uv_ready", l, 1)
                        values_summed(l, k, slice(64 * (k % 2), 64 * (k % 2) + 64),
                                      [vM[:, s, k * 64:(k + 1) * 64] for s in range(TT)])
                    else:
                        after(pe, "vE_ready", l)
                        k -= MLA_HEADS
                        values_summed(l, i - 3, slice(0, P), [vE[:, s, k * P:(k + 1) * P] for s in range(TT)])

            def level(l, g, m):
                if m == 0:
                    after(pe, "k_ready", l, g)
                    after(pe, "q_ready", l, g)
                else:
                    after(pe, "lvl_ready", l, 8 * g + m - 1)
                W = big[:, m % 3, :].rearrange("p (h t) -> p h t", t=T)
                for j in range(2 if m < 8 else 1):
                    key = (l, ("L", g, m, j))
                    bank_empty(pe, key)
                    B = bank_of(key)
                    for n in range(4):
                        if m == 8:
                            k, q = W[:, n, 0:P], W[:, n, P:T]
                        else:
                            hd, t = (4 * j + n) // TT, (4 * j + n) % TT
                            q = W[:, hd, t * P:(t + 1) * P]
                            k = q
                            if m == 0:
                                q = qT[:, GH * g + hd, t * P:(t + 1) * P]
                                k = kT[:, GH * g + hd, t * P:(t + 1) * P]
                        ins = nc.tensor.matmul(B[:, n * P:(n + 1) * P], k, q, start=True, stop=True)
                    last(ins)

            def readout(l, g, i):
                if i < 2:
                    key = (l, ("HO", 2 * g + i))
                    bank_empty(pe, key)
                    after(pe, "blended", l, 9 * g + 8)
                    after(pe, "hv_ready", l, g)
                    B = bank_of(key)
                    for k in range(2):
                        hd = 2 * i + k
                        c = (GH * g + hd) * P
                        v = [hv[:, t, c:c + P] for t in range(TT)]
                        o = B[:, k * T:(k + 1) * T]
                        nc.tensor.matmul(o[:, 0:P], v[0], pair[:, hd * TT, :], start=True, stop=True)
                        nc.tensor.matmul(o[:, P:T], v[0], far_pair[:, hd, :], start=True, stop=False)
                        ins = nc.tensor.matmul(o[:, P:T], v[1], pair[:, hd * TT + 1, :], start=False, stop=True)
                    last(ins)
                if i >= 1:
                    n = 2 * g + i - 1
                    key = (l, ("HN", n))
                    bank_empty(pe, key)
                    after(pe, "ho_sq", l, n)
                    last(nc.tensor.matmul(bank_of(key)[:, :], ones_mean[:, :],
                                          sq[:, 0:2, :].rearrange("p a t -> p (a t)"), start=True, stop=True))

            def modulation(l, task):
                j = int(task[2:])
                key = (l, (task,))
                bank_empty(pe, key)
                pe.wait_ge(sem("mod_partial"), j + 1)
                for m in range(COLS // P):
                    ins = nc.tensor.matmul(bank_of(key)[:, m:m + 1], mod_part[:, j % 2, m * P:(m + 1) * P],
                                           ones_mean[:, 0:1], start=True, stop=True)
                last(ins)
                pe.wait_ge(sem("bank_filled"), BANK[key] + 1)
                pe.sem_inc(sem("unit_done"), 1)

            for l in range(DEPTH):
                for task in TASKS[l]:
                    if task == "X":
                        if l:
                            transposed_x(l, "X", x, lambda a: after(pe, "x_next", l - 1, a))
                        else:
                            transposed_x(l, "X", x, lambda a: pe.wait_ge(sem("x_load"), 16))
                    elif task in ("G0", "G1", "GM", "GE", "F0", "F1", "Q0", "Q1", "C", "MQ"):
                        channel_major(l, task, xT, 416 if task == "C" else COLS)
                    elif task in ("I0", "I1"):
                        token_major(l, task, xT)
                    elif task == "MK":
                        pe.wait_ge(sem("memT_ready"), 4)
                        channel_major(l, task, memT)
                    elif task == "VEC":
                        pe.wait_ge(sem("consts_load"), 16 * N_CONST)
                        transposes((0, ("VEC",)), [(bank_of((0, ("VEC",)))[:, 0:P], vec_rows)])
                        pe.wait_ge(sem("ones_ready"), 1)
                    elif task == "MV":
                        token_major(l, task, memT)
                    elif task[0] == "L" and task != "LN":
                        level(l, int(task[1]), int(task[2]))
                    elif task[:2] == "AD":
                        modulation(l, task)
                    elif task[0] == "A":
                        attention(l, int(task[1:]))
                    elif task[0] == "H":
                        readout(l, int(task[1]), int(task[2]))
                    elif task == "N":
                        key = (l, ("N",))
                        bank_empty(pe, key)
                        after(pe, "c_sq", l)
                        B = bank_of(key)
                        for c in range(2):
                            nc.tensor.matmul(B[:, 0:T], ones_mean[:, :], sq[:, c, :], start=(c == 0), stop=(c == 1))
                        last(nc.tensor.matmul(B[:, T:2 * T], ones_mean[:, :], sq[:, 2, :], start=True, stop=True))
                        key = (l, ("KR",))
                        bank_empty(pe, key)
                        last(nc.tensor.matmul(bank_of(key)[0:32, 0:T], rot[0:32, :], cT[0:32, 3, :],
                                              start=True, stop=True))
                    elif task == "UP":
                        w_uq, w_uk, w_uv = up_weights(loaded(l, "UP"))
                        after(pe, "c_normed", l)
                        for j in range(4):
                            key = (l, ("UQ", j))
                            bank_empty(pe, key)
                            B = bank_of(key)
                            for k in range(2):
                                h = 2 * j + k
                                for c in range(2):
                                    ins = nc.tensor.matmul(B[0:96, k * T:(k + 1) * T], w_uq[:, c, h * 96:(h + 1) * 96],
                                                           cT[:, c, :], start=(c == 0), stop=(c == 1))
                            last(ins)
                        for j in range(4):
                            key = (l, ("UK", j))
                            bank_empty(pe, key)
                            for k in range(2):
                                h = 2 * j + k
                                ins = nc.tensor.matmul(bank_of(key)[0:64, k * T:(k + 1) * T],
                                                       w_uk[:, h * 64:(h + 1) * 64], cT[:, 2, :], start=True, stop=True)
                            last(ins)
                        for t in range(TT):
                            key = (l, ("UV", t))
                            bank_empty(pe, key)
                            last(nc.tensor.matmul(bank_of(key)[:, :], cT[:, 2, t * P:(t + 1) * P], w_uv,
                                                  start=True, stop=True))
                        pe.wait_ge(sem("bank_filled"), BANK[key] + 1)
                        pe.sem_inc(sem("unit_done"), 1)
                        for j in range(4):
                            key = (l, ("QR", j))
                            bank_empty(pe, key)
                            after(pe, "uq_ready", l, j)
                            last(nc.tensor.matmul(bank_of(key)[64:96, :], rot[64:96, :],
                                                  qM[64:96, 2 * j:2 * j + 2, :].rearrange("p a t -> p (a t)"),
                                                  start=True, stop=True))
                    elif output_unit(task):
                        signal, i = (("y_hg", 1), ("y_hg", 3), ("y_att", MLA_HEADS - 1), ("y_att", N_ATT - 1))[int(task[1])]
                        after(pe, signal, l, i)
                        output_product(l, task)

            l = B2
            for task in TASKS[l]:
                if task in ("X", "X2"):
                    k = 0 if task == "X" else TT
                    transposed_with_unit(l, task, normed, k, "BV" if task == "X" else "K0")
                elif task == "MB":
                    pe.wait_ge(sem("mod_ready"), 1)
                    for v, c in enumerate((2, 4, 3, 5)):
                        for k in range(2):
                            key = (l, ("MB", v, k))
                            bank_empty(pe, key)
                            for j in range(4):
                                n = 4 * k + j
                                ins = nc.tensor.matmul(bank_of(key)[:, j * P:(j + 1) * P],
                                                       modc[:, c, n:n + 1].to_broadcast([P, P]), eye[:, :],
                                                       start=True, stop=True)
                            last(ins)
                elif task in ("BQ", "BK", "BU", "K1", "K2", "K3"):
                    channel_major(l, task, xT)
                elif task == "PM":
                    pe.wait_ge(sem("b2_load"), 16 * N_B2)
                    pe.wait_ge(sem("pool_mixed"), 1)
                    for j in range(2):
                        key = (l, ("PL", j))
                        bank_empty(pe, key)
                        for g in range(2):
                            ins = nc.tensor.matmul(bank_of(key)[:, g * T:(g + 1) * T], w_pool[:, 2 * j + g, :],
                                                   mixed[:, 2 * j + g, :], start=True, stop=True)
                        last(ins)
                elif task == "SK":
                    pe.wait_ge(sem("b2_load"), 16 * N_B2)
                    transposes((l, ("SK",)), [(bank_of((l, ("SK",)))[:, k * P:(k + 1) * P],
                                               sub_rows[:, k * P:(k + 1) * P]) for k in range(2)])
                elif task[0] == "B" and task[1:].isdigit():
                    i = int(task[1:])
                    if i == 0:
                        pe.wait_ge(sem("qkv2_ready"), 3)
                    if i < HEADS2:
                        r = slice(64 * (i % 2), 64 * (i % 2) + 64)
                        scores(l, i, q2[r, i // 2, :], k2[r, i // 2, :])
                    if 2 <= i <= HEADS2 + 1:
                        weights_transposed(l, i - 2)
                    if i >= 3:
                        k = i - 3
                        values_summed(l, k, slice(64 * (k % 2), 64 * (k % 2) + 64),
                                      [v2[:, s, k * 64:(k + 1) * 64] for s in range(TT)])
                elif task[:2] == "AD":
                    modulation(l, task)
                elif output_unit(task):
                    if task == "O1":
                        pe.wait_ge(sem("pool_out"), 2)
                    else:
                        pe.wait_ge(sem("y2_ready"), HEADS2)
                    output_product(l, task)
                elif task[0] == "E":
                    i = int(task[1:])
                    key = (l, ("E", i))
                    bank_empty(pe, key)
                    pe.wait_ge(sem("skT_ready"), 1)
                    pe.wait_ge(sem("peer_q"), i // 2 + 1)
                    for t in range(TT):
                        for k in range(2):
                            g = 2 * t + k
                            ins = nc.tensor.matmul(bank_of(key)[:, g * P:(g + 1) * P],
                                                   yT[:, 2 * i + k, t * P:(t + 1) * P], skT[:, k, :],
                                                   start=True, stop=True)
                    last(ins)

        @block.scalar
        def _(act):
            a = nc.scalar
            do = steps(act, "act_step")

            def log_exp_tables():
                a.preload_act_table_set("natural_log_exp_and_others")

            for j in (0, 2):
                act.wait_ge(sem("bank_filled"), BANK["M", j] + 1)
                do(a.copy(memT[:, 2 * j:2 * j + 2, :].rearrange("p a t -> p (a t)"), bank_of(("M", j))[:, :]),
                   *bank_free(("M", j)))
                act.sem_inc(sem("memT_ready"), 1)
            def small_tables():
                act.wait_ge(sem("angles"), 1)
                do(a.activation(rope[:, 1, :], flat_b[:, 0:T], ACT.Sin))
                do(a.activation(rope[:, 0, :], flat_b[:, T:2 * T], ACT.Sin), "rope_ready")
                act.wait_ge(sem("lb_centred"), 1)
                do(a.activation(lbt[:, 1:3, :], lbt[:, 1:3, :], ACT.Exp), "lb_exp")

                act.wait_ge(sem("vec_ready"), 1)
                do(a.activation(silu_c, vec[:, V_C:V_C + DC], ACT.Silu), "silu_c")
                log_exp_tables()

            def freed(l, name):
                s, use = BIG[l, name]
                return f"pj_free{s}", use + 1

            def transposed_x(l, task, chunks=range(4), scale=None, shift=None):
                for j in chunks:
                    key = (l, (task, j))
                    bank_filled(act, key)
                    t, c0 = j // 2, 4 * (j % 2)
                    dst = xT[:, c0:c0 + 4, t * P:(t + 1) * P]
                    src = bank_of(key)[:, :].rearrange("p (c n) -> p c n", c=4)
                    if scale is None:
                        do(a.copy(dst, src), *bank_free(key))
                    else:
                        for c in range(4):
                            do(a.activation(dst[:, c, :], src[:, c, :], ACT.Identity, scale=scale[:, c0 + c:c0 + c + 1],
                                            bias=shift[:, c0 + c:c0 + c + 1]), *(bank_free(key) if c == 3 else ()))
                    act.sem_inc(sem("xT_ready"), 1)

            def exps(l, i):
                after(act, "sm_ready", l, i)
                st = stat[:, 4 * (i % 2):4 * (i % 2) + 4]
                for t in range(TT):
                    do(a.activation(sm[:, i % 2, t, :], sm[:, i % 2, t, :], ACT.Exp, bias=st[:, t:t + 1],
                                    accum_out=st[:, 2 + t:3 + t]), "exp_done" if t == TT - 1 else None)

            def weights_transposed(l, i):
                key = (l, ("PT", i))
                bank_filled(act, key)
                do(a.copy(pT[:, i % 2, :, :].rearrange("p a t -> p (a t)"), bank_of(key)[:, :]), *bank_free(key))
                act.sem_inc(sem("pt_ready"), 1)

            def row_norm(src, t, e, scale, done):
                do(a.activation(sm[:, :, :, :].rearrange("p a b t -> p (a b t)"), src, ACT.Square,
                                accum_out=stat[:, 10 + t:11 + t]))
                do(a.activation(stat[:, 12 + t:13 + t], stat[:, 10 + t:11 + t], ACT.Ln, scale=scale, bias=e))
                do(a.activation(stat[:, 12 + t:13 + t], stat[:, 12 + t:13 + t], ACT.Exp, scale=-0.5), done)

            for l in range(DEPTH):
                for task in TASKS[l]:
                    if (l, task) in BIG and task != "OUT":
                        s, _ = BIG[l, task]
                    if task == "X":
                        if l:
                            unit_done(act, l - 1, "G1")
                        transposed_x(l, "X")
                    elif task == "VEC":
                        small_tables()
                    elif task in ("G0", "G1", "GM", "GE"):
                        g = ("G0", "G1", "GM", "GE").index(task)
                        if l and task == "GM":
                            unit_done(act, l - 1, OUT_UNITS[l - 1][-1])
                        unit_done(act, l, task)
                        do(a.activation(yT[:, 4 * g:4 * g + 4, :].rearrange("p a t -> p (a t)"), pj[s][:, :], ACT.Silu),
                           *freed(l, task))
                        act.sem_inc(sem("gates"), 1)
                        log_exp_tables()
                    elif task[:2] == "FP":
                        g = int(task[2])
                        z = flat(b)[:, g * GH * T:(g + 1) * GH * T]
                        after(act, "fz", l, g)
                        if g:
                            bank_filled(act, (l, ("L", 0, 8, 0)))
                        do(a.activation(flat(kT)[:, g * GH * T:(g + 1) * GH * T], z, ACT.Sigmoid, scale=-1.0))
                        log_exp_tables()
                        do(a.activation(big[:, 0, :], z, ACT.Exp, scale=-1.0), "f_exp")
                        do(a.activation(big[:, 2, :], big[:, 0, :], ACT.Ln, bias=1.0))
                        after(act, "f_pos", l, g)
                        do(a.activation(big[:, 1, :], big[:, 1, :], ACT.Ln, bias=1.0), "f_ln")
                    elif task in ("Q0", "Q1"):
                        q = int(task[1])
                        unit_done(act, l, task)
                        do(a.copy(qT[:, 4 * q:4 * q + 4, :].rearrange("p a t -> p (a t)"), pj[s][:, :]), *freed(l, task))
                        act.sem_inc(sem("q_ready"), 1)
                    elif task == "C":
                        unit_done(act, l, task)
                        do(a.copy(cT[0:32, 3, :], pj[s][0:32, 3 * T:4 * T]))
                        do(a.copy(cT[:, 0:3, :].rearrange("p a t -> p (a t)"), pj[s][:, 0:3 * T]), *freed(l, task))
                        act.sem_inc(sem("c_ready"), 1)
                        if l:
                            bank_filled(act, (l - 1, ("HN", 3)))
                        do(a.activation(sq[:, :, :], cT[:, 0:3, :], ACT.Square), "c_sq")
                    elif task[:2] == "Da":
                        m = int(task[3])
                        after(act, "lvl_sub", l, 8 * int(task[2]) + m - 1)
                        do(a.activation(big[:, m % 3, :], big[:, m % 3, :], ACT.Exp), "lvl_exp")
                    elif task == "N":
                        key = (l, ("N",))
                        bank_filled(act, key)
                        B = bank_of(key)
                        do(a.activation(rstd[:, 0, :], B[:, 0:T], ACT.Ln, scale=P / Q_RANK, bias=eps[:, 0:1]))
                        do(a.activation(rstd[:, 1, :], B[:, T:2 * T], ACT.Ln, bias=eps[:, 0:1]))
                        do(a.activation(rstd[:, :, :], rstd[:, :, :], ACT.Exp, scale=-0.5), "c_rstd")
                        after(act, "kr_ready", l)
                        do(a.copy(kM[64:96, :, :], cT[0:32, 3:4, :].to_broadcast([32, MLA_HEADS, T])), "kr_spread")
                    elif task == "UP":
                        for j in range(4):
                            key = (l, ("UQ", j))
                            bank_filled(act, key)
                            do(a.copy(qM[:, 2 * j:2 * j + 2, :].rearrange("p a t -> p (a t)"), bank_of(key)[0:96, :]),
                               *bank_free(key))
                            act.sem_inc(sem("uq_ready"), 1)
                        for j in range(4):
                            key = (l, ("UK", j))
                            bank_filled(act, key)
                            do(a.copy(kM[0:64, 2 * j:2 * j + 2, :].rearrange("p a t -> p (a t)"), bank_of(key)[0:64, :]),
                               *bank_free(key))
                            act.sem_inc(sem("uk_ready"), 1)
                        for t in range(TT):
                            key = (l, ("UV", t))
                            bank_filled(act, key)
                            do(a.copy(vM[:, t, :], bank_of(key)[:, :]), *bank_free(key))
                            act.sem_inc(sem("uv_ready"), 1)
                    elif task in ("I0", "I1"):
                        q = int(task[1])
                        unit_done(act, l, task)
                        do(a.copy(hv[:, :, q * COLS:(q + 1) * COLS], pj[s][:, :].rearrange("p (a n) -> p a n", a=TT)),
                           *freed(l, task))
                        act.sem_inc(sem("hv_ready"), 1)
                    elif task in ("MQ", "MK", "MV"):
                        unit_done(act, l, task)
                        dst, done = {"MQ": (qE, "qE_ready"), "MK": (kE, "kE_ready"), "MV": (vE, "vE_ready")}[task]
                        do(a.copy(dst[:, :, :].rearrange("p a t -> p (a t)"), pj[s][:, :]), *freed(l, task))
                        act.sem_inc(sem(done), 1)
                    elif task[0] == "A" and task[1:].isdigit():
                        i = int(task[1:])
                        if i < N_ATT:
                            exps(l, i)
                        if 2 <= i <= N_ATT + 1:
                            weights_transposed(l, i - 2)
                    elif task[0] == "H":
                        g, i = int(task[1]), int(task[2])
                        if i >= 1:
                            n = 2 * g + i - 1
                            key = (l, ("HN", n))
                            bank_filled(act, key)
                            if n:
                                after(act, "y_hg", l, n - 1)
                            do(a.activation(rstd[:, :, :].rearrange("p a t -> p (a t)"), bank_of(key)[:, :], ACT.Ln,
                                            bias=eps[:, 0:1]))
                            do(a.activation(rstd[:, :, :], rstd[:, :, :], ACT.Exp, scale=-0.5), "ho_rstd")
                        if i < 2:
                            key = (l, ("HO", 2 * g + i))
                            bank_filled(act, key)
                            do(a.activation(sq[:, 0:2, :].rearrange("p a t -> p (a t)"), bank_of(key)[:, :], ACT.Square),
                               "ho_sq")
                    elif task == "LN":
                        for t in range(TT):
                            after(act, "ln_in", l, t)
                            row_norm(x[:, t, :], t, eps[:, 1:2], 1.0 / D_MODEL, "ln_rstd")
                            if l == DEPTH - 1:
                                if t:
                                    act.wait_ge(sem("scale1"), 1)
                                    transposed_x(B2, "X", (0, 1), modc[:, 1, :], modc[:, 0, :])
                                after(act, "x_next", l, t)
                                row_norm(x[:, t, :], t, eps[:, 0:1], 1.0 / D_MODEL, "row_rstd")

            l = B2
            for task in TASKS[l]:
                if task == "OUT":
                    for t in range(TT):
                        if t:
                            transposed_x(l, "X2", (0, 1), modc[:, 4, :], modc[:, 3, :])
                        act.wait_ge(sem("x_mid"), t + 1)
                        row_norm(x[:, t, :], t, eps[:, 0:1], 1.0 / D_MODEL, "row_rstd")
                elif task == "X":
                    transposed_x(l, task, (2,), modc[:, 1, :], modc[:, 0, :])
                elif task == "X2":
                    transposed_x(l, task, (2,), modc[:, 4, :], modc[:, 3, :])
                elif task == "MB":
                    for v, row in enumerate((row_gate1, row_scale2, row_shift2, row_gate2)):
                        for k in range(2):
                            key = (l, ("MB", v, k))
                            bank_filled(act, key)
                            do(a.copy(row[:, k * COLS:(k + 1) * COLS], bank_of(key)[:, :]), *bank_free(key))
                    act.sem_inc(sem("rows_ready"), 1)
                elif task in ("BQ", "BK", "BV", "BU"):
                    s, _ = BIG[l, task]
                    unit_done(act, l, task)
                    dst = {"BQ": q2, "BK": k2, "BV": v2[:, :, :], "BU": uT}[task]
                    dst = dst.rearrange("p a t -> p (a t)")
                    if task == "BQ":
                        do(a.mul(dst, pj[s][:, :], HD2 ** -0.5), *freed(l, task))
                    else:
                        do(a.copy(dst, pj[s][:, :]), *freed(l, task))
                    act.sem_inc(sem("uT_ready" if task == "BU" else "qkv2_ready"), 1)
                elif task == "PM":
                    for j in range(2):
                        key = (l, ("PL", j))
                        bank_filled(act, key)
                        for g in range(2):
                            c = 2 * j + g
                            do(a.activation(yT[:, 4 + c, :], bank_of(key)[:, g * T:(g + 1) * T], ACT.Copy,
                                            scale=vec[:, V_POOL + c:V_POOL + c + 1]),
                               *(bank_free(key) if g else ()))
                        act.sem_inc(sem("pool_out"), 1)
                elif task == "SK":
                    key = (l, ("SK",))
                    bank_filled(act, key)
                    do(a.copy(flat(sq)[:, 512:768], bank_of(key)[:, 0:2 * P]), *bank_free(key))
                    act.sem_inc(sem("skT_ready"), 1)
                elif task[0] == "B" and task[1:].isdigit():
                    i = int(task[1:])
                    if i < HEADS2:
                        exps(l, i)
                    if 2 <= i <= HEADS2 + 1:
                        weights_transposed(l, i - 2)
                    if i >= 3:
                        k = i - 3
                        key = (l, ("AO", k))
                        bank_filled(act, key)
                        r = slice(64 * (k % 2), 64 * (k % 2) + 64)
                        do(a.copy(yT[r, k // 2, :], bank_of(key)[r, 0:T]), *bank_free(key))
                        act.sem_inc(sem("y2_ready"), 1)
                elif task[0] == "K":
                    j = int(task[1:])
                    s, _ = BIG[l, task]
                    unit_done(act, l, task)
                    do(a.copy(yT[:, 4 * j:4 * j + 4, :].rearrange("p a t -> p (a t)"), pj[s][:, :]), *freed(l, task))
                    act.sem_inc(sem("peer_q"), 1)
                elif task[0] == "E":
                    i = int(task[1:])
                    key = (l, ("E", i))
                    bank_filled(act, key)
                    if i >= 2:
                        act.wait_ge(sem("sub_best"), i - 1)
                    do(a.copy(sm[:, i % 2, 0, :], bank_of(key)[:, 0:T]))
                    act.sem_inc(sem("sub_scores"), 1)
                    do(a.copy(later_scores[:, i, :], bank_of(key)[:, T:2 * T]), *bank_free(key))
            def top_exp(t):
                act.wait_ge(sem("top_centred"), t + 1)
                do(a.activation(top_val[:, t], top_val[:, t], ACT.Exp), "top_exp")

            def gelu(t):
                act.wait_ge(sem("dots_ready"), t + 1)
                do(a.activation(dots[:, t, :], dots[:, t, :], ACT.Gelu), "gelu_done")

            def final_norm(t):
                act.wait_ge(sem("x_last"), t + 1)
                row_norm(x[:, t, :], t, eps[:, 0:1], 1.0 / D_MODEL, "row_rstd")

            top_exp(0)
            gelu(0)
            top_exp(1)
            final_norm(0)
            gelu(1)
            final_norm(1)

        @block.vector
        def _(dve):
            v = nc.vector
            do = steps(dve, "dve_step")
            do(v.memset(vec_rows, 0.0), "vec_zeroed")
            do(v.memset(ones_mean[:, :], 1.0 / P), "ones_ready")
            do(v.memset(eps[:, 0:1], RMS_EPS))
            do(v.memset(eps[:, 1:2], LN_EPS))
            for j in (1, 3):
                dve.wait_ge(sem("bank_filled"), BANK["M", j] + 1)
                do(v.tensor_copy(memT[:, 2 * j:2 * j + 2, :].rearrange("p a t -> p (a t)"), bank_of(("M", j))[:, :]),
                   *bank_free(("M", j)))
                dve.sem_inc(sem("memT_ready"), 1)
            dve.wait_ge(sem("bank_filled"), BANK[0, ("VEC",)] + 1)
            do(v.tensor_copy(vec[:, :], bank_of((0, ("VEC",)))[:, 0:104]), *bank_free((0, ("VEC",))))
            dve.sem_inc(sem("vec_ready"), 1)
            dve.wait_ge(sem("consts_load"), 16 * N_CONST)
            ang, turns = flat_b[:, T:2 * T], flat_b[:, 2 * T:3 * T]
            do(v.tensor_copy(ang, flat_b[:, 0:T].bitcast(i32)))
            do(v.tensor_scalar(ang, ang, vec[:, V_INV:V_INV + 1], None, ALU.mult))
            MAGIC = 12582912.0
            do(v.tensor_scalar(turns, ang, 1.0 / (2 * np.pi), None, ALU.mult))
            do(v.tensor_scalar(turns, turns, MAGIC, None, ALU.add))
            do(v.tensor_scalar(turns, turns, MAGIC, None, ALU.subtract))
            C1 = 6.28125
            C2 = float(np.float32(int((2 * np.pi - C1) * 2 ** 20) / 2 ** 20))
            C3 = 2 * np.pi - C1 - C2
            for c in (C1, C2, C3):
                do(v.scalar_tensor_tensor(out=ang, in0=turns, scalar=-c, in1=ang, op0=ALU.mult, op1=ALU.add))
            PI = 3.1415925
            do(v.tensor_scalar(flat_b[:, 0:T], ang, PI, -PI, ALU.min, ALU.max))
            do(v.tensor_scalar(turns, ang, float(np.pi / 2), -2 * np.pi, ALU.is_gt, ALU.mult))
            do(v.tensor_tensor(ang, ang, turns, ALU.add))
            do(v.tensor_scalar(ang, ang, float(np.pi / 2), PI, ALU.add, ALU.min))
            do(v.tensor_scalar(ang, ang, -PI, None, ALU.max), "angles")
            do(v.tensor_copy(level_mask[:, :, :].rearrange("p m t -> p (m t)"), flat_b[:, 800:1696].bitcast(i32)))
            l0, l1 = vec[:, V_LB:V_LB + 8], vec[:, V_LB + 8:V_LB + 16]
            do(v.tensor_tensor(lbt[:, 0, :], l0, l1, ALU.max))
            do(v.tensor_tensor(lbt[:, 1, :], l0, lbt[:, 0, :], ALU.subtract))
            do(v.tensor_tensor(lbt[:, 2, :], l1, lbt[:, 0, :], ALU.subtract), "lb_centred")
            dve.wait_ge(sem("lb_exp"), 1)
            do(v.tensor_tensor(lbt[:, 3, :], lbt[:, 1, :], lbt[:, 2, :], ALU.add))
            do(v.reciprocal(lbt[:, 3, :], lbt[:, 3, :]))
            do(v.tensor_tensor(lbt[:, 1:3, :], lbt[:, 1:3, :], lbt[:, 3:4, :].to_broadcast([P, 2, 8]), ALU.mult))
            do(v.tensor_tensor(lower[:, 0, 0, :], lbt[:, 1, :], lbt[:, 1, :], ALU.subtract))
            do(v.tensor_tensor(lower[:, 1, 0, :], lbt[:, 1, :], lbt[:, 2, :], ALU.add))
            do(v.tensor_tensor(lower[:, 1, 0, :], lower[:, 1, 0, :], lbt[:, 1, :], ALU.subtract))
            do(v.tensor_scalar(lower[:, :, 1, :], lower[:, :, 0, :], -1.0, 1.0, ALU.mult, ALU.add))
            dve.wait_ge(sem("rope_ready"), 1)
            cos, sin = rope[:, 0, :], rope[:, 1, :]

            def refine(y, mean, e, tmp, scale=1.0, free=None):
                do(v.tensor_scalar(tmp, mean, scale, e, ALU.mult, ALU.add))
                do(v.tensor_tensor(tmp, tmp, y, ALU.mult))
                do(v.tensor_tensor(tmp, tmp, y, ALU.mult))
                do(v.tensor_scalar(tmp, tmp, -0.5, 1.5, ALU.mult, ALU.add))
                do(v.tensor_tensor(y, y, tmp, ALU.mult), *(free or ()))

            def heads(k):
                return big[:, k, :].rearrange("p (h t) -> p h t", t=T)

            def wide(x3):
                return x3.rearrange("p h t -> p (h t)")

            def level_views(g, m):
                s = slice(GH * g, GH * (g + 1))
                if m == 8:
                    W = heads(m % 3)
                    return (b[:, s, 0:P], b[:, s, P:T], W[:, :, 0:P], W[:, :, P:T], kT[:, s, 0:P], qT[:, s, P:T],
                            b[:, s, P - 1:P].to_broadcast([P, GH, P]))
                n = 2 ** (m - 1)

                def split(y):
                    z = y.rearrange("p (n two m) -> p n two m", two=2, m=n)
                    return z[:, :, 0, :], z[:, :, 1, :]
                b0, b1 = split(wide(b[:, s, :]))
                w0, w1 = split(big[:, m % 3, :])
                return (b0, b1, w0, w1, split(wide(kT[:, s, :]))[0], split(wide(qT[:, s, :]))[1],
                        b0[:, :, n - 1:n].to_broadcast([P, GH * T // (2 * n), n]))

            def modulation(l, task):
                j = int(task[2:])
                key = (l, (task,))
                bank_filled(dve, key)
                n = COLS // P
                do(v.scalar_tensor_tensor(out=modc[:, :, :].rearrange("p a c -> p (a c)")[:, j * n:(j + 1) * n],
                                          in0=bank_of(key)[:, 0:n], scalar=float(P),
                                          in1=vec[:, V_BADA + j * n:V_BADA + (j + 1) * n], op0=ALU.mult, op1=ALU.add),
                   *bank_free(key))

            def scale_gain(c, gain, done=None):
                do(v.scalar_tensor_tensor(out=modc[:, c, :], in0=modc[:, c, :], scalar=1.0,
                                          in1=vec[:, gain:gain + DC], op0=ALU.add, op1=ALU.mult), done)

            def norm_rows(part, t):
                dve.wait_ge(sem("row_rstd"), TT * part + t + 1)
                refine(stat[:, 12 + t:13 + t], stat[:, 10 + t:11 + t], RMS_EPS, stat[:, 14:15], 1.0 / D_MODEL)
                do(v.tensor_scalar(normed[:, t, :], x[:, t, :], stat[:, 12 + t:13 + t], None, ALU.mult), "row_normed")

            def normalise(i):
                st = stat[:, 4 * (i % 2):4 * (i % 2) + 4]
                do(v.reciprocal(st[:, 2:4], st[:, 2:4]))
                P3 = sm[:, i % 2, :, :]
                do(v.tensor_tensor(P3, P3, st[:, 2:4].unsqueeze(2).to_broadcast([P, TT, T]), ALU.mult), "p_ready")

            for l in range(DEPTH):
                for task in TASKS[l]:
                    if task in ("F0", "F1"):
                        q = int(task[1])
                        s, use = BIG[l, task]
                        unit_done(dve, l, task)
                        do(v.tensor_scalar(wide(b[:, GH * q:GH * (q + 1), :]), pj[s][:, :], -44.0, None, ALU.max),
                           f"pj_free{s}", use + 1)
                        dve.sem_inc(sem("fz"), 1)
                    elif task[:2] == "AD":
                        modulation(l, task)
                    elif task[:2] == "FP":
                        g = int(task[2])
                        s = slice(GH * g, GH * (g + 1))
                        after(dve, "f_exp", l, g)
                        lb = lower[:, l, 0, s].unsqueeze(2).to_broadcast([P, GH, T])
                        omlb = lower[:, l, 1, s].unsqueeze(2).to_broadcast([P, GH, T])
                        do(v.tensor_tensor(heads(1), heads(0), lb, ALU.mult), "f_pos")
                        do(v.tensor_tensor(kT[:, s, :], kT[:, s, :], omlb, ALU.mult), "k_ready")
                        after(dve, "f_ln", l, g)
                        do(v.tensor_tensor(big[:, 2, :], big[:, 1, :], big[:, 2, :], ALU.subtract))
                        sums = wide(b[:, s, :])
                        for n in range(GH * TT):
                            seg = big[:, 2, n * P:(n + 1) * P]
                            do(v.tensor_tensor_scan(sums[:, n * P:(n + 1) * P], seg, seg, 0.0, ALU.add, ALU.bypass))
                    elif task[:2] == "Da":
                        g, m = int(task[2]), int(task[3])
                        if m >= 3:
                            bank_filled(dve, (l, ("L", g, m - 3, 1)))
                        b0, b1, w0, w1, _, _, mid = level_views(g, m)
                        do(v.tensor_tensor(w0, mid, b0, ALU.subtract))
                        if m == 8:
                            do(v.tensor_copy(w1, b1), "lvl_sub")
                        else:
                            do(v.tensor_tensor(w1, b1, mid, ALU.subtract), "lvl_sub")
                    elif task[:2] == "Db":
                        g, m = int(task[2]), int(task[3])
                        after(dve, "lvl_exp", l, 8 * g + m - 1)
                        _, _, w0, w1, k0, q1, _ = level_views(g, m)
                        if m == 1:
                            after(dve, "q_ready", l, g)
                        do(v.tensor_tensor(w0, w0, k0, ALU.mult))
                        do(v.tensor_tensor(w1, w1, q1, ALU.mult), "lvl_ready")
                    elif task[0] == "L" and task != "LN":
                        g, m = int(task[1]), int(task[2])
                        if g and m == 0:
                            bank_filled(dve, (l, ("HO", 1)))
                        for j in range(2 if m < 8 else 1):
                            key = (l, ("L", g, m, j))
                            bank_filled(dve, key)
                            B = bank_of(key)[:, :].rearrange("p (g t) -> p g t", t=P)
                            dst = pair[:, 4 * j:4 * j + 4, :]
                            if m == 0:
                                do(v.tensor_tensor(dst, B, eye[:, :].unsqueeze(1).to_broadcast([P, 4, P]), ALU.mult),
                                   *bank_free(key))
                            elif m < 8:
                                do(v.copy_predicated(dst, level_mask[:, m - 1:m, :].to_broadcast([P, 4, P]), B),
                                   *bank_free(key))
                            else:
                                do(v.tensor_copy(far_pair[:, :, :], B), *bank_free(key))
                        dve.sem_inc(sem("blended"), 1)
                    elif task == "N":
                        after(dve, "c_rstd", l)
                        B = bank_of((l, ("N",)))
                        refine(rstd[:, 0, :], B[:, 0:T], RMS_EPS, sm[:, 0, 0, :], P / Q_RANK)
                        refine(rstd[:, 1, :], B[:, T:2 * T], RMS_EPS, sm[:, 0, 0, :], 1.0, bank_free((l, ("N",))))
                        for c in range(3):
                            g = V_QN + 2 * l + c if c < 2 else V_KN + l
                            do(v.scalar_tensor_tensor(out=cT[:, c, :], in0=cT[:, c, :], scalar=vec[:, g:g + 1],
                                                      in1=rstd[:, c // 2, :], op0=ALU.mult, op1=ALU.mult),
                               "c_normed" if c == 2 else None)
                        key = (l, ("KR",))
                        bank_filled(dve, key)
                        tmp = sm[0:32, 0, 0, :]
                        do(v.tensor_tensor(tmp, bank_of(key)[0:32, 0:T], sin[0:32, :], ALU.mult), *bank_free(key))
                        do(v.tensor_tensor(cT[0:32, 3, :], cT[0:32, 3, :], cos[0:32, :], ALU.mult))
                        do(v.tensor_tensor(cT[0:32, 3, :], cT[0:32, 3, :], tmp, ALU.add), "kr_ready")
                    elif task == "UP":
                        for j in range(4):
                            key = (l, ("QR", j))
                            bank_filled(dve, key)
                            r = slice(64, 96)
                            q = qM[r, 2 * j:2 * j + 2, :]
                            tmp = sm[r, 0, :, :]
                            B = bank_of(key)[r, :].rearrange("p (a t) -> p a t", a=2)
                            do(v.tensor_tensor(tmp, B, sin[r, :].unsqueeze(1).to_broadcast([32, 2, T]), ALU.mult),
                               *bank_free(key))
                            do(v.tensor_tensor(q, q, cos[r, :].unsqueeze(1).to_broadcast([32, 2, T]), ALU.mult))
                            do(v.tensor_tensor(q, q, tmp, ALU.add), "qrope_ready")
                    elif task[0] == "A" and task[1:].isdigit():
                        i = int(task[1:])
                        st = stat[:, 4 * (i % 2):4 * (i % 2) + 4]
                        if i < N_ATT:
                            key = (l, ("S", i))
                            bank_filled(dve, key)
                            if i >= 2:
                                bank_filled(dve, (l, ("PT", i - 2)))
                            B = bank_of(key)[:, :].rearrange("p (a t) -> p a t", a=TT)
                            if i < MLA_HEADS:
                                do(v.scalar_tensor_tensor(out=sm[:, i % 2, :, :], in0=B, scalar=MLA_SCALE,
                                                          in1=causal[:, :, :], op0=ALU.mult, op1=ALU.add),
                                   *bank_free(key))
                            else:
                                do(v.tensor_scalar(sm[:, i % 2, :, :], B, MEM_SCALE, None, ALU.mult), *bank_free(key))
                            do(v.tensor_reduce(st[:, 0:2], sm[:, i % 2, :, :], X, ALU.max, negate=True), "sm_ready")
                        if 1 <= i <= N_ATT:
                            after(dve, "exp_done", l, i - 1)
                            normalise(i - 1)
                        if i >= 3:
                            h = i - 3
                            key = (l, ("AO", h))
                            bank_filled(dve, key)
                            if h < MLA_HEADS:
                                r = slice(64 * (h % 2), 64 * (h % 2) + 64)
                                g = yT[r, 8 + h // 2, :]
                            else:
                                r = slice(0, P)
                                g = yT[:, 12 + h - MLA_HEADS, :]
                            if h in (0, MLA_HEADS):
                                after(dve, "gates", l, GATE_OF["GM" if h == 0 else "GE"])
                            do(v.tensor_tensor(g, bank_of(key)[r, 0:T], g, ALU.mult), *bank_free(key))
                            dve.sem_inc(sem("y_att"), 1)
                    elif task[0] == "H":
                        g, i = int(task[1]), int(task[2])
                        if i < 2:
                            n = 2 * g + i
                            key = (l, ("HO", n))
                            after(dve, "ho_sq", l, n)
                            after(dve, "gates", l, GATE_OF[f"G{g}"])
                            y = wide(yT[:, 2 * n:2 * n + 2, :])
                            do(v.scalar_tensor_tensor(out=y, in0=bank_of(key)[:, :], scalar=vec[:, V_OUT + l:V_OUT + l + 1],
                                                      in1=y, op0=ALU.mult, op1=ALU.mult), *bank_free(key))
                        if i >= 1:
                            n = 2 * g + i - 1
                            after(dve, "ho_rstd", l, n)
                            key = (l, ("HN", n))
                            B = bank_of(key)[:, :]
                            refine(wide(rstd[:, :, :]), B, RMS_EPS, B, 1.0, bank_free(key))
                            y = wide(yT[:, 2 * n:2 * n + 2, :])
                            do(v.tensor_tensor(y, y, wide(rstd[:, :, :]), ALU.mult), "y_hg")
                    elif task == "LN":
                        if l == DEPTH - 1:
                            scale_gain(1, V_N1, "scale1")
                        for t in range(TT):
                            if t == 0:
                                after(dve, "out_tile", l)
                            else:
                                unit_done(dve, l, OUT_UNITS[l][-1])
                            do(v.scalar_tensor_tensor(out=x[:, t, :], in0=x[:, t, :], scalar=ALPHA, in1=pj[t][:, :],
                                                      op0=ALU.mult, op1=ALU.add, accum_out=stat[:, 8 + t:9 + t]),
                               f"pj_free{t}", BIG[l, "OUT"][t] + 1)
                            do(v.tensor_scalar(stat[:, 8 + t:9 + t], stat[:, 8 + t:9 + t], 1.0 / D_MODEL, None, ALU.mult))
                            do(v.tensor_scalar(x[:, t, :], x[:, t, :], stat[:, 8 + t:9 + t], None, ALU.subtract), "ln_in")
                            if t == 0:
                                dve.wait_ge(sem("gb_load"), (l + 1) * 32)
                            elif l == DEPTH - 1:
                                norm_rows(0, 0)
                            after(dve, "ln_rstd", l, t)
                            refine(stat[:, 12 + t:13 + t], stat[:, 10 + t:11 + t], LN_EPS, stat[:, 14:15], 1.0 / D_MODEL)
                            do(v.scalar_tensor_tensor(out=x[:, t, :], in0=x[:, t, :], scalar=stat[:, 12 + t:13 + t],
                                                      in1=ln_gb[:, 0:D_MODEL], op0=ALU.mult, op1=ALU.mult))
                            do(v.tensor_tensor(x[:, t, :], x[:, t, :], ln_gb[:, D_MODEL:], ALU.add), "x_next")
                            if l == DEPTH - 1 and t == TT - 1:
                                norm_rows(0, t)


            l = B2

            def route(t, e):
                if t == 0:
                    dve.wait_ge(sem("sub_scores"), e + 1)
                values = sm[:, e % 2, 0, :] if t == 0 else later_scores[:, e, :]
                keys = [(values[:, k * P:(k + 1) * P], keys_left[:, k * P:(k + 1) * P],
                         sub_val[:, t, e, k, :], sub_id[:, t, e, k, :]) for k in range(2)]
                sums = (cand, cand_left, top_val[:, t, e, :], top_pos[:, t, e * TOPK:(e + 1) * TOPK])

                def weave(ins):
                    do(ins, behind=1)

                def first8(chain):
                    weave(v.max(chain[2][:, 0:8], chain[0]))

                def without(chain):
                    weave(v.match_replace(chain[1], chain[2][:, 0:8], chain[0], -3e38))

                def next8(chain):
                    weave(v.max(chain[2][:, 8:16], chain[1]))

                def place8(chain):
                    weave(v.max_index(chain[3][:, 0:8], chain[2][:, 0:8], chain[0]))

                def next_place8(chain):
                    weave(v.max_index(chain[3][:, 8:16], chain[2][:, 8:16], chain[1]))

                for stage in (first8, without, next8):
                    for chain in keys:
                        stage(chain)
                place8(keys[0])
                weave(v.tensor_tensor(cand.rearrange("p (i j) -> p i j", i=TOPK),
                                      sub_val[:, t, e, 0, :].unsqueeze(2).to_broadcast([P, TOPK, TOPK]),
                                      sub_val[:, t, e, 1, :].unsqueeze(1).to_broadcast([P, TOPK, TOPK]), ALU.add))
                place8(keys[1])
                first8(sums)
                next_place8(keys[0])
                without(sums)
                next_place8(keys[1])
                next8(sums)
                if t == 0:
                    dve.sem_inc(sem("sub_best"), 1)
                place8(sums)
                do(v.max_index(sums[3][:, 8:16], sums[2][:, 8:16], sums[1]))

            def experts_of(t, first, last):
                assert (t, first, last) in EXPERT_PARTS
                H = last - first
                n = H * TOPK
                js, es = slice(first * TOPK, last * TOPK), slice(first, last)
                do(v.tensor_copy(sub_idf[:, t, es], sub_id[:, t, es]))
                half_ids = ((ALU.logical_shift_right, 4, first_of, id_a), (ALU.bitwise_and, 15, second_of, id_b))
                digits = [digit[:, k * n:(k + 1) * n] for k in range(2)]
                ohs = [onehot[:, k * n:(k + 1) * n, :] for k in range(2)]
                for k, (op, arg, place, found) in enumerate(half_ids):
                    do(v.tensor_scalar(digits[k], top_pos[:, t, js], arg, None, op), behind=1)
                for k, (op, arg, place, found) in enumerate(half_ids):
                    do(v.tensor_copy(place[:, 0:n], digits[k]), behind=1)
                for k, (op, arg, place, found) in enumerate(half_ids):
                    do(v.tensor_tensor(ohs[k], iota.unsqueeze(1).to_broadcast([P, n, TOPK]),
                                       place[:, 0:n].unsqueeze(2).to_broadcast([P, n, TOPK]), ALU.is_equal), behind=1)
                for k, (op, arg, place, found) in enumerate(half_ids):
                    oh4 = ohs[k].rearrange("p (e j) i -> p e j i", e=H)
                    do(v.tensor_tensor(oh4, oh4, sub_idf[:, t, es, k, :].unsqueeze(2)
                                       .to_broadcast([P, H, TOPK, TOPK]), ALU.mult), behind=1)
                for k, (op, arg, place, found) in enumerate(half_ids):
                    do(v.tensor_reduce(found[:, 0:n], ohs[k], X, ALU.add), behind=1 - k)
                do(v.scalar_tensor_tensor(out=id_a[:, 0:n], in0=id_a[:, 0:n], scalar=float(NKEYS), in1=id_b[:, 0:n],
                                          op0=ALU.mult, op1=ALU.add))
                do(v.tensor_copy(expert[:, t, js], id_a[:, 0:n]), "experts")

            def gates_of(t):
                do(v.tensor_copy(stat[:, 0:8].unsqueeze(2), top_val[:, t, :, 0:1]))
                do(v.tensor_tensor(top_val[:, t], top_val[:, t],
                                   stat[:, 0:8].unsqueeze(2).to_broadcast([P, PEER_HEADS, TOPK]), ALU.subtract),
                   "top_centred")
                dve.wait_ge(sem("top_exp"), t + 1)
                do(v.tensor_reduce(stat[:, 0:8], top_val[:, t], X, ALU.add))
                do(v.reciprocal(stat[:, 0:8], stat[:, 0:8]))
                do(v.tensor_tensor(gate[:, t, :].rearrange("p (e j) -> p e j", e=PEER_HEADS), top_val[:, t],
                                   stat[:, 0:8].unsqueeze(2).to_broadcast([P, PEER_HEADS, TOPK]), ALU.mult))

            for task in TASKS[l]:
                if task == "MB":
                    scale_gain(4, V_N2, "mod_ready")
                elif task[0] == "B" and task[1:].isdigit():
                    i = int(task[1:])
                    if i < HEADS2:
                        st = stat[:, 4 * (i % 2):4 * (i % 2) + 4]
                        key = (l, ("S", i))
                        bank_filled(dve, key)
                        if i >= 2:
                            bank_filled(dve, (l, ("PT", i - 2)))
                        if i == 0:
                            dve.wait_ge(sem("table_load"), 32)
                        do(v.scalar_tensor_tensor(out=sm[:, i % 2, :, :], in0=dist, scalar=-2.0 ** -(i + 1),
                                                  in1=bank_of(key)[:, :].rearrange("p (a t) -> p a t", a=TT),
                                                  op0=ALU.mult, op1=ALU.add), *bank_free(key))
                        do(v.tensor_reduce(st[:, 0:2], sm[:, i % 2, :, :], X, ALU.max, negate=True), "sm_ready")
                    if 1 <= i <= HEADS2:
                        st = stat[:, 4 * ((i - 1) % 2):4 * ((i - 1) % 2) + 4]
                        after(dve, "exp_done", l, i - 1)
                        for t in range(TT):
                            p = sm[:, (i - 1) % 2, t, :]
                            do(v.scalar_tensor_tensor(out=p, in0=p, scalar=1.0, in1=count[:, t, :], op0=ALU.mult,
                                                      op1=ALU.mult, accum_out=st[:, 2 + t:3 + t]))
                        normalise(i - 1)
                elif task == "OUT":
                    for t in range(TT):
                        if t == 0:
                            dve.wait_ge(sem("rows_ready"), 1)
                            after(dve, "out_tile", l)
                        else:
                            unit_done(dve, l, OUT_UNITS[l][-1])
                        tmp = product
                        do(v.tensor_tensor(tmp, pj[t][:, :], row_gate1, ALU.mult), f"pj_free{t}", BIG[l, "OUT"][t] + 1)
                        do(v.tensor_tensor(x[:, t, :], x[:, t, :], tmp, ALU.add), "x_mid")
                        norm_rows(1, t)
                elif task in ("X", "X2"):
                    scale, shift = (modc[:, 1, :], modc[:, 0, :]) if task == "X" else (modc[:, 4, :], modc[:, 3, :])
                    key = (l, (task, 3))
                    bank_filled(dve, key)
                    src = bank_of(key)[:, :].rearrange("p (c n) -> p c n", c=4)
                    for c in range(4):
                        do(v.tensor_scalar(xT[:, 4 + c, P:T], src[:, c, :], scale[:, 4 + c:5 + c],
                                           shift[:, 4 + c:5 + c], ALU.mult, ALU.add),
                           *(bank_free(key) if c == 3 else ()))
                    dve.sem_inc(sem("xT_ready"), 1)
                elif task == "K0":
                    bank_filled(dve, (l, ("X2", 3)))
                    for t in range(TT):
                        do(v.tensor_tensor(normed[:, t, :], normed[:, t, :], row_scale2, ALU.mult))
                        do(v.tensor_tensor(normed[:, t, :], normed[:, t, :], row_shift2, ALU.add))
                elif task in ("E0", "E1", "E2", "E3"):
                    if task == "E2":
                        unit_done(dve, l, "K1")
                        dve.sem_inc(sem("slots_free"), GHALF)
                    route(0, int(task[1:]))
                    if task == "E1":
                        experts_of(0, 0, 2)

            experts_of(0, 2, 4)
            unit_done(dve, l, "K2")
            dve.sem_inc(sem("slots_free"), GHALF)

            def row(run, k, turn, consume):
                dve.wait_ge(sem(f"row_load{k}"), turn * 16 + (16 * TURNS * run + 16))
                dve.wait_ge(sem("slots_free"), turn * GSLOTS + (GSLOTS + PICKS * run + k - 1))
                consume(k, turn * GSLOTS + k).then_inc(sem("slots_free"), 1)

            def turn_rows(run, turn, consume, slots=range(GSLOTS)):
                for k in slots:
                    row(run, k, turn, consume)

            def rows(run, consume, first=0):
                with dve.Fori(0, TURNS - first) as turn:
                    turn_rows(run, turn + first if first else turn, consume)
                dve.wait_ge(sem("slots_free"), GSLOTS + PICKS * (run + 1))

            def at(tile, t, j):
                return tile[:, t, j:j + 1] if isinstance(j, int) else tile[:, t, bass.ds(j, 1)]

            def dot(t):
                return lambda k, j: v.scalar_tensor_tensor(
                    out=product[:, :] if k % 2 else spare_product, in0=gslot[k], scalar=1.0, in1=normed[:, t, :],
                    op0=ALU.mult, op1=ALU.mult, accum_out=at(dots, t, j))

            def weighted(t):
                return lambda k, j: v.scalar_tensor_tensor(
                    out=spare_product if k % 2 else acc[:, t, :], in0=gslot[k], scalar=at(gate, t, j),
                    in1=spare_product if k % 2 else acc[:, t, :], op0=ALU.mult, op1=ALU.add)

            def begin_sums(t):
                if t == 0:
                    unit_done(dve, l, "K3")
                do(v.memset(acc[:, t, :], 0.0))
                do(v.memset(spare_product, 0.0))
                dve.wait_ge(sem("gelu_done"), t + 1)
                do(v.tensor_tensor(gate[:, t, :], gate[:, t, :], dots[:, t, :], ALU.mult))

            def end_sums(t):
                do(v.tensor_tensor(acc[:, t, :], acc[:, t, :], spare_product, ALU.add))
                do(v.tensor_tensor(acc[:, t, :], acc[:, t, :], row_gate2, ALU.mult))
                do(v.tensor_tensor(x[:, t, :], x[:, t, :], acc[:, t, :], ALU.add), "x_last")

            def finish(t):
                dve.wait_ge(sem("row_rstd"), 2 * TT + t + 1)
                refine(stat[:, 12 + t:13 + t], stat[:, 10 + t:11 + t], RMS_EPS, stat[:, 14:15], 1.0 / D_MODEL)
                do(v.scalar_tensor_tensor(out=x[:, t, :], in0=x[:, t, :], scalar=stat[:, 12 + t:13 + t],
                                          in1=final_g, op0=ALU.mult, op1=ALU.mult), "result")

            half_turns = (range(GHALF), range(GHALF, GSLOTS))
            turn_rows(0, 0, dot(0))
            route(0, 4)
            turn_rows(0, 1, dot(0), half_turns[0])
            route(0, 5)
            turn_rows(0, 1, dot(0), half_turns[1])
            route(0, 6)
            route(0, 7)
            turn_rows(0, 2, dot(0), half_turns[0])
            experts_of(0, 4, 8)
            turn_rows(0, 2, dot(0), half_turns[1])
            for turn in range(3, TURNS):
                turn_rows(0, turn, dot(0))
                route(1, turn - 3)
            dve.wait_ge(sem("slots_free"), GSLOTS + PICKS)
            dve.sem_inc(sem("dots_ready"), 1)
            gates_of(0)
            begin_sums(0)
            turn_rows(1, 0, weighted(0))
            route(1, 5)
            turn_rows(1, 1, weighted(0))
            route(1, 6)
            turn_rows(1, 2, weighted(0))
            route(1, 7)
            turn_rows(1, 3, weighted(0))
            experts_of(1, 0, 4)
            turn_rows(1, 4, weighted(0))
            gates_of(1)
            turn_rows(1, 5, weighted(0))
            experts_of(1, 4, 8)
            rows(1, weighted(0), 6)
            end_sums(0)

            rows(2, dot(1))
            dve.sem_inc(sem("dots_ready"), 1)
            finish(0)
            begin_sums(1)
            rows(3, weighted(1))
            end_sums(1)
            finish(1)


_NAMES = ["x", "mem", "positions", "w_in", "hgrn_lb_logits", "hgrn_out_norm", "mla_q_norm", "mla_kv_norm",
          "w_mla_uq", "w_mla_uk", "w_mla_uv", "w_mem_k", "w_mem_v", "w_out", "ln_g", "ln_b", "c_2", "pool_scale_2",
          "w_ada_2", "b_ada_2", "norm1_g_2", "w_in_2", "pool_w_2", "w_out_2", "norm2_g_2", "peer_wq_2",
          "peer_subkeys_2", "peer_u_2", "peer_v_2", "final_g_2"]


def kernel(**inputs):
    import concourse.bacc as bacc
    from concourse import mybir
    from concourse.bass_utils import run_bass_kernel_spmd

    nc = bacc.Bacc("TRN2", target_bir_lowering=False, num_devices=1)
    arrays = {n: np.ascontiguousarray(inputs[n]) for n in _NAMES}
    arrays.update(constants())
    d = {n: nc.dram_tensor(f"in_{n}", a.shape, mybir.dt.from_np(a.dtype), kind="ExternalInput").ap()
         for n, a in arrays.items()}
    out = nc.dram_tensor("out", (T, D_MODEL), mybir.dt.float32, kind="ExternalOutput").ap()
    build(nc, d, out)
    got = run_bass_kernel_spmd(nc, [{f"in_{n}": a for n, a in arrays.items()}], core_ids=[0])
    return got.results[0]["out"].reshape(1, T, D_MODEL)
```
